# Optimizing a Trainium2 kernel written in Bass

```python
import jax, jax.numpy as jnp
from jax import lax
import numpy as np

D_MODEL = 1024
BATCH = 1
SEQ = 1024
DEPTH = 1
DEC_BATCH = 8
DEC_SEQ = 1
PAST_LEN = 8192
PAGE_SIZE = 128

N_MEM = 256
CHUNK = 64
CONV_W = 4
EPS = 1e-6
GDN_HEADS = 8
GDN_DK = 128
GDN_DV = 128
GDN_QK = GDN_HEADS * GDN_DK
GDN_V = GDN_HEADS * GDN_DV
GDN_CONV_CH = 2 * GDN_QK + GDN_V
SSM_DINNER = 2 * D_MODEL
SSM_HEADDIM = 64
SSM_HEADS = SSM_DINNER // SSM_HEADDIM
SSM_GROUPS = 8
SSM_DSTATE = 128
SSM_BC = SSM_GROUPS * SSM_DSTATE
SSM_CONV_CH = SSM_DINNER + 2 * SSM_BC
X_HEADS = 4
X_HEADDIM = D_MODEL // X_HEADS
D_FF = 4 * D_MODEL
IN_SPLITS = (GDN_CONV_CH, GDN_V, GDN_HEADS, GDN_HEADS, SSM_DINNER, SSM_CONV_CH, SSM_HEADS, D_MODEL, D_MODEL)
IN_COLS = GDN_CONV_CH + GDN_V + 2 * GDN_HEADS + SSM_DINNER + SSM_CONV_CH + SSM_HEADS + 2 * D_MODEL

kernel_name = "hybrid_gdn_ssd_memxattn_step"

def split_cols(t, sizes):
    out, start = [], 0
    for s in sizes:
        out.append(t[..., start:start + s])
        start += s
    return out

def rmsnorm(x, g):
    xf = x.astype(jnp.float32)
    xf = xf * lax.rsqrt(jnp.mean(xf * xf, axis=-1, keepdims=True) + EPS)
    return (xf * g.astype(jnp.float32)).astype(x.dtype)

def l2norm(x):
    return x * lax.rsqrt(jnp.sum(x * x, axis=-1, keepdims=True) + EPS)

def chunk_len(L):
    return CHUNK if L % CHUNK == 0 else L

def causal_dwconv(x, buf, w):
    xc = jnp.concatenate([buf.astype(x.dtype), x], axis=1)
    y = lax.conv_general_dilated(xc, w[:, None, :].astype(x.dtype), window_strides=(1,), padding='VALID',
                                 dimension_numbers=('NWC', 'WIO', 'NWC'), feature_group_count=x.shape[-1])
    return y, xc[:, -(CONV_W - 1):]

def gated_delta_chunked(q, k, v, g, beta, S0):
    Bsz, L, H, dk = q.shape
    dv = v.shape[-1]
    C = chunk_len(L)
    n = L // C

    def blk(t):
        return jnp.moveaxis(t.reshape((Bsz, n, C, H) + t.shape[3:]), 3, 2)

    q, k, v, g, beta = blk(q), blk(k), blk(v), blk(g), blk(beta)
    gc = jnp.cumsum(g, axis=-1)
    idx = jnp.arange(C)
    tril = idx[:, None] >= idx[None, :]
    strict = idx[:, None] > idx[None, :]
    diff = gc[..., :, None] - gc[..., None, :]
    decay = jnp.where(tril, jnp.exp(jnp.where(tril, diff, 0.0)), 0.0)
    kb = k * beta[..., None]
    A = jnp.where(strict, jnp.einsum('bnhid,bnhjd->bnhij', kb, k) * decay, 0.0)
    rhs = jnp.concatenate([v * beta[..., None], kb * jnp.exp(gc)[..., None]], axis=-1)
    sol = lax.linalg.triangular_solve(A + jnp.eye(C, dtype=A.dtype), rhs, left_side=True, lower=True)
    u, w = sol[..., :dv], sol[..., dv:]
    aqk = jnp.einsum('bnhid,bnhjd->bnhij', q, k) * decay
    qg = q * jnp.exp(gc)[..., None]
    kd = k * jnp.exp(gc[..., -1:] - gc)[..., None]
    dch = jnp.exp(gc[..., -1])

    def step(S, inp):
        qg_i, kd_i, u_i, w_i, aqk_i, dch_i = inp
        v_new = u_i - jnp.einsum('bhcd,bhde->bhce', w_i, S)
        o_i = jnp.einsum('bhcd,bhde->bhce', qg_i, S) + jnp.einsum('bhij,bhje->bhie', aqk_i, v_new)
        S = S * dch_i[..., None, None] + jnp.einsum('bhcd,bhce->bhde', kd_i, v_new)
        return S, o_i

    xs = tuple(jnp.moveaxis(t, 1, 0) for t in (qg, kd, u, w, aqk, dch))
    S, o = lax.scan(step, S0, xs)
    o = jnp.moveaxis(jnp.moveaxis(o, 0, 1), 2, 3).reshape(Bsz, L, H, dv)
    return o, S

def ssd_chunked(x, dt, A, Bm, Cm, S0):
    Bsz, L, H, P = x.shape
    G, N = Bm.shape[2], Bm.shape[3]
    R = H // G
    C = chunk_len(L)
    n = L // C
    xdt = (x * dt[..., None]).reshape(Bsz, n, C, G, R, P)
    dA = (dt * A).reshape(Bsz, n, C, G, R).transpose(0, 1, 3, 4, 2)
    cs = jnp.cumsum(dA, axis=-1)
    idx = jnp.arange(C)
    tril = idx[:, None] >= idx[None, :]
    seg = cs[..., :, None] - cs[..., None, :]
    Lmat = jnp.where(tril, jnp.exp(jnp.where(tril, seg, 0.0)), 0.0)
    Bc = Bm.reshape(Bsz, n, C, G, N)
    Cc = Cm.reshape(Bsz, n, C, G, N)
    CB = jnp.einsum('bclgs,bcmgs->bcglm', Cc, Bc)
    y_diag = jnp.einsum('bcglm,bcgrlm,bcmgrp->bclgrp', CB, Lmat, xdt)
    decay_in = jnp.exp(cs)
    decay_out = jnp.exp(cs[..., -1:] - cs)
    chunk_decay = jnp.exp(cs[..., -1])

    def step(S, inp):
        Cc_i, Bc_i, xdt_i, din, dout, dch = inp
        y_off = jnp.einsum('blgs,bgrps,bgrl->blgrp', Cc_i, S, din)
        S = S * dch[..., None, None] + jnp.einsum('blgs,bgrl,blgrp->bgrps', Bc_i, dout, xdt_i)
        return S, y_off

    xs = tuple(jnp.moveaxis(t, 1, 0) for t in (Cc, Bc, xdt, decay_in, decay_out, chunk_decay))
    S, y_off = lax.scan(step, S0.reshape(Bsz, G, R, P, N), xs)
    y = y_diag + jnp.moveaxis(y_off, 0, 1)
    return y.reshape(Bsz, L, H, P), S.reshape(Bsz, H, P, N)

def mem_kv(mem, g_mem, w_mk, w_mv):
    Bsz = mem.shape[0]
    m = rmsnorm(mem, g_mem)
    k = (m @ w_mk).reshape(Bsz, N_MEM, X_HEADS, X_HEADDIM)
    v = (m @ w_mv).reshape(Bsz, N_MEM, X_HEADS, X_HEADDIM)
    return k, v

def cross_attn(h, mk, mv, w_cq, w_co):
    Bsz, L, _ = h.shape
    q = (h @ w_cq).reshape(Bsz, L, X_HEADS, X_HEADDIM)
    s = jnp.einsum('blhd,bmhd->bhlm', q, mk.astype(h.dtype)).astype(jnp.float32) * (X_HEADDIM ** -0.5)
    p = jax.nn.softmax(s, axis=-1).astype(h.dtype)
    o = jnp.einsum('bhlm,bmhd->blhd', p, mv.astype(h.dtype)).reshape(Bsz, L, D_MODEL)
    return o @ w_co

def block(x, mk, mv, gdn_buf, gdn_S, ssm_buf, ssm_S,
          g_mix, w_in, gdn_conv_w, gdn_A_log, gdn_dt_bias, gdn_norm_w, w_gdn_up,
          ssm_conv_w, ssm_conv_b, ssm_dt_bias, ssm_A_log, ssm_D, ssm_norm_w, w_ssm_up, w_out,
          g_x, w_cq, w_co, g_ff, w_ff_up, w_ff_down):
    f32 = jnp.float32
    Bsz, L, _ = x.shape
    h = rmsnorm(x, g_mix)
    proj = h @ w_in
    qkv, gdn_gate, b_raw, a_raw, z, xbc, dt_raw, gate_a, gate_b = split_cols(proj, IN_SPLITS)
    qkv, gdn_buf_new = causal_dwconv(qkv, gdn_buf, gdn_conv_w)
    qkv = jax.nn.silu(qkv).astype(f32)
    q, k, v = split_cols(qkv, (GDN_QK, GDN_QK, GDN_V))
    q = l2norm(q.reshape(Bsz, L, GDN_HEADS, GDN_DK)) * (GDN_DK ** -0.5)
    k = l2norm(k.reshape(Bsz, L, GDN_HEADS, GDN_DK))
    v = v.reshape(Bsz, L, GDN_HEADS, GDN_DV)
    beta = jax.nn.sigmoid(b_raw.astype(f32))
    g = -jnp.exp(gdn_A_log.astype(f32)) * jax.nn.softplus(a_raw.astype(f32) + gdn_dt_bias.astype(f32))
    o_a, gdn_S_new = gated_delta_chunked(q, k, v, g, beta, gdn_S.astype(f32))
    o_a = rmsnorm(o_a, gdn_norm_w) * jax.nn.silu(gdn_gate.astype(f32).reshape(Bsz, L, GDN_HEADS, GDN_DV))
    o_a = o_a.reshape(Bsz, L, GDN_V).astype(x.dtype)
    xbc, ssm_buf_new = causal_dwconv(xbc, ssm_buf, ssm_conv_w)
    xbc = jax.nn.silu(xbc + ssm_conv_b).astype(f32)
    xs_, Bm, Cm = split_cols(xbc, (SSM_DINNER, SSM_BC, SSM_BC))
    xs_ = xs_.reshape(Bsz, L, SSM_HEADS, SSM_HEADDIM)
    dt = jax.nn.softplus(dt_raw.astype(f32) + ssm_dt_bias.astype(f32))
    A = -jnp.exp(ssm_A_log.astype(f32))
    y_b, ssm_S_new = ssd_chunked(xs_, dt, A, Bm.reshape(Bsz, L, SSM_GROUPS, SSM_DSTATE),
                                 Cm.reshape(Bsz, L, SSM_GROUPS, SSM_DSTATE), ssm_S.astype(f32))
    y_b = y_b + ssm_D.astype(f32)[:, None] * xs_
    y_b = y_b.reshape(Bsz, L, SSM_DINNER) * jax.nn.silu(z.astype(f32))
    y_b = rmsnorm(y_b.reshape(Bsz, L, SSM_GROUPS, SSM_DINNER // SSM_GROUPS),
                  ssm_norm_w.reshape(SSM_GROUPS, SSM_DINNER // SSM_GROUPS))
    y_b = y_b.reshape(Bsz, L, SSM_DINNER).astype(x.dtype)
    merged = jax.nn.sigmoid(gate_a) * (o_a @ w_gdn_up) + jax.nn.sigmoid(gate_b) * (y_b @ w_ssm_up)
    x = x + merged @ w_out
    x = x + cross_attn(rmsnorm(x, g_x), mk, mv, w_cq, w_co)
    hf = rmsnorm(x, g_ff) @ w_ff_up
    x = x + jnp.square(jax.nn.relu(hf)) @ w_ff_down
    return x, gdn_buf_new, gdn_S_new.astype(x.dtype), ssm_buf_new, ssm_S_new.astype(x.dtype)

def setup_inputs(seed: int = 0) -> dict:
    key = jax.random.key(seed)
    ks = iter(jax.random.split(key, 64))

    def nrm(shape, scale=1.0):
        return jax.random.normal(next(ks), shape, jnp.float32) * scale

    def gain(shape):
        return 1.0 + nrm(shape, 0.02)

    def inv_softplus_dt(shape):
        dt = jnp.exp(jax.random.uniform(next(ks), shape, jnp.float32, np.log(1e-3), np.log(1e-1)))
        return dt + jnp.log(-jnp.expm1(-dt))

    def a_log(shape):
        return jnp.log(jax.random.uniform(next(ks), shape, jnp.float32, 1.0, 16.0))

    Ld = DEPTH
    inp = {}
    inp['x_prompt'] = nrm((BATCH, SEQ, D_MODEL))
    inp['x_sample'] = nrm((DEC_BATCH, DEC_SEQ, D_MODEL))
    inp['mem_prompt'] = nrm((BATCH, N_MEM, D_MODEL))
    inp['state_gdn_conv'] = nrm((Ld, DEC_BATCH, CONV_W - 1, GDN_CONV_CH))
    inp['state_gdn'] = nrm((Ld, DEC_BATCH, GDN_HEADS, GDN_DK, GDN_DV), 0.1)
    inp['state_ssm_conv'] = nrm((Ld, DEC_BATCH, CONV_W - 1, SSM_CONV_CH))
    inp['state_ssm'] = nrm((Ld, DEC_BATCH, SSM_HEADS, SSM_HEADDIM, SSM_DSTATE), 0.1)
    inp['cache_mem_k'] = nrm((Ld, DEC_BATCH, N_MEM, X_HEADS, X_HEADDIM))
    inp['cache_mem_v'] = nrm((Ld, DEC_BATCH, N_MEM, X_HEADS, X_HEADDIM))
    inp['g_mix'] = gain((Ld, D_MODEL))
    inp['w_in'] = nrm((Ld, D_MODEL, IN_COLS), D_MODEL ** -0.5)
    inp['gdn_conv_w'] = nrm((Ld, CONV_W, GDN_CONV_CH), CONV_W ** -0.5)
    inp['gdn_A_log'] = a_log((Ld, GDN_HEADS))
    inp['gdn_dt_bias'] = inv_softplus_dt((Ld, GDN_HEADS))
    inp['gdn_norm_w'] = gain((Ld, GDN_DV))
    inp['w_gdn_up'] = nrm((Ld, GDN_V, D_MODEL), GDN_V ** -0.5)
    inp['ssm_conv_w'] = nrm((Ld, CONV_W, SSM_CONV_CH), CONV_W ** -0.5)
    inp['ssm_conv_b'] = nrm((Ld, SSM_CONV_CH), 0.01)
    inp['ssm_dt_bias'] = inv_softplus_dt((Ld, SSM_HEADS))
    inp['ssm_A_log'] = a_log((Ld, SSM_HEADS))
    inp['ssm_D'] = gain((Ld, SSM_HEADS))
    inp['ssm_norm_w'] = gain((Ld, SSM_DINNER))
    inp['w_ssm_up'] = nrm((Ld, SSM_DINNER, D_MODEL), SSM_DINNER ** -0.5)
    inp['w_out'] = nrm((Ld, D_MODEL, D_MODEL), D_MODEL ** -0.5)
    inp['g_mem'] = gain((Ld, D_MODEL))
    inp['w_mk'] = nrm((Ld, D_MODEL, D_MODEL), D_MODEL ** -0.5)
    inp['w_mv'] = nrm((Ld, D_MODEL, D_MODEL), D_MODEL ** -0.5)
    inp['g_x'] = gain((Ld, D_MODEL))
    inp['w_cq'] = nrm((Ld, D_MODEL, D_MODEL), D_MODEL ** -0.5)
    inp['w_co'] = nrm((Ld, D_MODEL, D_MODEL), D_MODEL ** -0.5)
    inp['g_ff'] = gain((Ld, D_MODEL))
    inp['w_ff_up'] = nrm((Ld, D_MODEL, D_FF), D_MODEL ** -0.5)
    inp['w_ff_down'] = nrm((Ld, D_FF, D_MODEL), D_FF ** -0.5)
    inp['g_final'] = gain((D_MODEL,))
    return inp

def reference(x_prompt, x_sample, mem_prompt, state_gdn_conv, state_gdn, state_ssm_conv, state_ssm,
              cache_mem_k, cache_mem_v, g_mix, w_in, gdn_conv_w, gdn_A_log, gdn_dt_bias, gdn_norm_w, w_gdn_up,
              ssm_conv_w, ssm_conv_b, ssm_dt_bias, ssm_A_log, ssm_D, ssm_norm_w, w_ssm_up, w_out,
              g_mem, w_mk, w_mv, g_x, w_cq, w_co, g_ff, w_ff_up, w_ff_down, g_final):
    xp, xs = x_prompt, x_sample
    Bp = x_prompt.shape[0]
    p_gc, p_g, p_sc, p_s, p_mk, p_mv = [], [], [], [], [], []
    s_gc, s_g, s_sc, s_s = [], [], [], []
    for l in range(DEPTH):
        lw = (g_mix[l], w_in[l], gdn_conv_w[l], gdn_A_log[l], gdn_dt_bias[l], gdn_norm_w[l], w_gdn_up[l],
              ssm_conv_w[l], ssm_conv_b[l], ssm_dt_bias[l], ssm_A_log[l], ssm_D[l], ssm_norm_w[l], w_ssm_up[l],
              w_out[l], g_x[l], w_cq[l], w_co[l], g_ff[l], w_ff_up[l], w_ff_down[l])
        mk, mv = mem_kv(mem_prompt, g_mem[l], w_mk[l], w_mv[l])
        zb_g = jnp.zeros((Bp, CONV_W - 1, GDN_CONV_CH), xp.dtype)
        zs_g = jnp.zeros((Bp, GDN_HEADS, GDN_DK, GDN_DV), jnp.float32)
        zb_s = jnp.zeros((Bp, CONV_W - 1, SSM_CONV_CH), xp.dtype)
        zs_s = jnp.zeros((Bp, SSM_HEADS, SSM_HEADDIM, SSM_DSTATE), jnp.float32)
        xp, bg, sg, bs, ss = block(xp, mk, mv, zb_g, zs_g, zb_s, zs_s, *lw)
        p_gc.append(bg); p_g.append(sg); p_sc.append(bs); p_s.append(ss); p_mk.append(mk); p_mv.append(mv)
        xs, bg2, sg2, bs2, ss2 = block(xs, cache_mem_k[l], cache_mem_v[l], state_gdn_conv[l], state_gdn[l],
                                       state_ssm_conv[l], state_ssm[l], *lw)
        s_gc.append(bg2); s_g.append(sg2); s_sc.append(bs2); s_s.append(ss2)
    y_prompt = rmsnorm(xp, g_final)
    y_sample = rmsnorm(xs, g_final)
    return (y_prompt, y_sample, jnp.stack(p_gc), jnp.stack(p_g), jnp.stack(p_sc), jnp.stack(p_s),
            jnp.stack(p_mk), jnp.stack(p_mv), jnp.stack(s_gc), jnp.stack(s_g), jnp.stack(s_sc), jnp.stack(s_s))


_drawn_inputs = setup_inputs


def setup_inputs(seed=0):
    import zlib

    import numpy as np

    out = dict(_drawn_inputs(seed))
    spreads = {}
    factors = {'gdn_norm_w': 8.0,
     'ssm_conv_b': 3.755,
     'ssm_D': 8.0,
     'ssm_norm_w': 5.609,
     'g_mem': 2.848,
     'g_x': 8.0,
     'g_ff': 3.277,
     'g_final': 2.846}
    for name, (base, spread) in spreads.items():
        noise = np.random.default_rng([zlib.crc32(name.encode()), seed]).standard_normal(out[name].shape)
        drawn = base * np.exp(spread * noise) if base else spread * noise
        out[name] = __import__('jax').numpy.asarray(drawn.astype(out[name].dtype))
    for name, factor in factors.items():
        out[name] = (out[name] * factor).astype(out[name].dtype)
    return out
```

```python
from contextlib import ExitStack

import concourse.bass as bass
from concourse import mybir

F32 = mybir.dt.float32
ALU = mybir.AluOpType
ACT = mybir.ActivationFunctionType
AX_X = mybir.AxisListType.X

P = 128


def wait(eng, sem, value):
    if isinstance(value, int) and value <= 0:
        return
    eng.wait_ge(sem, value)


class Banks:

    def __init__(self, base, names):
        self.base, self.place, self.per = dict(base), {}, {b: 0 for b in base}
        nxt, ring = 0, sorted(base)
        for name in names:
            if isinstance(name, tuple):
                name, bank = name
            else:
                bank = ring[nxt % len(ring)]
                nxt += 1
            self.place[name] = (bank, self.per[bank])
            self.per[bank] += 1

    def bank(self, name):
        return self.place[name][0]

    def before(self, name, it=0):
        b, n = self.place[name]
        return self.base[b] + it * self.per[b] + n

    def after(self, name, it=0):
        b, n = self.place[name]
        return it * self.per[b] + (self.base[b] + n + 1)

    def next_base(self, iterations=1):
        return {b: self.base[b] + iterations * self.per[b] for b in self.base}


class Lane:

    def __init__(self, eng, sem):
        self.eng, self.sem, self.n = eng, sem, 0

    def step(self, ins):
        if ins is self.eng:
            ins.sem_inc(self.sem, 1)
        else:
            ins.then_inc(self.sem, 1)
        self.n += 1

    def settle(self):
        if self.n:
            self.eng.wait_ge(self.sem, self.n)

    def restart(self):
        self.settle()
        self.eng.sem_clear(self.sem)
        self.n = 0


def hybrid_step(nc, io):
    x_prompt, x_sample, mem_prompt = io["x_prompt"], io["x_sample"], io["mem_prompt"]
    T, D = x_prompt.shape[1:]
    NB = x_sample.shape[0]
    NT = T + NB
    KT = D // P
    NC = T // P
    NG = 3
    GW = NT // NG
    GH_N = io["state_gdn"].shape[2]
    GC = io["gdn_conv_w"].shape[2]
    GQ = GC // 3
    SC_ = io["ssm_conv_w"].shape[2]
    SH_N = io["ssm_A_log"].shape[1]
    SDI = io["w_ssm_up"].shape[1]
    SG_N = 8
    HPG = SH_N // SG_N
    HD = SDI // SH_N
    FF = io["w_ff_up"].shape[2]
    CW = io["gdn_conv_w"].shape[1]
    CT_N = (GC + SC_) // P
    GT_N = GC // P
    EPS = 1e-6
    assert NG * GW == NT and GW <= 512 and HD * 2 == P and CW == 4

    c_qkv, c_ggate = 0, GC
    c_b = c_ggate + GQ
    c_a = c_b + GH_N
    c_z = c_a + GH_N
    c_xbc = c_z + SDI
    c_dt = c_xbc + SC_
    c_ga = c_dt + SH_N
    c_gb = c_ga + D

    with ExitStack() as ctx:
        def sb(name, cols, rows=P):
            return ctx.enter_context(nc.sbuf_tensor(name, [rows, cols], F32))

        def sem(name):
            return ctx.enter_context(nc.semaphore(name))

        def scratch(name, shape):
            return nc.dram_tensor(name, shape, F32).ap()

        d_xT = scratch("d_xT", [KT, P, NT])
        d_rows = scratch("d_rows", [SH_N + GH_N, T])
        d_gb8 = scratch("d_gb8", [2, GH_N * NB])
        d_mg = scratch("d_mg", [KT, P, NT])
        d_yb = scratch("d_yb", [SDI // P, P, NT])

        ident = sb("ident", P)
        ones = sb("ones", P)
        triu = sb("triu", P)
        eps = sb("eps", 1)
        VT_N = 5 * KT + SDI // P + 1
        vt = sb("vt", VT_N)
        tables = sb("tables", 7 * P + NB * P + CT_N * 29 + GH_N * 5 * NC + SG_N * 4 * NC * HPG)
        tcut = [0]

        def table(cols):
            tcut[0] += cols
            return tables[:, tcut[0] - cols:tcut[0]]

        lvl = table(7 * P)
        bd8 = table(NB * P)[0:NB, :]
        ct = table(CT_N * 29)
        ctv = ct[:, :].rearrange("p (t r) -> p t r", r=29)
        gh = table(GH_N * 5 * NC)
        sh = table(SG_N * 4 * NC * HPG)
        dtx = sb("dtx", (SH_N // 2) * 17)
        gb8 = sb("gb8", GH_N * NB)
        bb8 = sb("bb8", GH_N * NB)
        xn = sb("xn", KT * NT)
        xnv = xn[:, :].rearrange("p (k t) -> p k t", k=KT)
        slab = [sb(f"slab{i}", KT * P) for i in range(2)]
        slabv = [s[:, :].rearrange("p (k c) -> p k c", k=KT) for s in slab]
        AR = 37100
        arena = sb("arena", AR)
        cut = [0]

        def carve(cols):
            a = cut[0]
            cut[0] += cols
            assert cut[0] <= AR, cut[0]
            return arena[:, a:a + cols]

        psum = ctx.enter_context(nc.psum_tensor("psum", [P, 8, 512], F32))

        slab_loaded = [sem(f"slab_loaded{i}") for i in range(2)]
        proj_full = sem("proj_full")
        proj_taken = sem("proj_taken")
        bank_full = {b: sem(f"bank_full{b}") for b in range(3, 8)}
        bank_taken = {b: sem(f"bank_taken{b}") for b in range(3, 8)}
        phase_done = sem("phase_done")
        pe_step, act_step, dve_step, pool_step = (sem(n) for n in ("pe_step", "act_step", "dve_step", "pool_step"))
        consts_ready = sem("consts_ready")
        params_loaded = sem("params_loaded")
        x_loaded = sem("x_loaded")
        sq_ready = sem("sq_ready")
        rn_ready = sem("rn_ready")
        raw72_done, rows_ready, rx_ready, tab_exp = (sem(n) for n in ("raw72_done", "rows_ready", "rx_ready", "tab_exp"))
        dve_to_act, act_to_dve = sem("dve_to_act"), sem("act_to_dve")
        gbr_loaded, sdec_loaded, sdec_stored, S_stored, rw_stored = (
            sem(n) for n in ("gbr_loaded", "sdec_loaded", "sdec_stored", "S_stored", "rw_stored"))
        qg_ready = sem("qg_ready")
        tanh_ready = sem("tanh_ready")
        tanh_used = sem("tanh_used")
        conv_done = sem("conv_done")
        qkv_ready = sem("qkv_ready")
        gate_ready = sem("gate_ready")
        cw_ready, hs_ready = sem("cw_ready"), sem("hs_ready")
        dec_diff, dec_exp, dec_masked, eg_ready = (sem(n) for n in ("dec_diff", "dec_exp", "dec_masked", "eg_ready"))
        am_full_ready = sem("am_full_ready")
        am_ready = sem("am_ready")
        sd_ready = sem("sd_ready")
        oa_ready = sem("oa_ready")
        sum_taken = sem("sum_taken")
        tg_ready = sem("tg_ready")
        mg_ready, mg_stored = sem("mg_ready"), [sem(f"mg_stored{i}") for i in range(2)]
        sp_step = sem("sp_step")
        csb_loaded, ssd_loaded, ssd_stored, stf_stored, srw_stored, yb_stored, late_loaded = (
            sem(n) for n in ("csb_loaded", "ssd_loaded", "ssd_stored", "stf_stored", "srw_stored", "yb_stored",
                             "late_loaded"))
        sconv_done, sx_ready, z_ready, stanh_ready, stanh_used = (
            sem(n) for n in ("sconv_done", "sx_ready", "z_ready", "stanh_ready", "stanh_used"))
        scw_ready, shx_ready, sdiff, sdec_exp, ecs_ready, ml_ready, cd_ready, ssd_ready, y_ready, yb_ready = (
            sem(n) for n in ("scw_ready", "shx_ready", "sdiff", "sdec_exp", "ecs_ready", "ml_ready", "cd_ready",
                             "ssd_ready", "y_ready", "yb_ready"))
        x_used = sem("x_used")
        mem_loaded, mem_stored, copies_done, gfin_loaded = (
            sem(n) for n in ("mem_loaded", "mem_stored", "copies_done", "gfin_loaded"))
        kc_loaded = [sem(f"kc_loaded{i}") for i in range(2)]
        vc_loaded = [sem(f"vc_loaded{i}") for i in range(2)]
        q_ready, vh_ready, mx_ready, rs_ready, p_ready = (
            sem(n) for n in ("q_ready", "vh_ready", "mx_ready", "rs_ready", "p_ready"))
        kprod_ready, s8_ready, m4_ready, p4_ready = (
            sem(n) for n in ("kprod_ready", "s8_ready", "m4_ready", "p4_ready"))
        yt_ready, y_stored = sem("yt_ready"), sem("y_stored")
        stored = sem("stored")

        w_in = io["w_in"][0].rearrange("(k p) c -> p k c", p=P)

        v_mix, v_mem, v_x, v_ff, v_fin, v_ssm = 0, KT, 2 * KT, 3 * KT, 4 * KT, 5 * KT
        v_gdn = v_ssm + SDI // P

        cut[0] = 0
        xload = carve(9 * D).rearrange("p (t d) -> p t d", t=9)
        xT = carve(KT * NT).rearrange("p (k t) -> p k t", k=KT)
        cstage = carve(GC + SC_)
        vstage = carve(P)
        expand = carve(SH_N * HD)
        wsc = carve(KT * 72).rearrange("p (k c) -> p k c", k=KT)
        raw72 = carve(NT)
        hb = carve(2)
        sp_t = carve(NT)
        xl_flat = arena[:, 0:9 * D]
        t_e, t_u, t_l, t_c = (xl_flat[:, i * NT:(i + 1) * NT] for i in range(4))
        rows72 = xl_flat[:, 4 * NT:5 * NT]
        tok72 = xl_flat[:, 5 * NT:5 * NT + NC * 72].rearrange("p (c h) -> p c h", c=NC)
        tokd = xl_flat[:, 6 * NT:6 * NT + NC * 32].rearrange("p (c h) -> p c h", c=NC)
        cst = xl_flat[:, 6 * NT + 256:6 * NT + 256 + 320].rearrange("p (c h) -> p c h", c=NC)
        tote = xl_flat[:, 6 * NT + 576:6 * NT + 576 + 320].rearrange("p (c h) -> p c h", c=NC)
        dout = xl_flat[:, 7 * NT:7 * NT + 320].rearrange("p (c h) -> p c h", c=NC)
        rx = carve(17)
        egc = carve(GH_N * NC).rearrange("p (c h) -> p c h", c=NC)
        stat = carve(9)
        rnorm = carve(9)
        csr_full = carve(T)

        cut[0] = 0
        oa = carve(KT * NT)
        oav = oa.rearrange("p (k t) -> p k t", k=KT)
        raw = [carve(NT + 3) for _ in range(3)]
        conv = [carve(NT) for _ in range(3)]
        ggr, ggs = carve(NT), carve(NT)
        tnh = [carve(NT) for _ in range(2)]
        qn, kn = carve(NT), carve(NT)
        gbr = carve(T)
        dec1, dec2 = carve(T), carve(T)
        amat, aml1 = carve(T), carve(T)
        aml0 = dec1
        X, Y, Pp = carve(T), carve(T), carve(T)
        kbe, kd, vb, qg = carve(T), carve(T), carve(T), carve(T)
        wtn = X
        aml = [aml0, aml1]
        vnew = [carve(P) for _ in range(2)]
        Sst = [carve(P) for _ in range(2)]
        oT = carve(NT)
        sdec = carve(NB * P)
        hs = carve(5 * NC)
        hs8 = carve(2 * NB)
        st2, rn2 = carve(18), carve(18)
        cwf = carve(3 * 29).rearrange("p (u r) -> p u r", u=3)
        rwst = carve(3 * P)
        k8, v8n, vs8 = carve(P), carve(NB), carve(NB)
        tap = carve(512 + NB)
        vbd = amat
        sq2 = qn

        cut[0] = KT * NT
        tgate = [carve(NT) for _ in range(2)]
        mgst = [carve(NT) for _ in range(2)]

        cut[0] = 0
        sraw = [carve(NT + 3) for _ in range(4)]
        sconv = [carve(NT) for _ in range(4)]
        zraw, zs = [carve(NT) for _ in range(2)], [carve(NT) for _ in range(2)]
        stnh = [carve(NT) for _ in range(2)]
        csb = carve(HPG * T)
        btok = carve(T)
        xdt, xdd = carve(T * 2), carve(T * 2)
        cbm = carve(T)
        ml = carve(HPG * T)
        SST = [carve(2 * P) for _ in range(2)]
        yT = [carve(NT) for _ in range(2)]
        ml_sq = [ml[:, 0:NT], ml[:, NT:2 * NT]]
        ssd = carve(2 * NB * P)
        shs, shx, snw = carve(4 * NC * HPG), carve(2 * 17), carve(2)
        scw = carve(4 * 29).rearrange("p (u r) -> p u r", u=4)
        bdg, cdg = carve(NB * P), carve(NB * P)
        stmp = carve(4 * P)
        ssq, srn = carve(9), carve(9)
        xdts, ysm = carve(2 * NB), carve(2 * NB)
        srw = carve(4 * P)
        stf = carve(2 * P)
        stap = lvl[:, 0:512 + NB]

        cut[0] = 0
        x1 = carve(KT * NT)
        x1v = x1.rearrange("p (k t) -> p k t", k=KT)
        mg = carve(KT * NT)
        mgv = mg.rearrange("p (k t) -> p k t", k=KT)
        yb = carve(2 * KT * NT)
        ybv = yb.rearrange("p (k t) -> p k t", k=2 * KT)
        tgate2 = [carve(NT) for _ in range(2)]
        tsum = carve(NT)

        tcut[0] = 0
        spare = table

        M_N, XH_N = io["cache_mem_k"].shape[2], io["cache_mem_k"].shape[3]
        MT, XD = M_N // P, D // XH_N
        assert MT == 2 and XD == 2 * P and KT * P == XH_N * XD and NB == 2 * XH_N
        x_scale = float(XD) ** -0.5
        cut[0] = KT * NT
        qT = carve(KT * NT)
        at = carve(KT * NT)
        atv = at.rearrange("p (k t) -> p k t", k=KT)
        KTm = carve(KT * M_N)
        Vtok = carve(MT * D).rearrange("p (t c) -> p t c", t=MT)
        kc = [carve(MT * D).rearrange("p (t c) -> p t c", t=MT) for _ in range(2)]
        vc = [carve(MT * D).rearrange("p (t c) -> p t c", t=MT) for _ in range(2)]
        memtok, memT, memsq = kc[0], kc[1].rearrange("p t c -> p (t c)"), vc[0].rearrange("p t c -> p (t c)")
        memTv, memsqv = (m.rearrange("p (k m) -> p k m", k=KT) for m in (memT, memsq))
        mn = qT[:, 0:KT * M_N].rearrange("p (k m) -> p k m", k=KT)
        Ktok = at[:, 0:MT * D].rearrange("p (t c) -> p t c", t=MT)
        cut2 = [0]

        def part(buf, at_, n):
            at_[0] += n
            return buf[:, at_[0] - n:at_[0]]

        qtok = part(xn, cut2, D)
        qm = [part(xn, cut2, D) for _ in range(2)]
        pr = [part(xn, cut2, 4 * M_N).rearrange("p (c m) -> p c m", c=4) for _ in range(2)]
        PT = part(xn, cut2, 4 * M_N).rearrange("p (t i) -> p t i", t=MT)
        qh = [part(xn, cut2, 2 * 512).rearrange("p (k i) -> p k i", k=2) for _ in range(2)]
        vh = spare(MT * XD).rearrange("p (t d) -> p t d", t=MT)
        qrep = [spare(D), spare(D)]
        xstat, xrn, mstat, mrn = spare(9), spare(9), spare(MT), spare(MT)
        nmx, psm, prs = ([spare(4) for _ in range(2)] for _ in range(3))
        s8 = [spare(MT * XH_N).rearrange("p (t h) -> p t h", t=MT) for _ in range(2)]
        pT8 = [spare(MT * XH_N) for _ in range(2)]
        mx4, sm4, r4 = ([spare(1) for _ in range(2)] for _ in range(3))
        e4 = [spare(M_N) for _ in range(2)]

        cut[0] = KT * NT
        hf = carve(2 * KT * NT)
        hfv = hf.rearrange("p (k t) -> p k t", k=2 * KT)
        gfin = carve(D)
        ytok = hf[:, 0:9 * D].rearrange("p (c d) -> p c d", c=9)

        base0 = {b: 0 for b in range(3, 8)}
        setup_plan = Banks(base0, [f"xt{t}_{j}" for t in range(9) for j in range(2)]
                           + ["vt"] + [f"ct{i}" for i in range(4)]
                           + ["st", "bc0", "bc1", "bc2"]
                           + ["sc0", "sc1", "sc2"] + ["ta0", "ta1", "td", "cs", "tot", "csr0", "csr1", "dtx"])
        names = ["rw", "st", "bq0", "bq1", "bk0", "bk1", "b8", "tv0", "tv1", "tk0", "tk1", "t8",
                 "kk0", "kk1", "qk0", "qk1", "y0", "y1"]
        for L in range(1, 7):
            names += [f"p{L}_0", f"p{L}_1"]
            for j in range(2):
                names += [f"yp{L}_{j}"] + ([f"xp{L}_{j}"] if L < 6 else [])
        names += ["w0", "w1"]
        for c in range(NC):
            if c % 4 == 0:
                names += [(f"ot{c // 4}", 7)]
            names += [(f"vn{c}", 3 + c % 2), (f"su{c}", 5 + c % 2)]
        names += ["ks", "v8", "oo0", "oo1", "od", "nst", "nb0", "nb1", "nb8"]
        gdn_plan = Banks(setup_plan.next_base(), names)
        FILL = {"rw": 8, "norm": 8, "turn": 8, "kkqk": 8, "scan": 4, "decode": 8, "level": 4}
        STEPS = ["rw", "norm", "turn", "kkqk"] + [f"level{L}" for L in range(1, 7)] \
            + [f"scan{c}" for c in range(NC)] + ["decode"]

        def fills(step):
            n = lambda s: FILL[s.rstrip("0123456789")]
            i = STEPS.index(step)
            return sum(n(s) for s in STEPS[:i]), sum(n(s) for s in STEPS[:i + 1])

        snames = ["rw"] + ["tb0", "tb1", "tx0", "tx1", "tx2", "tx3", "t8", "cb0", "cb1"]
        for c in range(NC):
            snames += [(f"su{c}", 5 + c % 2)] + ([(f"y{c // 2}", 3 + c // 2 % 2)] if c % 2 == 0 else [])
        snames += [("fs", 7), "bb0", "bb1", "cc0", "cc1", "nst", "nb0", "nb1", "nb8"]
        ssm_plan = Banks(gdn_plan.next_base(GH_N), snames)
        SFILL = {"rw": 16, "tb": 8, "tx": 16, "cb": 24, "scan": 8, "fs": 8, "decode": 8}
        SSTEPS = ["rw", "tb", "tx", "cb"] + [f"scan{c}" for c in range(NC)] + ["fs", "decode"]

        def sfills(step):
            n = lambda s: SFILL[s.rstrip("0123456789")]
            i = SSTEPS.index(step)
            return sum(n(s) for s in SSTEPS[:i]), sum(n(s) for s in SSTEPS[:i + 1])

        mem_plan = Banks(ssm_plan.next_base(SG_N), ["mt00", "mt01", "mt10", "mt11", "xst", "mst", "mbc",
                                                    "xb0", "xb1", "xb2"] + [f"kt{i}" for i in range(4)]
                         + ["qt0", "qt1"])
        anames = [f"{n}{s}{i}" for s in range(2) for n in ("sc", "qb") for i in range(2)]
        for s in range(2):
            anames += [f"pt{s}0", f"pt{s}1", f"st{s}", f"o{s}0", f"o{s}1", f"pb{s}", f"os{s}"]
        attn_plan = Banks(mem_plan.next_base(), anames)
        ff_plan = Banks(attn_plan.next_base(XH_N), ["fst", "fb0", "fb1", "fb2", "zst"]
                        + [f"y{c}_{j}" for c in range(NC + 1) for j in range(2)])

        W_UPA = 4 * GH_N
        W_SSM = W_UPA + 2 * KT
        W_UPB = W_SSM + 6 * SG_N
        W_OUT = W_UPB + 3 * KT
        A_UPA = 3 * W_UPA
        A_SSM = A_UPA + 3 * KT
        A_UPB = A_SSM + 18 * SG_N
        V_UPB = 3 * KT
        V_OUT = V_UPB + 3 * KT
        W_MK = W_OUT + KT
        W_MV = W_MK + KT
        W_CQ = W_MV + KT
        W_CO = W_CQ + KT
        W_FU = W_CO + KT
        FH = FF // P // 2
        assert FH == 2 * KT
        A_MV = A_UPB + 3 * KT
        A_CQ = A_MV + KT
        A_END = A_CQ + 3 * KT
        V_MK = V_OUT + 3 * KT
        V_CO = V_MK + KT
        V_FU = V_CO + 3 * KT
        V_HALF = 3 * FH + 3 * KT
        SQ_SSM, RN_SSM = KT + 3 * GH_N, 1 + 2 * GH_N
        SQ_X, RN_X = SQ_SSM + 2 * SG_N, RN_SSM + SG_N

        block = ctx.enter_context(nc.Block())

        def token_range(c):
            return (c * P, (c + 1) * P) if c < NC else (NT - P, NT)

        def cols(ap, c):
            return ap[:, c * P:(c + 1) * P]

        def half(ap, j):
            return ap[:, j * 512:(j + 1) * 512].rearrange("p (c i) -> p c i", c=4)

        def spread(col, n=P):
            return col.unsqueeze(2).broadcast_to([col.shape[0], col.shape[1], n])

        def per_chunk(mat, n):
            return mat.unsqueeze(1).broadcast_to([mat.shape[0], n, mat.shape[1]])

        SETUP_ENDS = 5

        @block.sync
        def _(sp):
            def load_slab(base, it, k, src):
                wait(sp, proj_full, 3 * it + 3 * (base + k - 1))
                if not isinstance(it, int):
                    sp.sem_inc(sp_step, 1)
                sp.dma_start(slabv[k % 2], src).then_inc(slab_loaded[k % 2], 16)

            def par(dst, src):
                sp.dma_start(dst, src).then_inc(params_loaded, 16)

            for t in range(NC):
                sp.dma_start(xload[:, t, :], x_prompt[0, t * P:(t + 1) * P, :]).then_inc(x_loaded, 16)
            sp.dma_start(xload[0:NB, NC, :], x_sample[:, 0, :]).then_inc(x_loaded, 16)
            for n, name in enumerate(["g_mix", "g_mem", "g_x", "g_ff"]):
                par(vstage[n * KT:(n + 1) * KT, :], io[name][0].rearrange("(t p) -> t p", p=P))
            par(vstage[4 * KT:5 * KT, :], io["g_final"].rearrange("(t p) -> t p", p=P))
            par(vstage[v_ssm:v_gdn, :], io["ssm_norm_w"][0].rearrange("(t p) -> t p", p=P))
            par(vstage[v_gdn:VT_N, :], io["gdn_norm_w"])
            sp.wait_ge(consts_ready, 1)
            par(cstage[0:24, 0:GC], io["state_gdn_conv"][0].rearrange("b i c -> (b i) c"))
            par(cstage[0:24, GC:GC + SC_], io["state_ssm_conv"][0].rearrange("b i c -> (b i) c"))
            par(cstage[24:28, 0:GC], io["gdn_conv_w"][0])
            par(cstage[24:28, GC:GC + SC_], io["ssm_conv_w"][0])
            par(cstage[28:29, GC:GC + SC_], io["ssm_conv_b"])
            par(hb[32:32 + GH_N, 0:1], io["gdn_dt_bias"].rearrange("o h -> h o"))
            par(hb[0:SH_N, 0:1], io["ssm_dt_bias"].rearrange("o h -> h o"))
            par(hb[32:32 + GH_N, 1:2], io["gdn_A_log"].rearrange("o h -> h o"))
            par(hb[0:SH_N, 1:2], io["ssm_A_log"].rearrange("o h -> h o"))
            par(wsc[:, :, 0:SH_N], w_in[:, :, c_dt:c_dt + SH_N])
            par(wsc[:, :, 32:32 + GH_N], w_in[:, :, c_a:c_a + GH_N])
            par(wsc[:, :, 64:64 + GH_N], w_in[:, :, c_b:c_b + GH_N])
            par(rx[0:SH_N, 16:17], io["ssm_D"].rearrange("o h -> h o"))
            for b in range(3, 8):
                sp.wait_ge(bank_taken[b], setup_plan.after([n for n in setup_plan.place if n.startswith("xt")
                                                            and setup_plan.bank(n) == b][-1]))
            sp.dma_start(d_xT.rearrange("k p t -> p k t"), xT).then_inc(stored, 16)
            sp.wait_ge(rows_ready, 1)
            sp.dma_start(d_rows[:, :], csr_full[0:SH_N + GH_N, :]).then_inc(stored, 16)
            sp.dma_start(d_gb8[0].rearrange("(h b) -> h b", b=NB), rows72[32:32 + GH_N, T:NT]).then_inc(stored, 16)
            sp.dma_start(d_gb8[1].rearrange("(h b) -> h b", b=NB), rows72[64:64 + GH_N, T:NT]).then_inc(stored, 16)
            sp.wait_ge(stored, 64)
            sp.dma_start(gb8[:, :], d_gb8[0].partition_broadcast(P)).then_inc(params_loaded, 16)
            sp.dma_start(bb8[:, :], d_gb8[1].partition_broadcast(P)).then_inc(params_loaded, 16)

            for kind in ("gdn", "ssm"):
                sp.dma_start(io[f"s_{kind}_conv"][0, :, 0:CW - 2, :], io[f"state_{kind}_conv"][0, :, 1:CW - 1, :]
                             ).then_inc(copies_done, 16)

            def head_slab(h, u):
                col = h * P + (u * GQ if u < 3 else c_ggate)
                load_slab(0, 4 * h, u, w_in[:, :, bass.ds(col, P)])

            def gb_load(h):
                sp.dma_start(gbr, d_rows[bass.ds(h + SH_N, 1), :].rearrange("o t -> (o t)").partition_broadcast(P)
                             ).then_inc(gbr_loaded, 16)

            def sd_load(h):
                sp.dma_start(sdec.rearrange("p (b e) -> p b e", b=NB),
                             io["state_gdn"][0, :, bass.ds(h, 1)].rearrange("b o k e -> k (b o) e")
                             ).then_inc(sdec_loaded, 16)

            head_slab(0, 0)
            head_slab(0, 1)
            sp.drain().then_inc(phase_done, 1)
            sp.wait_ge(phase_done, SETUP_ENDS)
            gb_load(0)
            head_slab(0, 2)
            head_slab(0, 3)

            def body(h):
                wait(sp, sdec_stored, h * 16)
                sd_load(h)
                for u in range(3):
                    head_slab(h + 1, u)
                wait(sp, qg_ready, h + 1)
                gb_load(h + 1)
                head_slab(h + 1, 3)

            body(0)
            with sp.Fori(1, GH_N - 1) as h:
                body(h)
            sp.wait_ge(sdec_stored, (GH_N - 1) * 16)
            sd_load(GH_N - 1)

            w_gup = io["w_gdn_up"][0].rearrange("(k p) c -> p k c", p=P)

            def upa_slab(j, u):
                src = w_in[:, :, bass.ds(j * P + c_ga, P)] if u == 0 else w_gup[:, :, bass.ds(j * P, P)]
                load_slab(W_UPA, 2 * j, u, src)

            def merged_store(j, i):
                sp.wait_ge(mg_ready, j + i + 1)
                sp.sem_inc(sp_step, 1)
                sp.dma_start(d_mg[bass.ds(j + i, 1)].rearrange("o p t -> p (o t)"), mgst[i]).then_inc(mg_stored[i], 16)

            upa_slab(0, 0)
            upa_slab(0, 1)
            sp.drain().then_inc(phase_done, 1)
            sp.wait_ge(phase_done, 10)
            for u in range(2):
                upa_slab(1, u)
            with sp.Fori(0, KT // 2 - 1) as pair:
                j = pair * 2
                for i in range(2):
                    for u in range(2):
                        upa_slab(j + (2 + i), u)
                    merged_store(j, i)
            for i in range(2):
                merged_store(KT - 2, i)

            def ssm_slab(g, u):
                col = [g * P + (c_xbc + SDI), g * P + (c_xbc + SDI + SG_N * P), g * 2 * P + c_xbc,
                       g * 2 * P + (c_xbc + P), g * 2 * P + c_z, g * 2 * P + (c_z + P)][u]
                load_slab(W_SSM, 6 * g, u, w_in[:, :, bass.ds(col, P)])

            def csb_load(g):
                for r in range(HPG):
                    sp.dma_start(csb[:, r * T:(r + 1) * T],
                                 d_rows[bass.ds(HPG * g + r, 1), :].rearrange("o t -> (o t)").partition_broadcast(P)
                                 ).then_inc(csb_loaded, 16)

            s_in = io["state_ssm"][0].rearrange("b (i r) p n -> (r p) i b n", r=2)

            def ssd_load(g):
                for q in range(2):
                    sp.dma_start(ssd[:, q * NB * P:(q + 1) * NB * P].rearrange("p (b n) -> p b n", b=NB),
                                 s_in[:, bass.ds(2 * g + q, 1)].rearrange("p o b n -> p (o b) n")
                                 ).then_inc(ssd_loaded, 16)

            ssm_slab(0, 0)
            ssm_slab(0, 1)
            sp.drain().then_inc(phase_done, 1)
            sp.wait_ge(phase_done, 15)
            for u in range(2, 6):
                ssm_slab(0, u)

            def body(g, more):
                wait(sp, bank_full[ssm_plan.bank("y3")], 0 if isinstance(g, int) and g == 0
                     else ssm_plan.after("y3", g - 1))
                csb_load(g)
                if more:
                    ssm_slab(g + 1, 0)
                    ssm_slab(g + 1, 1)
                wait(sp, ssd_stored, 32 * g)
                ssd_load(g)
                if more:
                    for u in range(2, 6):
                        ssm_slab(g + 1, u)

            body(0, True)
            with sp.Fori(1, SG_N - 1) as g:
                body(g, True)
            body(SG_N - 1, False)

            w_sup = io["w_ssm_up"][0].rearrange("(s k p) c -> s p k c", p=P, k=KT)

            def upb_slab(j, i, u):
                src = (w_in[:, :, bass.ds(j * P + (c_gb + i * P), P)] if u == 0
                       else w_sup[u - 1][:, :, bass.ds(j * P + i * P, P)])
                load_slab(W_UPB, 3 * j, 3 * i + u, src)

            upb_slab(0, 0, 0)
            upb_slab(0, 0, 1)
            sp.drain().then_inc(phase_done, 1)
            sp.wait_ge(phase_done, 20)
            sp.wait_ge(yb_stored, 32 * SG_N)
            sp.dma_start(ybv, d_yb.rearrange("k p t -> p k t")).then_inc(late_loaded, 16)
            for i in range(2):
                sp.wait_ge(mg_stored[i], 16 * KT // 2)
            sp.dma_start(mgv, d_mg.rearrange("k p t -> p k t")).then_inc(late_loaded, 16)
            sp.dma_start(x1v, d_xT.rearrange("k p t -> p k t")).then_inc(late_loaded, 16)
            for i, u in ((0, 2), (1, 0), (1, 1), (1, 2)):
                upb_slab(0, i, u)
            with sp.Fori(1, KT // 2) as pair:
                j = pair * 2
                for i in range(2):
                    for u in range(3):
                        upb_slab(j, i, u)
            def square_slabs(base, w):
                wv = w.rearrange("(k p) c -> p k c", p=P)
                with sp.Fori(0, wv.shape[2] // P // 2) as pair:
                    j = pair * 2
                    for i in range(2):
                        load_slab(base, j, i, wv[:, :, bass.ds(j * P + i * P, P)])

            sp.wait_ge(sum_taken, V_OUT)
            sp.dma_start(memtok, mem_prompt[0].rearrange("(t p) c -> p t c", p=P)).then_inc(mem_loaded, 16)
            square_slabs(W_OUT, io["w_out"][0])
            sp.drain().then_inc(phase_done, 1)

            square_slabs(W_MK, io["w_mk"][0])
            square_slabs(W_MV, io["w_mv"][0])
            sp.wait_ge(sum_taken, V_MK + KT)
            sp.dma_start(io["p_mem_k"][0, 0].rearrange("(t p) h d -> p t (h d)", p=P), Ktok).then_inc(mem_stored, 16)
            square_slabs(W_CQ, io["w_cq"][0])
            sp.wait_ge(proj_taken, A_CQ)
            sp.dma_start(io["p_mem_v"][0, 0].rearrange("(t p) h d -> p t (h d)", p=P), Vtok).then_inc(mem_stored, 16)
            w_co = io["w_co"][0].rearrange("(k p) c -> p k c", p=P)
            for i in range(2):
                load_slab(W_CO, 0, i, w_co[:, :, i * P:(i + 1) * P])
            with sp.Fori(0, XH_N - 1) as h:
                for s in range(2):
                    for name, slot, loaded in (("cache_mem_k", kc[s], kc_loaded[s]), ("cache_mem_v", vc[s], vc_loaded[s])):
                        if slot is kc[s]:
                            sp.wait_ge(s8_ready, 2 * h + s + 1)
                        else:
                            sp.wait_ge(bank_full[attn_plan.bank(f"os{s}")], attn_plan.after(f"os{s}", h))
                        sp.sem_inc(sp_step, 1)
                        sp.dma_start(slot, io[name][0, bass.ds(h * 2 + (s + 2), 1)].rearrange(
                            "b (t p) h d -> p (b t) (h d)", p=P)).then_inc(loaded, 16)
            with sp.Fori(1, KT // 2) as pair:
                j = pair * 2
                for i in range(2):
                    load_slab(W_CO, j, i, w_co[:, :, bass.ds(j * P + i * P, P)])

            w_down = io["w_ff_down"][0].rearrange("(s k p) c -> s p k c", p=P, k=KT)
            for half_ in range(2):
                base = W_FU + half_ * 2 * FH
                square_slabs(base, io["w_ff_up"][0][:, half_ * FH * P:(half_ + 1) * FH * P])
                if half_ == 0:
                    sp.dma_start(gfin, io["g_final"].partition_broadcast(P)).then_inc(gfin_loaded, 16)
                with sp.Fori(0, KT) as j:
                    for u in range(2):
                        load_slab(base + FH, 2 * j, u, w_down[2 * half_ + u][:, :, bass.ds(j * P, P)])
            for c in range(NC + 1):
                sp.wait_ge(yt_ready, c + 1)
                if c < NC:
                    sp.dma_start(io["y_prompt"][0, c * P:(c + 1) * P, :], ytok[:, c, :]).then_inc(y_stored, 16)
                else:
                    sp.dma_start(io["y_sample"][:, 0, :], ytok[P - NB:P, c, :]).then_inc(y_stored, 16)
            sp.wait_ge(y_stored, 16 * (NC + 1))
            sp.wait_ge(mem_stored, 32)
            sp.wait_ge(copies_done, 32)

        @block.tensor
        def _(pe):
            def hand(plan, name, it, mms):
                b = plan.bank(name)
                wait(pe, bank_taken[b], plan.before(name, it))
                for mm in mms(psum[:, b, :]):
                    last = mm
                last.then_inc(bank_full[b], 1)

            def taken(plan, name, it=0):
                pe.wait_ge(bank_taken[plan.bank(name)], plan.after(name, it))

            def stats(sq, n, bank, col=0, k=KT):
                for c in range(NC + 1):
                    a, z = token_range(c)
                    for i in range(k):
                        yield pe.matmul(bank[:, col + c:col + c + 1], sq[i][:, a:z], ones[:, 0:1],
                                        start=(i == 0), stop=(i == k - 1))

            def across(bank, rn, cs, at=0):
                for c in cs:
                    if c < NC:
                        yield pe.matmul(bank[:, (c % 4) * P:(c % 4 + 1) * P], rn(c).broadcast_to([P, P]), ident[:, :],
                                        start=True, stop=True)
                    else:
                        yield pe.matmul(bank[:, at:at + NB], rn(c).broadcast_to([P, P]), ident[:, P - NB:P],
                                        start=True, stop=True)

            pe.wait_ge(consts_ready, 2)
            pe.wait_ge(x_loaded, 16 * 9)
            for t in range(9):
                rows = P if t < NC else NB
                for j in range(2):
                    hand(setup_plan, f"xt{t}_{j}", 0, lambda bk, t=t, j=j, rows=rows: (
                        pe.transpose(bk[:, i * P:i * P + rows], xload[0:rows, t, (4 * j + i) * P:(4 * j + i + 1) * P],
                                     ident[0:rows, 0:rows]) for i in range(4)))
            pe.wait_ge(params_loaded, 16 * 20)
            hand(setup_plan, "vt", 0, lambda bk: [pe.transpose(bk[:, 0:VT_N], vstage[0:VT_N, :], ident[0:VT_N, 0:VT_N])])
            for q in range(4):
                hand(setup_plan, f"ct{q}", 0, lambda bk, q=q: (
                    pe.transpose(bk[:, i * 29:(i + 1) * 29], cstage[0:29, (14 * q + i) * P:(14 * q + i + 1) * P],
                                 ident[0:29, 0:29]) for i in range(CT_N // 4)))
            pe.wait_ge(sq_ready, KT)
            hand(setup_plan, "st", 0, lambda bk: stats([xnv[:, k, :] for k in range(KT)], NT, bk))
            pe.wait_ge(rn_ready, 1)
            for j in range(3):
                hand(setup_plan, f"bc{j}", 0, lambda bk, j=j: across(
                    bk, lambda c: rnorm[:, c:c + 1], range(4 * j, min(4 * j + 4, NC + 1))))
            taken(setup_plan, "bc2")
            for n in range(3):
                hand(setup_plan, f"sc{n}", 0, lambda bk, n=n: (
                    pe.matmul(bk[0:72, 0:GW], wsc[:, k, :], xnv[:, k, n * GW:(n + 1) * GW],
                              start=(k == 0), stop=(k == KT - 1)) for k in range(KT)))
            pe.wait_ge(raw72_done, 1)
            for j in range(2):
                hand(setup_plan, f"ta{j}", 0, lambda bk, j=j: (
                    pe.transpose(bk[:, i * 72:(i + 1) * 72], rows72[0:72, (4 * j + i) * P:(4 * j + i + 1) * P],
                                 ident[0:72, 0:72]) for i in range(4)))
            hand(setup_plan, "td", 0, lambda bk: (
                pe.transpose(bk[:, c * 32:(c + 1) * 32], sp_t[0:32, c * P:(c + 1) * P], ident[0:32, 0:32])
                for c in range(NC)))
            taken(setup_plan, "ta0")
            taken(setup_plan, "ta1")
            hand(setup_plan, "cs", 0, lambda bk: [
                pe.matmul(bk[:, 0:40 * NC], triu[:, :], tok72[:, :, 0:40], start=True, stop=True)])
            hand(setup_plan, "tot", 0, lambda bk: [
                pe.matmul(bk[:, 0:40 * NC], ones[:, :], tok72[:, :, 0:40], start=True, stop=True)])
            for j in range(2):
                hand(setup_plan, f"csr{j}", 0, lambda bk, j=j: (
                    pe.matmul(bk[0:40, i * P:(i + 1) * P], tok72[:, 4 * j + i, 0:40], triu[:, :],
                              start=True, stop=True) for i in range(4)))
            pe.wait_ge(rx_ready, 1)
            hand(setup_plan, "dtx", 0, lambda bk: (
                pe.matmul(bk[:, i * 17:(i + 1) * 17], expand[0:SH_N, i * P:(i + 1) * P], rx[0:SH_N, :],
                          start=True, stop=True) for i in range(SH_N // 2)))
            pe.drain().then_inc(phase_done, 1)
            pe.wait_ge(phase_done, SETUP_ENDS)

            def project(it, base, m0, m1, before, act_in=None, join=()):
                for m in range(m0, m1):
                    u, n, k = m // (3 * KT), m // KT % 3, m % KT
                    if k == 0:
                        if n == 0:
                            pe.wait_ge(slab_loaded[(base + u) % 2], 8 * it + 16 * ((base + u) // 2 + 1))
                        if u not in join:
                            wait(pe, *before(u, n))
                    src = xnv if act_in is None else act_in[u]
                    mm = pe.matmul(psum[:, n, 0:GW], slabv[(base + u) % 2][:, k, :], src[:, k, n * GW:(n + 1) * GW],
                                   start=(k == 0 and u not in join), stop=(k == KT - 1 and u + 1 not in join))
                    if k == KT - 1:
                        mm.then_inc(proj_full, 1)

            def qkvg(h, m0, m1):
                project(4 * h, 0, m0, m1, lambda u, n: (proj_taken, 12 * h + 3 * u + n - 2))

            G = gdn_plan
            qkvg(0, 0, 96)

            def body(h, more):
                def fill(step, part=None):
                    if more:
                        a, z = fills(step)
                        if part is not None:
                            mid = (a + z) // 2
                            a, z = ((a, mid), (mid, z))[part]
                        qkvg(h + 1, a, z)

                pe.wait_ge(proj_taken, 12 * h + 12)
                hand(G, "rw", h, lambda bk: (
                    pe.transpose(bk[0:11, u * P:(u + 1) * P], raw[u][:, T:T + 11], ident[:, :]) for u in range(3)))
                fill("rw")
                pe.wait_ge(sq_ready, KT + 3 * h + 2)
                hand(G, "st", h, lambda bk: [m for i, s in enumerate((sq2, oT)) for m in stats([s], NT, bk, 9 * i, 1)])
                pe.wait_ge(rn_ready, 2 * h + 2)
                for i, t in enumerate("qk"):
                    for j in range(2):
                        hand(G, f"b{t}{j}", h, lambda bk, i=i, j=j: across(
                            bk, lambda c: rn2[:, 9 * i + c:9 * i + c + 1], range(4 * j, 4 * j + 4)))
                hand(G, "b8", h, lambda bk: [m for i in range(2) for m in across(
                    bk, lambda c: rn2[:, 9 * i + c:9 * i + c + 1], [NC], at=NB * i)])
                fill("norm")
                pe.wait_ge(qkv_ready, 3 * h + 3)
                for j in range(2):
                    hand(G, f"tv{j}", h, lambda bk, j=j: (
                        pe.transpose(cols(bk, i), cols(conv[2], 4 * j + i), ident[:, :]) for i in range(4)))
                taken(G, "b8", h)
                for j in range(2):
                    hand(G, f"tk{j}", h, lambda bk, j=j: (
                        pe.transpose(cols(bk, i), cols(kn, 4 * j + i), ident[:, :]) for i in range(4)))
                hand(G, "t8", h, lambda bk: [pe.transpose(bk[0:NB, 0:P], kn[:, T:NT], ident[:, :])])
                fill("turn")
                for name, rhs in (("kk", kn), ("qk", qn)):
                    for j in range(2):
                        hand(G, f"{name}{j}", h, lambda bk, j=j, rhs=rhs: (
                            pe.matmul(cols(bk, i), cols(kn, 4 * j + i), cols(rhs, 4 * j + i), start=True, stop=True)
                            for i in range(4)))
                fill("kkqk")
                pe.wait_ge(am_ready, 7 * h + 1)
                for j in range(2):
                    hand(G, f"y{j}", h, lambda bk, j=j: (
                        pe.transpose(cols(bk, i), cols(aml[0], 4 * j + i), ident[:, :]) for i in range(4)))
                for L in range(1, 7):
                    pe.wait_ge(am_ready, 7 * h + L + 1)
                    for j in range(2):
                        taken(G, f"y{j}" if L == 1 else f"yp{L - 1}_{j}", h)
                        hand(G, f"p{L}_{j}", h, lambda bk, j=j, L=L: (
                            pe.matmul(cols(bk, i), cols(aml[L % 2], 4 * j + i), cols(Y, 4 * j + i),
                                      start=True, stop=True) for i in range(4)))
                    fill(f"level{L}")
                    for j in range(2):
                        taken(G, f"p{L}_{j}", h)
                        if L > 1:
                            taken(G, f"xp{L - 1}_{j}", h)
                        hand(G, f"yp{L}_{j}", h, lambda bk, j=j: (
                            pe.matmul(cols(bk, i), cols(X, 4 * j + i), cols(Pp, 4 * j + i),
                                      start=True, stop=True) for i in range(4)))
                        if L < 6:
                            hand(G, f"xp{L}_{j}", h, lambda bk, j=j: (
                                pe.matmul(cols(bk, i), cols(Pp, 4 * j + i), cols(X, 4 * j + i),
                                          start=True, stop=True) for i in range(4)))
                for j in range(2):
                    taken(G, f"yp6_{j}", h)
                    hand(G, f"w{j}", h, lambda bk, j=j: (
                        pe.matmul(cols(bk, i), cols(kbe, 4 * j + i), cols(Y, 4 * j + i), start=True, stop=True)
                        for i in range(4)))
                pe.wait_ge(qg_ready, h + 1)
                for c in range(NC):
                    j = c // 4

                    def new_values(bk, c=c):
                        yield pe.matmul(bk[:, 0:P], cols(Y, c), cols(vb, c), start=True, stop=(c == 0))
                        if c:
                            yield pe.matmul(bk[:, 0:P], cols(wtn, c), Sst[c % 2], start=False, stop=True)

                    if c % 4 == 0:
                        taken(G, f"w{j}", h)
                    if c:
                        taken(G, f"su{c - 1}", h)
                    hand(G, f"vn{c}", h, new_values)
                    fill(f"scan{c}", 0)
                    taken(G, f"vn{c}", h)
                    hand(G, f"su{c}", h, lambda bk, c=c: [
                        pe.matmul(bk[:, 0:P], cols(kd, c), vnew[c % 2], start=True, stop=True)])
                    if c % 4 == 0:
                        wait(pe, bank_taken[7], G.before(f"ot{j}", h))
                    out = psum[:, 7, (c % 4) * P:(c % 4 + 1) * P]
                    if c:
                        pe.matmul(out, Sst[c % 2], cols(qg, c), start=True, stop=False)
                    mm = pe.matmul(out, vnew[c % 2], cols(dec2, c), start=(c == 0), stop=True)
                    if c % 4 == 3:
                        mm.then_inc(bank_full[7], 1)
                    fill(f"scan{c}", 1)
                pe.wait_ge(sd_ready, h + 1)
                sdv = sdec.rearrange("p (b e) -> p b e", b=NB)
                hand(G, "ks", h, lambda bk: (
                    pe.matmul(bk[:, b:b + 1], sdv[:, b, :], kn[:, T + b:T + b + 1], start=True, stop=True)
                    for b in range(NB)))
                taken(G, "ks", h)
                hand(G, "v8", h, lambda bk: [pe.transpose(bk[0:NB, 0:P], v8n, ident[:, :])])
                fill("decode")
                taken(G, "v8", h)
                for j in range(2):
                    hand(G, f"oo{j}", h, lambda bk, j=j: [
                        pe.matmul(bk[:, :], k8[0:NB, :], vbd[0:NB, j * 512:(j + 1) * 512], start=True, stop=True)])
                taken(G, "oo0", h)
                taken(G, "oo1", h)
                hand(G, "od", h, lambda bk: (
                    pe.matmul(bk[:, b:b + 1], sdv[:, b, :], qn[:, T + b:T + b + 1], start=True, stop=True)
                    for b in range(NB)))
                pe.wait_ge(sq_ready, KT + 3 * h + 3)
                hand(G, "nst", h, lambda bk: stats([sq2], NT, bk, 0, 1))
                pe.wait_ge(rn_ready, 2 * h + 3)
                for j, name in enumerate(("nb0", "nb1", "nb8")):
                    hand(G, name, h, lambda bk, j=j: across(
                        bk, lambda c: rn2[:, c:c + 1], range(4 * j, min(4 * j + 4, NC + 1))))

            body(0, True)
            with pe.Fori(1, GH_N - 1) as h:
                body(h, True)
            body(GH_N - 1, False)
            pe.wait_ge(oa_ready, GH_N)
            pe.drain().then_inc(phase_done, 1)
            pe.wait_ge(phase_done, 10)

            def up_a(j, first):
                project(2 * j, W_UPA, 0, 2 * 24, lambda u, n: (
                    (proj_taken, 3 * j + (A_UPA + n + 1)) if u else
                    (proj_taken, A_UPA) if first else (sum_taken, 3 * j + (n - 2))), [xnv, oav])

            up_a(0, True)
            with pe.Fori(1, KT) as j:
                up_a(j, False)
            pe.drain().then_inc(phase_done, 1)
            pe.wait_ge(phase_done, 15)

            G = ssm_plan

            def bcxz(g, m0, m1):
                project(6 * g, W_SSM, m0, m1, lambda u, n: (proj_taken, 18 * g + (A_SSM + 3 * u + n - 2)))

            bcxz(0, 0, 144)
            bT, cT, xT0, xT1 = sconv

            def body(g, more):
                def fill(step):
                    if more:
                        bcxz(g + 1, *sfills(step))

                pe.wait_ge(proj_taken, 18 * g + (A_SSM + 18))
                hand(G, "rw", g, lambda bk: (
                    pe.transpose(bk[0:11, u * P:(u + 1) * P], sraw[u][:, T:T + 11], ident[:, :]) for u in range(4)))
                fill("rw")
                pe.wait_ge(sx_ready, 4 * g + 4)
                for j in range(2):
                    hand(G, f"tb{j}", g, lambda bk, j=j: (
                        pe.transpose(cols(bk, i), cols(bT, 4 * j + i), ident[:, :]) for i in range(4)))
                fill("tb")
                for j in range(4):
                    hand(G, f"tx{j}", g, lambda bk, j=j: (
                        pe.transpose(cols(bk, i), cols(sconv[2 + i % 2], 2 * j + i // 2), ident[:, :])
                        for i in range(4)))
                hand(G, "t8", g, lambda bk: (
                    pe.transpose(bk[0:NB, i * P:(i + 1) * P], sconv[i][:, T:NT], ident[:, :]) for i in range(2)))
                fill("tx")
                for j in range(2):
                    hand(G, f"cb{j}", g, lambda bk, j=j: (
                        pe.matmul(cols(bk, i), cols(bT, 4 * j + i), cols(cT, 4 * j + i), start=True, stop=True)
                        for i in range(4)))
                fill("cb")
                taken(G, "tb1", g)
                taken(G, "tx3", g)
                pe.wait_ge(ml_ready, 4 * g + 4)
                pe.wait_ge(cd_ready, g + 1)
                for c in range(NC):
                    if c:
                        taken(G, f"su{c - 1}", g)
                    hand(G, f"su{c}", g, lambda bk, c=c: [
                        pe.matmul(bk[:, 0:2 * P], cols(btok, c), xdd[:, 2 * P * c:2 * P * (c + 1)],
                                  start=True, stop=True)])
                    name = f"y{c // 2}"
                    if c % 2 == 0:
                        wait(pe, bank_taken[G.bank(name)], G.before(name, g))
                    for r in range(HPG):
                        rows, col = slice(HD * (r % 2), HD * (r % 2 + 1)), (2 * (c % 2) + r // 2) * P
                        out = psum[rows, G.bank(name), col:col + P]
                        head = slice(r * HD, (r + 1) * HD)
                        mm = pe.matmul(out, xdt[:, 2 * P * c:2 * P * (c + 1)][:, head],
                                       cols(ml[:, r * T:(r + 1) * T], c), start=True, stop=(c == 0))
                        if c:
                            mm = pe.matmul(out, SST[c % 2][:, head], cols(csb[:, r * T:(r + 1) * T], c),
                                           start=False, stop=True)
                    if c % 2:
                        mm.then_inc(bank_full[G.bank(name)], 1)
                    fill(f"scan{c}")
                taken(G, "su7", g)
                hand(G, "fs", g, lambda bk: (
                    pe.transpose(bk[:, i * P:(i + 1) * P], cols(SST[0], i), ident[:, :]) for i in range(2)))
                fill("fs")
                for name, rhs in (("bb", bdg), ("cc", cdg)):
                    for j in range(2):
                        hand(G, f"{name}{j}", g, lambda bk, j=j, rhs=rhs: [
                            pe.matmul(bk[:, :], ones[0:NB, :], rhs[0:NB, j * 512:(j + 1) * 512],
                                      start=True, stop=True)])
                fill("decode")
                pe.wait_ge(sq_ready, 2 * g + (SQ_SSM + 2))
                hand(G, "nst", g, lambda bk: stats(ml_sq, NT, bk, 0, 2))
                pe.wait_ge(rn_ready, g + (RN_SSM + 1))
                for j, name in enumerate(("nb0", "nb1", "nb8")):
                    hand(G, name, g, lambda bk, j=j: across(
                        bk, lambda c: srn[:, c:c + 1], range(4 * j, min(4 * j + 4, NC + 1))))

            body(0, True)
            with pe.Fori(1, SG_N - 1) as g:
                body(g, True)
            body(SG_N - 1, False)
            pe.drain().then_inc(phase_done, 1)
            pe.wait_ge(phase_done, 20)

            pe.wait_ge(late_loaded, 48)

            def up_b(j, i, first):
                project(3 * j, W_UPB + 3 * i, 0, 3 * 24, lambda u, n: (
                    (proj_taken, 3 * j + (A_UPB + 3 * i + n + 1)) if u else
                    (proj_taken, A_UPB) if first else (sum_taken, 3 * j + (V_UPB + 3 * i + n - 2))),
                    [xnv, ybv[:, 0:KT, :], ybv[:, KT:2 * KT, :]], join=(2,))

            up_b(0, 0, True)
            up_b(0, 1, False)
            with pe.Fori(1, KT // 2) as pair:
                j = pair * 2
                up_b(j, 0, False)
                up_b(j, 1, False)
            pe.wait_ge(sum_taken, V_OUT)
            with pe.Fori(0, KT // 2) as pair:
                j = pair * 2
                project(j, W_OUT, 0, 48, lambda u, n: (sum_taken, 3 * j + (V_OUT + 3 * u + n - 2)), [mgv, mgv])
            pe.drain().then_inc(phase_done, 1)
            pe.wait_ge(phase_done, 25)

            G = mem_plan
            pe.wait_ge(mem_loaded, 16)
            for t in range(MT):
                for j in range(2):
                    hand(G, f"mt{t}{j}", 0, lambda bk, t=t, j=j: (
                        pe.transpose(cols(bk, i), memtok[:, t, (4 * j + i) * P:(4 * j + i + 1) * P], ident[:, :])
                        for i in range(4)))
            pe.wait_ge(sq_ready, SQ_X + KT)
            hand(G, "xst", 0, lambda bk: stats([xnv[:, k, :] for k in range(KT)], NT, bk))
            pe.wait_ge(sq_ready, SQ_X + KT + 1)
            hand(G, "mst", 0, lambda bk: (
                pe.matmul(bk[:, c:c + 1], memsqv[:, k, c * P:(c + 1) * P], ones[:, 0:1], start=(k == 0),
                          stop=(k == KT - 1)) for c in range(MT) for k in range(KT)))
            pe.wait_ge(rn_ready, RN_X + 1)
            hand(G, "mbc", 0, lambda bk: across(bk, lambda c: mrn[:, c:c + 1], range(MT)))
            taken(G, "mbc")

            def mem_rows(base, sem_, count):
                with pe.Fori(0, KT // 2) as pair:
                    j = pair * 2
                    for i in range(2):
                        pe.wait_ge(slab_loaded[(base + i) % 2], 8 * j + 16 * ((base + i) // 2 + 1))
                        pe.wait_ge(sem_, j + (count + i - 1))
                        for t in range(MT):
                            for k in range(KT):
                                mm = pe.matmul(psum[:, i, t * P:(t + 1) * P], mn[:, k, t * P:(t + 1) * P],
                                               slabv[(base + i) % 2][:, k, :], start=(k == 0), stop=(k == KT - 1))
                        mm.then_inc(proj_full, 3)

            mem_rows(W_MK, sum_taken, V_MK)
            pe.wait_ge(rn_ready, RN_X + 2)
            for j in range(3):
                hand(G, f"xb{j}", 0, lambda bk, j=j: across(
                    bk, lambda c: xrn[:, c:c + 1], range(4 * j, min(4 * j + 4, NC + 1))))
            pe.wait_ge(sum_taken, V_MK + KT)
            mem_rows(W_MV, proj_taken, A_MV)
            for q in range(4):
                hand(G, f"kt{q}", 0, lambda bk, q=q: (
                    pe.transpose(cols(bk, 2 * i + t), Ktok[:, t, (2 * q + i) * P:(2 * q + i + 1) * P], ident[:, :])
                    for i in range(2) for t in range(MT)))
            taken(G, "xb2")
            pe.wait_ge(proj_taken, A_CQ)
            with pe.Fori(0, KT // 2) as pair:
                j = pair * 2
                project(j, W_CQ, 0, 48, lambda u, n: (proj_taken, 3 * j + (A_CQ + 3 * u + n - 2)))
            pe.wait_ge(proj_taken, A_END)
            for j in range(2):
                hand(G, f"qt{j}", 0, lambda bk, j=j: (
                    pe.transpose(bk[0:NB, i * P:(i + 1) * P], qT[:, (4 * j + i) * NT + T:(4 * j + i + 1) * NT],
                                 ident[:, :]) for i in range(4)))
            G = attn_plan
            with pe.Fori(0, XH_N) as h:
                for s in range(2):
                    pe.wait_ge(q_ready, 2 * h + s + 1)
                    for i in range(2):
                        hand(G, f"sc{s}{i}", h, lambda bk, i=i, s=s: (
                            pe.matmul(bk[:, c * M_N:(c + 1) * M_N], qh[s][:, k, (2 * i + c) * P:(2 * i + c + 1) * P],
                                      KTm[:, bass.ds(h * 2 * M_N + k * M_N, M_N)], start=(k == 0), stop=(k == 1))
                            for c in range(2) for k in range(2)))
                    for i in range(2):
                        hand(G, f"qb{s}{i}", h, lambda bk, i=i, s=s: [
                            pe.matmul(bk, ones[0:NB, :], qm[s][0:NB, i * 512:(i + 1) * 512], start=True, stop=True)])
                for s in range(2):
                    pe.wait_ge(p_ready, 2 * h + s + 1)
                    for t in range(MT):
                        hand(G, f"pt{s}{t}", h, lambda bk, s=s, t=t: (
                            pe.transpose(cols(bk, c), pr[s][:, c, t * P:(t + 1) * P], ident[:, :]) for c in range(4)))
                    pe.wait_ge(s8_ready, 2 * h + s + 1)
                    hand(G, f"st{s}", h, lambda bk, s=s: (
                        pe.transpose(bk[0:XH_N, t * P:(t + 1) * P], s8[s][:, t, :], ident[:, :]) for t in range(MT)))
                    pe.wait_ge(vh_ready, h + 1)
                    taken(G, f"pt{s}0", h)
                    taken(G, f"pt{s}1", h)
                    for k in range(2):
                        hand(G, f"o{s}{k}", h, lambda bk, k=k: (
                            pe.matmul(bk, vh[:, t, k * P:(k + 1) * P], PT[:, t, :], start=(t == 0), stop=(t == MT - 1))
                            for t in range(MT)))
                    pe.wait_ge(p4_ready, 2 * h + s + 1)
                    hand(G, f"pb{s}", h, lambda bk, s=s: (
                        pe.matmul(bk[:, t * XH_N:(t + 1) * XH_N], e4[s][0:XH_N, t * P:(t + 1) * P],
                                  ident[0:XH_N, 0:XH_N], start=True, stop=True) for t in range(MT)))
                    taken(G, f"pb{s}", h)
                    pe.wait_ge(vc_loaded[s], 16 * h + 16)
                    hand(G, f"os{s}", h, lambda bk, s=s: (
                        pe.matmul(bk[:, k:k + 1], vc[s][:, t, k * P:(k + 1) * P],
                                  pT8[s][:, t * XH_N + k // 2:t * XH_N + k // 2 + 1], start=(t == 0), stop=(t == MT - 1))
                        for k in range(KT) for t in range(MT)))
            taken(G, "os1", XH_N - 1)
            with pe.Fori(0, KT // 2) as pair:
                j = pair * 2
                project(j, W_CO, 0, 48, lambda u, n: (sum_taken, 3 * j + (V_CO + 3 * u + n - 2)), [atv, atv])

            G = ff_plan
            pe.wait_ge(sq_ready, SQ_X + 2 * KT + 1)
            hand(G, "fst", 0, lambda bk: stats([xnv[:, k, :] for k in range(KT)], NT, bk))
            pe.wait_ge(rn_ready, RN_X + 3)
            for j in range(3):
                hand(G, f"fb{j}", 0, lambda bk, j=j: across(
                    bk, lambda c: xrn[:, c:c + 1], range(4 * j, min(4 * j + 4, NC + 1))))
            taken(G, "fb2")
            for half_ in range(2):
                base, v0 = W_FU + half_ * 2 * FH, V_FU + half_ * V_HALF
                with pe.Fori(0, FH // 2) as pair:
                    j = pair * 2
                    project(j, base, 0, 48, lambda u, n: (sum_taken, 3 * j + (v0 + 3 * u + n - 2)))
                pe.wait_ge(sum_taken, v0 + 3 * FH)
                with pe.Fori(0, KT) as j:
                    project(2 * j, base + FH, 0, 48, lambda u, n: (sum_taken, 3 * j + (v0 + 3 * FH + n - 2)),
                            [hfv[:, 0:KT, :], hfv[:, KT:2 * KT, :]], join=(1,))
            pe.wait_ge(sq_ready, SQ_X + 3 * KT + 1)
            hand(G, "zst", 0, lambda bk: stats([xnv[:, k, :] for k in range(KT)], NT, bk))
            for c in range(NC + 1):
                a, z = token_range(c)
                for j in range(2):
                    hand(G, f"y{c}_{j}", 0, lambda bk, j=j, a=a, z=z: (
                        pe.transpose(cols(bk, i), x1v[:, 4 * j + i, a:z], ident[:, :]) for i in range(4)))

        @block.scalar
        def _(act):
            lane = Lane(act, act_step)

            def got(plan, name, it=0):
                b = plan.bank(name)
                act.wait_ge(bank_full[b], plan.after(name, it))
                return psum[:, b, :]

            def move(plan, name, it, dst, src, func=ACT.Copy, **kw):
                act.activation(dst, src(got(plan, name, it)), func, **kw).then_inc(bank_taken[plan.bank(name)], 1)

            S0 = setup_plan
            for t in range(9):
                n = P if t < NC else NB
                for j in range(2):
                    move(S0, f"xt{t}_{j}", 0, xT[:, 4 * j:4 * j + 4, t * P:t * P + n],
                         lambda bk, n=n: bk.rearrange("p (k i) -> p k i", k=4)[:, :, 0:n])
            move(S0, "vt", 0, vt[:, :], lambda bk: bk[:, 0:VT_N])
            for q in range(4):
                move(S0, f"ct{q}", 0, ct[:, q * 14 * 29:(q + 1) * 14 * 29], lambda bk: bk[:, 0:14 * 29])
            act.wait_ge(bank_taken[S0.bank("ct3")], S0.after("ct3"))
            for k in range(KT):
                act.activation(xnv[:, k, :], xT[:, k, :], ACT.Square).then_inc(sq_ready, 1)
            act.wait_ge(consts_ready, 2)
            move(S0, "st", 0, stat, lambda bk: bk[:, 0:9], ACT.Sqrt, scale=1.0 / D, bias=eps[:, :])
            for n in range(3):
                move(S0, f"sc{n}", 0, raw72[0:72, n * GW:(n + 1) * GW], lambda bk: bk[0:72, 0:GW])
            act.wait_ge(bank_taken[S0.bank("sc2")], S0.after("sc2"))
            act.wait_ge(params_loaded, 16 * 20)
            act.activation(hb[0:40, 1:2], hb[0:40, 1:2], ACT.Exp).then_inc(act_to_dve, 1)
            act.activation(rows72[64:72, :], raw72[64:72, :], ACT.Exp, scale=-1.0).then_inc(act_to_dve, 1)
            act.wait_ge(dve_to_act, 1)
            act.activation(t_e[0:40, :], t_e[0:40, :], ACT.Exp).then_inc(act_to_dve, 1)
            act.wait_ge(dve_to_act, 2)
            act.activation(t_l[0:40, :], t_u[0:40, :], ACT.Ln).then_inc(act_to_dve, 1)
            for j in range(2):
                move(S0, f"ta{j}", 0, tok72[:, 4 * j:4 * j + 4, :],
                     lambda bk: bk[:, 0:288].rearrange("p (c h) -> p c h", c=4))
            move(S0, "td", 0, tokd, lambda bk: bk[:, 0:256].rearrange("p (c h) -> p c h", c=NC))
            move(S0, "cs", 0, cst, lambda bk: bk[:, 0:320].rearrange("p (c h) -> p c h", c=NC))
            for j in range(2):
                move(S0, f"csr{j}", 0, csr_full[0:40, j * 512:(j + 1) * 512], lambda bk: bk[0:40, :])
            act.wait_ge(bank_taken[S0.bank("csr1")], S0.after("csr1"))
            act.activation(egc, cst[:, :, 32:40], ACT.Exp).then_inc(rows_ready, 1)
            act.wait_ge(dve_to_act, 3)
            act.activation(tote, tote, ACT.Exp)
            act.activation(dout, dout, ACT.Exp).then_inc(tab_exp, 1)
            dtxv = dtx[:, :].rearrange("p (i c) -> p i c", c=17)
            move(S0, "dtx", 0, dtxv, lambda bk: bk[:, 0:SH_N // 2 * 17].rearrange("p (i c) -> p i c", c=17))
            act.wait_ge(bank_taken[S0.bank("dtx")], S0.after("dtx"))
            act.activation(dtxv[:, :, 8:16], dtxv[:, :, 8:16], ACT.Exp)
            act.wait_ge(params_loaded, 16 * 22)
            act.activation(gb8[:, :], gb8[:, :], ACT.Exp)
            act.drain().then_inc(phase_done, 1)
            act.wait_ge(phase_done, SETUP_ENDS)

            G = gdn_plan

            def evacuate(h, a, z):
                for g in range(a, z):
                    u, n = g // 3, g % 3
                    act.wait_ge(proj_full, 12 * h + g + 1)
                    if u < 3:
                        if n == 0:
                            wait(act, conv_done, 3 * (h - 1) + u + 1)
                        act.activation(raw[u][:, 3 + n * GW:3 + (n + 1) * GW], psum[:, n, 0:GW], ACT.Copy
                                       ).then_inc(proj_taken, 1)
                    else:
                        if n == 0:
                            wait(act, gate_ready, h)
                        act.activation(ggr[:, n * GW:(n + 1) * GW], psum[:, n, 0:GW], ACT.Copy, scale=0.5
                                       ).then_inc(proj_taken, 1)

            def tanh_conv(h, u):
                act.wait_ge(conv_done, 3 * h + u + 1)
                wait(act, tanh_used, 4 * h + u - 1)
                act.activation(tnh[u % 2], conv[u], ACT.Tanh).then_inc(tanh_ready, 1)

            def tanh_gate(h):
                act.wait_ge(proj_taken, 12 * h + 12)
                act.wait_ge(tanh_used, 4 * h + 2)
                act.activation(tnh[1], ggr, ACT.Tanh).then_inc(tanh_ready, 1)

            evacuate(0, 0, 12)
            for u in range(3):
                tanh_conv(0, u)

            def stores(h):
                act.wait_ge(bank_taken[G.bank("su7")], G.after("su7", h))
                act.dma_start(io["p_gdn"][0, 0, bass.ds(h, 1)].rearrange("o k e -> k (o e)"), Sst[0]
                              ).then_inc(S_stored, 16)
                act.wait_ge(bank_taken[G.bank("oo1")], G.after("oo1", h))
                act.dma_start(io["s_gdn"][0, :, bass.ds(h, 1)].rearrange("b o k e -> k (b o) e"),
                              sdec.rearrange("p (b e) -> p b e", b=NB)).then_inc(sdec_stored, 16)

            def body(h, first, more):
                def evac(step):
                    if more:
                        a, z = fills(step)
                        evacuate(h + 1, a // 8, z // 8)

                if not first:
                    stores(h - 1)
                wait(act, rw_stored, 32 * h)
                move(G, "rw", h, rwst[0:11, :], lambda bk: bk[0:11, 0:3 * P])
                act.wait_ge(bank_taken[G.bank("rw")], G.after("rw", h))
                pc = io["p_gdn_conv"][0, 0].rearrange("r (u x) -> r u x", u=3)[:, :, bass.ds(h * P, P)]
                sc = io["s_gdn_conv"][0, :, CW - 2, :].rearrange("b (u x) -> b u x", u=3)[:, :, bass.ds(h * P, P)]
                act.dma_start(pc, rwst[0:3, :].rearrange("r (u x) -> r u x", u=3)).then_inc(rw_stored, 16)
                act.dma_start(sc, rwst[3:11, :].rearrange("r (u x) -> r u x", u=3)).then_inc(rw_stored, 16)
                act.wait_ge(qkv_ready, 3 * h + 2)
                wait(act, oa_ready, h)
                act.activation(sq2, conv[0], ACT.Square).then_inc(sq_ready, 1)
                act.activation(oT, conv[1], ACT.Square).then_inc(sq_ready, 1)
                tanh_gate(h)
                evac("rw")
                move(G, "st", h, st2, lambda bk: bk[:, 0:18], ACT.Sqrt, bias=eps[:, :])
                act.wait_ge(dec_diff, h + 1)
                act.activation(dec1, dec1, ACT.Exp, scale=-1.0).then_inc(dec_exp, 1)
                act.activation(dec2, dec2, ACT.Exp).then_inc(dec_exp, 1)
                act.activation(gbr, gbr, ACT.Exp).then_inc(eg_ready, 1)
                evac("norm")
                evac("turn")
                evac("kkqk")
                for L in range(1, 7):
                    for j in range(2):
                        move(G, f"p{L}_{j}", h, half(Pp, j), lambda bk: bk.rearrange("p (c i) -> p c i", c=4))
                    evac(f"level{L}")
                for j in range(2):
                    bk = got(G, f"w{j}", h)
                    act.mul(half(wtn, j), bk.rearrange("p (c i) -> p c i", c=4), -1.0
                            ).then_inc(bank_taken[G.bank(f"w{j}")], 1)
                for c in range(NC):
                    move(G, f"vn{c}", h, vnew[c % 2], lambda bk: bk[:, 0:P])
                    if c % 4 == 3:
                        move(G, f"ot{c // 4}", h, oT[:, (c - 3) * P:(c + 1) * P], lambda bk: bk[:, :])
                    evac(f"scan{c}")
                    if more and c in (1, 4, 7):
                        tanh_conv(h + 1, c // 3)
                evac("decode")
                move(G, "od", h, oT[:, T:NT], lambda bk: bk[:, 0:NB])
                act.wait_ge(bank_taken[G.bank("od")], G.after("od", h))
                act.activation(sq2, oT, ACT.Square).then_inc(sq_ready, 1)
                move(G, "nst", h, st2[:, 0:9], lambda bk: bk[:, 0:9], ACT.Sqrt, scale=1.0 / P, bias=eps[:, :])

            body(0, True, True)
            with act.Fori(1, GH_N - 1) as h:
                body(h, False, True)
            body(GH_N - 1, False, False)
            stores(GH_N - 1)
            act.wait_ge(S_stored, 16 * GH_N)
            act.wait_ge(sdec_stored, 16 * GH_N)
            act.wait_ge(rw_stored, 32 * GH_N)
            act.drain().then_inc(phase_done, 1)
            act.wait_ge(phase_done, 10)

            def merge_gate(it, slab0, taken0, j, tg, free):
                wait(act, *free)
                for n in range(3):
                    act.wait_ge(proj_full, it[0] + (3 * slab0 + n + 1))
                    act.activation(tg[:, n * GW:(n + 1) * GW], psum[:, n, 0:GW], ACT.Tanh, scale=0.5
                                   ).then_inc(proj_taken, 1)

            for j0 in range(2):
                merge_gate((6 * j0,), W_UPA, 0, j0, tgate[j0], (mg_ready, 0))
            with act.Fori(1, KT // 2) as pair:
                j = pair * 2
                for i in range(2):
                    merge_gate((6 * j,), W_UPA + 2 * i, 0, j, tgate[i], (mg_ready, j + (i - 1)))
            act.drain().then_inc(phase_done, 1)
            act.wait_ge(phase_done, 15)

            G = ssm_plan

            def evacuate(g, a, z):
                for m in range(a, z):
                    u, n = m // 3, m % 3
                    act.wait_ge(proj_full, 18 * g + (3 * W_SSM + m + 1))
                    if n == 0 and u < 4:
                        wait(act, sconv_done, 4 * (g - 1) + u + 1)
                    elif n == 0:
                        wait(act, z_ready, 2 * (g - 1) + (u - 4) + 1)
                    if u < 4:
                        act.activation(sraw[u][:, 3 + n * GW:3 + (n + 1) * GW], psum[:, n, 0:GW], ACT.Copy
                                       ).then_inc(proj_taken, 1)
                    else:
                        act.activation(zraw[u - 4][:, n * GW:(n + 1) * GW], psum[:, n, 0:GW], ACT.Copy, scale=0.5
                                       ).then_inc(proj_taken, 1)

            def stanh(g, u):
                if u < 4:
                    act.wait_ge(sconv_done, 4 * g + u + 1)
                else:
                    act.wait_ge(proj_taken, 18 * g + (A_SSM + 3 * u + 3))
                wait(act, stanh_used, 6 * g + u - 1)
                act.activation(stnh[u % 2], sconv[u] if u < 4 else zraw[u - 4], ACT.Tanh).then_inc(stanh_ready, 1)

            evacuate(0, 0, 18)
            for u in range(4):
                stanh(0, u)
            s_out = io["s_ssm"][0].rearrange("b (i r) p n -> (r p) i b n", r=2)
            p_out = io["p_ssm"][0, 0].rearrange("(i r) p n -> (r p) i n", r=2)

            def stores(g):
                act.wait_ge(y_ready, 2 * g + 2)
                for q in range(2):
                    act.dma_start(s_out[:, bass.ds(2 * g + q, 1)].rearrange("p o b n -> p (o b) n"),
                                  ssd[:, q * NB * P:(q + 1) * NB * P].rearrange("p (b n) -> p b n", b=NB)
                                  ).then_inc(ssd_stored, 16)
                act.wait_ge(yb_ready, g + 1)
                for q in range(2):
                    act.dma_start(d_yb[bass.ds(2 * g + q, 1)].rearrange("o p t -> p (o t)"), yT[q]
                                  ).then_inc(yb_stored, 16)

            def body(g, first, more):
                def evac(step):
                    if more:
                        a, z = sfills(step)
                        evacuate(g + 1, a // 8, z // 8)

                if not first:
                    stores(g - 1)
                wait(act, srw_stored, 96 * g)
                move(G, "rw", g, srw[0:11, :], lambda bk: bk[0:11, :])
                act.wait_ge(bank_taken[G.bank("rw")], G.after("rw", g))
                pc, sc = io["p_ssm_conv"][0, 0], io["s_ssm_conv"][0, :, CW - 2, :]
                for a, n, col in ((0, P, SDI), (P, P, SDI + SG_N * P), (2 * P, 2 * P, 0)):
                    dst = bass.ds(g * n + col, n)
                    act.dma_start(pc[:, dst], srw[0:3, a:a + n]).then_inc(srw_stored, 16)
                    act.dma_start(sc[:, dst], srw[3:11, a:a + n]).then_inc(srw_stored, 16)
                for u in (4, 5):
                    stanh(g, u)
                evac("rw")
                for j in range(2):
                    move(G, f"tb{j}", g, half(btok, j), lambda bk: bk.rearrange("p (c i) -> p c i", c=4))
                evac("tb")
                for r in range(HPG):
                    act.wait_ge(sdiff, 4 * g + r + 1)
                    act.activation(ml[:, r * T:(r + 1) * T], ml[:, r * T:(r + 1) * T], ACT.Exp).then_inc(sdec_exp, 1)
                    act.activation(csb[:, r * T:(r + 1) * T], csb[:, r * T:(r + 1) * T], ACT.Exp
                                   ).then_inc(ecs_ready, 1)
                evac("tx")
                evac("cb")
                for c in range(NC):
                    evac(f"scan{c}")
                    if more and c in (1, 3, 5, 7):
                        stanh(g + 1, c // 2)
                wait(act, stf_stored, 32 * g)
                move(G, "fs", g, stf, lambda bk: bk[:, 0:2 * P])
                act.wait_ge(bank_taken[G.bank("fs")], G.after("fs", g))
                for q in range(2):
                    act.dma_start(p_out[:, bass.ds(2 * g + q, 1)].rearrange("p o n -> p (o n)"), cols(stf, q)
                                  ).then_inc(stf_stored, 16)
                evac("fs")
                evac("decode")
                for q in range(2):
                    act.wait_ge(y_ready, 2 * g + q + 1)
                    act.activation(ml_sq[q], yT[q], ACT.Square).then_inc(sq_ready, 1)
                move(G, "nst", g, ssq, lambda bk: bk[:, 0:9], ACT.Sqrt, scale=1.0 / (2 * P), bias=eps[:, :])

            body(0, True, True)
            with act.Fori(1, SG_N - 1) as g:
                body(g, False, True)
            body(SG_N - 1, False, False)
            stores(SG_N - 1)
            for s_ in (ssd_stored, stf_stored, yb_stored):
                act.wait_ge(s_, 32 * SG_N)
            act.wait_ge(srw_stored, 96 * SG_N)
            act.drain().then_inc(phase_done, 1)
            act.wait_ge(phase_done, 20)

            for i in range(2):
                merge_gate((0,), W_UPB + 3 * i, 0, 0, tgate2[i], (mg_ready, 0))
            with act.Fori(1, KT // 2) as pair:
                j = pair * 2
                for i in range(2):
                    merge_gate((9 * j,), W_UPB + 3 * i, 0, j, tgate2[i], (sum_taken, 3 * j + (V_UPB + 3 * (i - 1))))
            for k in range(KT):
                act.wait_ge(sum_taken, V_OUT + 3 * (k + 1))
                act.activation(xnv[:, k, :], x1v[:, k, :], ACT.Square).then_inc(sq_ready, 1)
            act.drain().then_inc(phase_done, 1)
            act.wait_ge(phase_done, 25)

            G = mem_plan
            for t in range(MT):
                for j in range(2):
                    move(G, f"mt{t}{j}", 0, memTv[:, 4 * j:4 * j + 4, t * P:(t + 1) * P],
                         lambda bk: bk.rearrange("p (k i) -> p k i", k=4))
            for name in ("mt00", "mt01", "mt10", "mt11"):
                act.wait_ge(bank_taken[G.bank(name)], G.after(name))
            act.activation(memsq, memT, ACT.Square).then_inc(sq_ready, 1)
            move(G, "xst", 0, xstat, lambda bk: bk[:, 0:9], ACT.Sqrt, scale=1.0 / D, bias=eps[:, :])
            move(G, "mst", 0, mstat, lambda bk: bk[:, 0:MT], ACT.Sqrt, scale=1.0 / D, bias=eps[:, :])
            act.wait_ge(bank_taken[G.bank("mbc")], G.after("mbc"))
            for b in range(2):
                act.dma_start(kc[b], io["cache_mem_k"][0, b].rearrange("(t p) h d -> p t (h d)", p=P)
                              ).then_inc(kc_loaded[b], 16)
                act.dma_start(vc[b], io["cache_mem_v"][0, b].rearrange("(t p) h d -> p t (h d)", p=P)
                              ).then_inc(vc_loaded[b], 16)
            with act.Fori(0, KT // 2) as pair:
                j = pair * 2
                for i in range(2):
                    act.wait_ge(proj_full, 3 * j + 3 * (W_MV + i + 1))
                    act.activation(Vtok[:, :, bass.ds(j * P + i * P, P)],
                                   psum[:, i, 0:MT * P].rearrange("p (t c) -> p t c", t=MT), ACT.Copy
                                   ).then_inc(proj_taken, 1)
            for q in range(4):
                move(G, f"kt{q}", 0, KTm[:, q * 512:(q + 1) * 512], lambda bk: bk)
            with act.Fori(0, KT // 2) as pair:
                j = pair * 2
                for i in range(2):
                    for n in range(3):
                        act.wait_ge(proj_full, 3 * j + (3 * (W_CQ + i) + n + 1))
                        act.activation(qT[:, bass.ds(j * NT + (i * NT + n * GW), GW)], psum[:, n, 0:GW], ACT.Copy
                                       ).then_inc(proj_taken, 1)
            for j in range(2):
                move(G, f"qt{j}", 0, qtok[0:NB, j * 512:(j + 1) * 512], lambda bk: bk[0:NB, :])
            G = attn_plan
            act.wait_ge(mem_stored, 16)
            with act.Fori(0, XH_N) as h:
                for s in range(2):
                    act.wait_ge(mx_ready, 2 * h + s + 1)
                    for i in range(2):
                        bk = got(G, f"sc{s}{i}", h)
                        for c in range(2):
                            ins = act.activation(pr[s][:, 2 * i + c, :], bk[:, c * M_N:(c + 1) * M_N], ACT.Exp,
                                                 scale=x_scale, bias=nmx[s][:, 2 * i + c:2 * i + c + 1],
                                                 accum_out=psm[s][:, 2 * i + c:2 * i + c + 1])
                        ins.then_inc(bank_taken[G.bank(f"sc{s}{i}")], 1)
                    for i in range(2):
                        move(G, f"qb{s}{i}", h, qrep[s][:, i * 512:(i + 1) * 512], lambda bk: bk)
                for s in range(2):
                    for t in range(MT):
                        move(G, f"pt{s}{t}", h, PT[:, t, :], lambda bk: bk)
                    act.wait_ge(m4_ready, 2 * h + s + 1)
                    move(G, f"st{s}", h, e4[s][0:XH_N, :], lambda bk: bk[0:XH_N, 0:M_N], ACT.Exp,
                         scale=x_scale, bias=mx4[s][0:XH_N, :], accum_out=sm4[s][0:XH_N, :])
                    for k in range(2):
                        move(G, f"o{s}{k}", h, at[:, bass.ds(h * 2 * NT + (k * NT + s * 512), 512)], lambda bk: bk)
                    move(G, f"pb{s}", h, pT8[s], lambda bk: bk[:, 0:MT * XH_N])

            G = ff_plan
            for k in range(KT):
                act.wait_ge(sum_taken, V_CO + 3 * (k + 1))
                act.activation(xnv[:, k, :], x1v[:, k, :], ACT.Square).then_inc(sq_ready, 1)
            move(G, "fst", 0, xstat, lambda bk: bk[:, 0:9], ACT.Sqrt, scale=1.0 / D, bias=eps[:, :])
            for half_ in range(2):
                with act.Fori(0, FH) as j:
                    for n in range(3):
                        act.wait_ge(proj_full, 3 * j + (3 * (W_FU + half_ * 2 * FH) + n + 1))
                        act.activation(hf[:, bass.ds(j * NT + n * GW, GW)], psum[:, n, 0:GW], ACT.Relu
                                       ).then_inc(proj_taken, 1)
            for k in range(KT):
                act.wait_ge(sum_taken, V_FU + V_HALF + 3 * FH + 3 * (k + 1))
                act.activation(xnv[:, k, :], x1v[:, k, :], ACT.Square).then_inc(sq_ready, 1)
            move(G, "zst", 0, xstat, lambda bk: bk[:, 0:9], ACT.Sqrt, scale=1.0 / D, bias=eps[:, :])

        @block.vector
        def _(dve):
            lane = Lane(dve, dve_step)

            def got(plan, name, it=0):
                b = plan.bank(name)
                dve.wait_ge(bank_full[b], plan.after(name, it))
                return psum[:, b, :]

            def give(plan, name, ins):
                ins.then_inc(bank_taken[plan.bank(name)], 1)

            def taken(plan, name, it=0):
                dve.wait_ge(bank_taken[plan.bank(name)], plan.after(name, it))

            def do(ins):
                lane.step(ins)
                lane.settle()

            S0 = setup_plan
            taken(S0, "ct3")
            taken(S0, "ct2")
            taken(S0, "ct1")
            taken(S0, "ct0")
            taken(S0, "vt")
            do(dve.tensor_scalar(ctv[:, :, 24:29], ctv[:, :, 24:29], 0.5, None, ALU.mult))
            taken(S0, "st")
            dve.reciprocal(rnorm, stat).then_inc(rn_ready, 1)
            for j in range(3):
                bk = got(S0, f"bc{j}")
                a, z = j * 512, min((j + 1) * 512, NT)
                for k in range(KT):
                    ins = dve.scalar_tensor_tensor(out=xnv[:, k, a:z], in0=xT[:, k, a:z],
                                                   scalar=vt[:, v_mix + k:v_mix + k + 1],
                                                   in1=bk[:, 0:z - a], op0=ALU.mult, op1=ALU.mult)
                give(S0, f"bc{j}", ins)
            do(dve.memset(rows72[0:64, :], 0.0))
            taken(S0, "sc2")
            taken(S0, "sc1")
            taken(S0, "sc0")
            do(dve.tensor_scalar(t_c[0:40, :], raw72[0:40, :], hb[0:40, 0:1], None, ALU.add))
            dve.scalar_tensor_tensor(out=t_e[0:40, :], in0=t_c[0:40, :], scalar=-1.0, in1=t_c[0:40, :],
                                     op0=ALU.mult, op1=ALU.min).then_inc(dve_to_act, 1)
            dve.wait_ge(act_to_dve, 3)
            dve.tensor_scalar(t_u[0:40, :], t_e[0:40, :], 1.0, None, ALU.add).then_inc(dve_to_act, 1)
            dve.wait_ge(dve_to_act, 2)
            do(dve.scalar_tensor_tensor(out=t_e[0:40, :], in0=t_u[0:40, :], scalar=1.0, in1=t_e[0:40, :],
                                        op0=ALU.subtract, op1=ALU.subtract))
            do(dve.reciprocal(sp_t[0:40, :], t_u[0:40, :]))
            do(dve.tensor_tensor(t_e[0:40, :], t_e[0:40, :], sp_t[0:40, :], ALU.mult))
            dve.wait_ge(act_to_dve, 4)
            do(dve.scalar_tensor_tensor(out=sp_t[0:40, :], in0=t_c[0:40, :], scalar=0.0, in1=t_l[0:40, :],
                                        op0=ALU.max, op1=ALU.add))
            do(dve.tensor_tensor(sp_t[0:40, :], sp_t[0:40, :], t_e[0:40, :], ALU.subtract))
            do(dve.tensor_scalar(hb[0:40, 1:2], hb[0:40, 1:2], -1.0, None, ALU.mult))
            do(dve.tensor_scalar(rows72[0:40, :], sp_t[0:40, :], hb[0:40, 1:2], None, ALU.mult))
            do(dve.tensor_scalar(rows72[64:72, :], rows72[64:72, :], 1.0, None, ALU.add))
            dve.reciprocal(rows72[64:72, :], rows72[64:72, :]).then_inc(raw72_done, 1)
            do(dve.tensor_copy(rx[0:32, 0:8], sp_t[0:32, T:NT]))
            dve.tensor_copy(rx[0:32, 8:16], rows72[0:32, T:NT]).then_inc(rx_ready, 1)
            taken(S0, "cs")
            bk = got(S0, "tot")
            do(dve.tensor_copy(tote, bk[:, 0:320].rearrange("p (c h) -> p c h", c=NC)))
            give(S0, "tot", dve.tensor_tensor(dout, bk[:, 0:320].rearrange("p (c h) -> p c h", c=NC), cst,
                                              ALU.subtract))
            taken(S0, "tot")
            do(dve.memset(raw72[0:1, 0:1], 0.0))
            dve.sem_inc(dve_to_act, 1)
            dve.wait_ge(tab_exp, 1)
            ghv = gh[:, :].rearrange("p (h r c) -> p h r c", h=GH_N, r=5)

            def by_head(t, a, z):
                return t[:, :, a:z].rearrange("p c h -> p h c")

            do(dve.tensor_copy(ghv[:, :, 0, :], by_head(cst, 32, 40)))
            do(dve.tensor_copy(ghv[:, :, 1, :], by_head(tok72, 64, 72)))
            do(dve.tensor_tensor(ghv[:, :, 2, :], by_head(tok72, 64, 72), by_head(egc, 0, GH_N), ALU.mult))
            do(dve.tensor_copy(ghv[:, :, 3, :], by_head(dout, 32, 40)))
            do(dve.tensor_copy(ghv[:, :, 4, :], by_head(tote, 32, 40)))
            shv = sh[:, :].rearrange("p (g q c r) -> p g q c r", g=SG_N, q=4, c=NC)
            for g in range(SG_N):
                hr = slice(HPG * g, HPG * (g + 1))
                do(dve.tensor_copy(shv[:, g, 0], cst[:, :, hr]))
                do(dve.tensor_copy(shv[:, g, 1], tokd[:, :, hr]))
                do(dve.tensor_tensor(shv[:, g, 2], tokd[:, :, hr], dout[:, :, hr], ALU.mult))
                do(dve.tensor_copy(shv[:, g, 3], tote[:, :, hr]))
            dve.drain().then_inc(phase_done, 1)
            dve.wait_ge(phase_done, SETUP_ENDS)

            G = gdn_plan
            for u in range(3):
                do(dve.memset(raw[u][:, 0:3], 0.0))
            ctg = ctv[:, 0:GT_N, :].rearrange("p (u h) r -> p u h r", u=3)

            def conv_columns(h):
                wait(dve, conv_done, 3 * h)
                dve.tensor_copy(cwf.unsqueeze(2), ctg[:, :, bass.ds(h, 1), :]).then_inc(cw_ready, 1)

            conv_columns(0)

            def body(h, more):
                lane.restart()
                wait(dve, sd_ready, h)
                do(dve.tensor_copy(hs, gh[:, bass.ds(h * 5 * NC, 5 * NC)]))
                do(dve.tensor_copy(hs8[:, 0:NB], gb8[:, bass.ds(h * NB, NB)]))
                dve.tensor_copy(hs8[:, NB:2 * NB], bb8[:, bass.ds(h * NB, NB)]).then_inc(hs_ready, 1)
                if more:
                    conv_columns(h + 1)
                gc, beta, bege, dko, dch = (hs[:, i * NC:(i + 1) * NC] for i in range(5))
                dve.wait_ge(gbr_loaded, 16 * h + 16)
                for c in range(NC):
                    dve.tensor_scalar(cols(dec1, c), cols(gbr, c), gc[:, c:c + 1], 0.0, ALU.subtract, ALU.max)
                    ins = dve.tensor_scalar(cols(dec2, c), cols(gbr, c), gc[:, c:c + 1], 0.0, ALU.subtract, ALU.min)
                ins.then_inc(dec_diff, 1)
                taken(G, "st", h)
                dve.reciprocal(rn2, st2).then_inc(rn_ready, 1)
                for t, src, dst, f in (("q", conv[0], qn, float(P) ** -0.5), ("k", conv[1], kn, 1.0)):
                    for j in range(2):
                        bk = got(G, f"b{t}{j}", h)
                        give(G, f"b{t}{j}", dve.scalar_tensor_tensor(
                            out=dst[:, j * 512:(j + 1) * 512], in0=src[:, j * 512:(j + 1) * 512], scalar=f,
                            in1=bk[:, :], op0=ALU.mult, op1=ALU.mult))
                bk = got(G, "b8", h)
                dve.scalar_tensor_tensor(out=qn[:, T:NT], in0=conv[0][:, T:NT], scalar=float(P) ** -0.5,
                                         in1=bk[:, 0:NB], op0=ALU.mult, op1=ALU.mult)
                give(G, "b8", dve.tensor_tensor(kn[:, T:NT], conv[1][:, T:NT], bk[:, NB:2 * NB], ALU.mult))
                dve.wait_ge(qkv_ready, 3 * h + 3)
                dve.tensor_copy(vs8, conv[2][:, T:NT])
                for j in range(2):
                    bk = got(G, f"tv{j}", h).rearrange("p (c i) -> p c i", c=4)
                    give(G, f"tv{j}", dve.tensor_tensor(half(vb, j), bk, spread(beta[:, 4 * j:4 * j + 4]), ALU.mult))
                for j in range(2):
                    bk = got(G, f"tk{j}", h).rearrange("p (c i) -> p c i", c=4)
                    dve.tensor_tensor(half(kbe, j), bk, spread(bege[:, 4 * j:4 * j + 4]), ALU.mult)
                    give(G, f"tk{j}", dve.tensor_tensor(half(kd, j), bk, spread(dko[:, 4 * j:4 * j + 4]), ALU.mult))
                give(G, "t8", dve.tensor_copy(k8[0:NB, :], got(G, "t8", h)[0:NB, 0:P]))
                dve.wait_ge(dec_masked, 2 * h + 2)
                for j in range(2):
                    bk = got(G, f"kk{j}", h)
                    for i in range(4):
                        c = 4 * j + i
                        ins = dve.scalar_tensor_tensor(out=cols(amat, c), in0=cols(bk, i), scalar=beta[:, c:c + 1],
                                                       in1=cols(dec1, c), op0=ALU.mult, op1=ALU.mult)
                    give(G, f"kk{j}", ins)
                for j in range(2):
                    bk = got(G, f"qk{j}", h).rearrange("p (c i) -> p c i", c=4)
                    give(G, f"qk{j}", dve.tensor_tensor(half(dec2, j), bk, half(dec2, j), ALU.mult))
                dve.wait_ge(eg_ready, h + 1)
                taken(G, "b8", h)
                dve.tensor_tensor(qg, qn[:, 0:T], gbr, ALU.mult).then_inc(qg_ready, 1)
                dve.wait_ge(am_ready, 7 * h + 1)
                for j in range(2):
                    dve.tensor_tensor(half(X, j), per_chunk(ident[:, :], 4), half(aml[0], j), ALU.subtract)
                for j in range(2):
                    bk = got(G, f"y{j}", h).rearrange("p (c i) -> p c i", c=4)
                    give(G, f"y{j}", dve.tensor_tensor(half(Y, j), per_chunk(ident[:, :], 4), bk, ALU.subtract))
                for L in range(1, 7):
                    for j in range(2):
                        bk = got(G, f"yp{L}_{j}", h).rearrange("p (c i) -> p c i", c=4)
                        give(G, f"yp{L}_{j}", dve.tensor_tensor(half(Y, j), half(Y, j), bk, ALU.subtract))
                        if L < 6:
                            bk = got(G, f"xp{L}_{j}", h).rearrange("p (c i) -> p c i", c=4)
                            give(G, f"xp{L}_{j}", dve.tensor_tensor(half(X, j), half(X, j), bk, ALU.subtract))
                for c in range(NC):
                    bk = got(G, f"su{c}", h)
                    new = Sst[(c + 1) % 2]
                    if c == 0:
                        ins = dve.tensor_copy(new, bk[:, 0:P])
                    else:
                        if c == 1:
                            wait(dve, S_stored, 16 * h)
                        taken(G, f"su{c - 1}", h)
                        ins = dve.scalar_tensor_tensor(out=new, in0=Sst[c % 2], scalar=dch[:, c:c + 1],
                                                       in1=bk[:, 0:P], op0=ALU.mult, op1=ALU.add)
                    give(G, f"su{c}", ins)
                bk = got(G, "ks", h)
                do(dve.tensor_tensor(v8n, vs8, bk[:, 0:NB], ALU.subtract))
                give(G, "ks", dve.tensor_tensor(v8n, v8n, hs8[:, NB:2 * NB], ALU.mult))
                bk = got(G, "v8", h)
                give(G, "v8", dve.tensor_tensor(
                    vbd[0:NB, :].rearrange("p (b e) -> p b e", b=NB), per_chunk(bk[0:NB, 0:P], NB),
                    bd8[:, :].rearrange("p (b e) -> p b e", b=NB), ALU.mult))
                for j in range(2):
                    bk = got(G, f"oo{j}", h)
                    part = sdec[:, j * 512:(j + 1) * 512]
                    give(G, f"oo{j}", dve.tensor_tensor(part, part, bk[:, :], ALU.add))
                taken(G, "nst", h)
                dve.reciprocal(rn2[:, 0:9], st2[:, 0:9]).then_inc(rn_ready, 1)
                for j, name in enumerate(("nb0", "nb1", "nb8")):
                    bk = got(G, name, h)
                    a, z = j * 512, min((j + 1) * 512, NT)
                    give(G, name, dve.scalar_tensor_tensor(
                        out=oT[:, a:z], in0=oT[:, a:z], scalar=vt[:, v_gdn:v_gdn + 1], in1=bk[:, 0:z - a],
                        op0=ALU.mult, op1=ALU.mult))
                dve.wait_ge(gate_ready, h + 1)
                for name in ("nb0", "nb1", "nb8"):
                    taken(G, name, h)
                dve.tensor_tensor(oa[:, bass.ds(h * NT, NT)], oT, ggs, ALU.mult).then_inc(oa_ready, 1)

            body(0, True)
            with dve.Fori(1, GH_N - 1) as h:
                body(h, True)
            body(GH_N - 1, False)
            dve.drain().then_inc(phase_done, 1)
            dve.wait_ge(phase_done, 10)

            def gated(j, i, first):
                if not first:
                    dve.wait_ge(mg_stored[i], 8 * j)
                for n in range(3):
                    dve.wait_ge(proj_full, 6 * j + (3 * (W_UPA + 2 * i + 1) + n + 1))
                    dve.wait_ge(proj_taken, 3 * j + (A_UPA + 3 * i + n + 1))
                    c = slice(n * GW, (n + 1) * GW)
                    dve.scalar_tensor_tensor(out=mgst[i][:, c], in0=tgate[i][:, c], scalar=1.0, in1=psum[:, n, 0:GW],
                                             op0=ALU.add, op1=ALU.mult).then_inc(sum_taken, 1)
                dve.wait_ge(sum_taken, 3 * j + (3 * i + 3))
                dve.sem_inc(mg_ready, 1)

            gated(0, 0, True)
            gated(0, 1, True)
            with dve.Fori(1, KT // 2) as pair:
                j = pair * 2
                gated(j, 0, False)
                gated(j, 1, False)
            dve.drain().then_inc(phase_done, 1)
            dve.wait_ge(phase_done, 15)

            G = ssm_plan
            for u in range(4):
                do(dve.memset(sraw[u][:, 0:3], 0.0))

            def conv_columns(g):
                wait(dve, sconv_done, 4 * g)
                nx = SDI // P
                dve.tensor_copy(scw[:, 0:1, :], ctv[:, bass.ds(g + (GT_N + nx), 1), :])
                dve.tensor_copy(scw[:, 1:2, :], ctv[:, bass.ds(g + (GT_N + nx + SG_N), 1), :])
                dve.tensor_copy(scw[:, 2:4, :], ctv[:, bass.ds(2 * g + GT_N, 2), :]).then_inc(scw_ready, 1)

            conv_columns(0)

            def body(g, more):
                lane.restart()
                wait(dve, ssd_ready, g)
                do(dve.tensor_copy(shs, sh[:, bass.ds(g * 4 * NC * HPG, 4 * NC * HPG)]))
                do(dve.tensor_copy(snw, vt[:, bass.ds(2 * g + v_ssm, 2)]))
                dve.tensor_copy(shx, dtx[:, bass.ds(g * 34, 34)]).then_inc(shx_ready, 1)
                if more:
                    conv_columns(g + 1)
                cs, dt, dtd, dch = (shs[:, i * NC * HPG:(i + 1) * NC * HPG].rearrange("p (c r) -> p c r", c=NC)
                                    for i in range(4))
                for j in range(4):
                    bk = got(G, f"tx{j}", g).rearrange("p (c r e) -> p c r e", c=2, r=HPG)
                    for t, dst in ((dt, xdt), (dtd, xdd)):
                        ins = dve.tensor_tensor(
                            dst[:, 512 * j:512 * (j + 1)].rearrange("p (c r e) -> p c r e", c=2, r=HPG), bk,
                            t[:, 2 * j:2 * j + 2, :].unsqueeze(3).broadcast_to([P, 2, HPG, HD]), ALU.mult)
                    give(G, f"tx{j}", ins)
                bk = got(G, "t8", g)
                for i, dst in enumerate((bdg, cdg)):
                    ins = dve.tensor_tensor(dst[0:NB, :].rearrange("p (b e) -> p b e", b=NB),
                                            per_chunk(bk[0:NB, i * P:(i + 1) * P], NB),
                                            bd8[:, :].rearrange("p (b e) -> p b e", b=NB), ALU.mult)
                give(G, "t8", ins)
                dve.wait_ge(csb_loaded, 64 * g + 64)
                for r in range(HPG):
                    for c in range(NC):
                        ins = dve.tensor_scalar(cols(ml[:, r * T:(r + 1) * T], c), cols(csb[:, r * T:(r + 1) * T], c),
                                                cs[:, c, r:r + 1], 0.0, ALU.subtract, ALU.min)
                    ins.then_inc(sdiff, 1)
                for j in range(2):
                    bk = got(G, f"cb{j}", g).rearrange("p (c i) -> p c i", c=4)
                    give(G, f"cb{j}", dve.tensor_tensor(half(cbm, j), bk, per_chunk(triu[:, :], 4), ALU.mult))
                taken(G, "cb0", g)
                taken(G, "cb1", g)
                for r in range(HPG):
                    m, e = ml[:, r * T:(r + 1) * T], csb[:, r * T:(r + 1) * T]
                    dve.wait_ge(sdec_exp, 4 * g + r + 1)
                    dve.tensor_tensor(m, m, cbm, ALU.mult).then_inc(ml_ready, 1)
                    dve.wait_ge(ecs_ready, 4 * g + r + 1)
                    ins = dve.tensor_tensor(e, e, sconv[1][:, 0:T], ALU.mult)
                ins.then_inc(cd_ready, 1)
                wait(dve, yb_stored, 32 * g)
                for q in range(2):
                    dve.tensor_scalar(yT[q], sconv[2 + q], shx[:, 17 * q + 16:17 * q + 17], None, ALU.mult)
                    ins = dve.tensor_tensor(xdts[:, q * NB:(q + 1) * NB], sconv[2 + q][:, T:NT],
                                            shx[:, 17 * q:17 * q + NB], ALU.mult)
                ins.then_inc(x_used, 1)
                dve.wait_ge(x_used, g + 1)
                for c in range(NC):
                    bk = got(G, f"su{c}", g)
                    new = SST[(c + 1) % 2]
                    if c == 0:
                        ins = dve.tensor_copy(new, bk[:, 0:2 * P])
                    else:
                        taken(G, f"su{c - 1}", g)
                        do(dve.tensor_tensor(new.rearrange("p (r e) -> p r e", r=HPG),
                                             SST[c % 2].rearrange("p (r e) -> p r e", r=HPG),
                                             spread(dch[:, c, :], HD), ALU.mult))
                        ins = dve.tensor_tensor(new, new, bk[:, 0:2 * P], ALU.add)
                    give(G, f"su{c}", ins)
                    if c % 2:
                        name = f"y{c // 2}"
                        bk = got(G, name, g)
                        for i in range(4):
                            q, cc = i % 2, c - 1 + i // 2
                            ins = dve.tensor_tensor(cols(yT[q], cc), cols(yT[q], cc), cols(bk, i), ALU.add)
                        give(G, name, ins)
                dve.wait_ge(ssd_ready, g + 1)
                def last_read(name, q, ins):
                    if q == 0:
                        do(ins)
                    else:
                        give(G, name, ins)
                        taken(G, name, g)

                for j in range(2):
                    bk = got(G, f"bb{j}", g).rearrange("p (b n) -> p b n", b=4)
                    for q in range(2):
                        part = ssd[:, (q * NB + 4 * j) * P:(q * NB + 4 * j + 4) * P]
                        last_read(f"bb{j}", q, dve.tensor_tensor(
                            stmp.rearrange("p (b n) -> p b n", b=4), bk,
                            spread(xdts[:, q * NB + 4 * j:q * NB + 4 * j + 4]), ALU.mult))
                        do(dve.tensor_tensor(part, part, stmp, ALU.add))
                for j in range(2):
                    bk = got(G, f"cc{j}", g)
                    for q in range(2):
                        part = ssd[:, (q * NB + 4 * j) * P:(q * NB + 4 * j + 4) * P]
                        last_read(f"cc{j}", q, dve.tensor_tensor(stmp, part, bk, ALU.mult))
                        do(dve.tensor_reduce(ysm[:, q * NB + 4 * j:q * NB + 4 * j + 4],
                                             stmp.rearrange("p (b n) -> p b n", b=4), AX_X, ALU.add))
                for q in range(2):
                    do(dve.tensor_tensor(yT[q][:, T:NT], yT[q][:, T:NT], ysm[:, q * NB:(q + 1) * NB], ALU.add))
                    dve.wait_ge(z_ready, 2 * g + q + 1)
                    taken(G, "y3", g)
                    dve.tensor_tensor(yT[q], yT[q], zs[q], ALU.mult).then_inc(y_ready, 1)
                taken(G, "nst", g)
                dve.reciprocal(srn, ssq).then_inc(rn_ready, 1)
                dve.wait_ge(y_ready, 2 * g + 2)
                for j, name in enumerate(("nb0", "nb1", "nb8")):
                    bk = got(G, name, g)
                    a, z = j * 512, min((j + 1) * 512, NT)
                    for q in range(2):
                        ins = dve.scalar_tensor_tensor(out=yT[q][:, a:z], in0=yT[q][:, a:z],
                                                       scalar=snw[:, q:q + 1], in1=bk[:, 0:z - a],
                                                       op0=ALU.mult, op1=ALU.mult)
                    if name != "nb8":
                        give(G, name, ins)
                    else:
                        give(G, name, ins)
                taken(G, "nb8", g)
                dve.sem_inc(yb_ready, 1)

            body(0, True)
            with dve.Fori(1, SG_N - 1) as g:
                body(g, True)
            body(SG_N - 1, False)
            dve.drain().then_inc(phase_done, 1)
            dve.wait_ge(phase_done, 20)

            lane.restart()
            dve.wait_ge(late_loaded, 48)

            def mixed(j, i):
                m = mg[:, bass.ds(j * NT + i * NT, NT)]
                for n in range(3):
                    dve.wait_ge(proj_full, 9 * j + (3 * (W_UPB + 3 * i + 2) + n + 1))
                    dve.wait_ge(proj_taken, 3 * j + (A_UPB + 3 * i + n + 1))
                    c = slice(n * GW, (n + 1) * GW)
                    lane.step(dve.scalar_tensor_tensor(out=tsum[:, c], in0=tgate2[i][:, c], scalar=1.0,
                                                       in1=psum[:, n, 0:GW], op0=ALU.add, op1=ALU.mult))
                    lane.settle()
                    dst = mg[:, bass.ds(j * NT + (i * NT + n * GW), GW)]
                    dve.tensor_tensor(dst, dst, tsum[:, c], ALU.add).then_inc(sum_taken, 1)

            mixed(0, 0)
            mixed(0, 1)
            with dve.Fori(1, KT // 2) as pair:
                j = pair * 2
                lane.restart()
                mixed(j, 0)
                mixed(j, 1)
            with dve.Fori(0, KT // 2) as pair:
                j = pair * 2
                for i in range(2):
                    for n in range(3):
                        dve.wait_ge(proj_full, 3 * j + (3 * (W_OUT + i) + n + 1))
                        dst = x1[:, bass.ds(j * NT + (i * NT + n * GW), GW)]
                        dve.scalar_tensor_tensor(out=dst, in0=psum[:, n, 0:GW], scalar=0.5, in1=dst,
                                                 op0=ALU.mult, op1=ALU.add).then_inc(sum_taken, 1)
            dve.drain().then_inc(phase_done, 1)
            dve.wait_ge(phase_done, 25)

            lane.restart()
            G = mem_plan
            taken(G, "mst")
            dve.reciprocal(mrn, mstat).then_inc(rn_ready, 1)
            dve.reciprocal(xrn, xstat).then_inc(rn_ready, 1)
            bk = got(G, "mbc")
            for k in range(KT):
                ins = dve.scalar_tensor_tensor(out=mn[:, k, :], in0=memTv[:, k, :], scalar=vt[:, v_mem + k:v_mem + k + 1],
                                               in1=bk[:, 0:M_N], op0=ALU.mult, op1=ALU.mult)
            give(G, "mbc", ins)
            with dve.Fori(0, KT // 2) as pair:
                j = pair * 2
                for i in range(2):
                    dve.wait_ge(proj_full, 3 * j + 3 * (W_MK + i + 1))
                    dve.tensor_copy(Ktok[:, :, bass.ds(j * P + i * P, P)],
                                    psum[:, i, 0:MT * P].rearrange("p (t c) -> p t c", t=MT)).then_inc(sum_taken, 1)

            def normed(plan, name, v):
                for j in range(3):
                    bk = got(plan, f"{name}{j}")
                    a, z = j * 512, min((j + 1) * 512, NT)
                    for k in range(KT):
                        ins = dve.scalar_tensor_tensor(out=xnv[:, k, a:z], in0=x1v[:, k, a:z],
                                                       scalar=vt[:, v + k:v + k + 1], in1=bk[:, 0:z - a],
                                                       op0=ALU.mult, op1=ALU.mult)
                    give(plan, f"{name}{j}", ins)

            normed(G, "xb", v_x)
            for name in ("qt0", "qt1"):
                taken(G, name)
            G = attn_plan

            lane.restart()
            with dve.Fori(0, XH_N) as h:
                for s in range(2):
                    dve.tensor_copy(qh[s], qT[:, bass.ds(h * 2 * NT, 2 * NT)].rearrange(
                        "p (k t) -> p k t", k=2)[:, :, s * 512:(s + 1) * 512])
                    dve.tensor_tensor(qm[s][0:NB, :], qtok[0:NB, :],
                                      ident[0:NB, bass.ds(h * 2 + s, 1)].broadcast_to([NB, D]), ALU.mult
                                      ).then_inc(q_ready, 1)
                dve.tensor_copy(vh, Vtok[:, :, bass.ds(h * XD, XD)]).then_inc(vh_ready, 1)
                for s in range(2):
                    for i in range(2):
                        bk = got(G, f"sc{s}{i}", h)
                        do(dve.tensor_reduce(nmx[s][:, 2 * i:2 * i + 2], bk.rearrange("p (c m) -> p c m", c=2),
                                             AX_X, ALU.max))
                    dve.tensor_scalar(nmx[s], nmx[s], -x_scale, None, ALU.mult).then_inc(mx_ready, 1)
                for s in range(2):
                    taken(G, f"sc{s}1", h)
                    dve.reciprocal(prs[s], psm[s]).then_inc(rs_ready, 1)

                def key_products(s, t):
                    if t == 0:
                        dve.wait_ge(kc_loaded[s], 16 * h + 16)
                        taken(G, f"qb{s}1", h)
                        do(dve.tensor_tensor(kc[s][:, 0, :], kc[s][:, 0, :], qrep[s], ALU.mult))
                    else:
                        dve.wait_ge(kprod_ready, 2 * h + s + 1)
                    ins = dve.tensor_reduce(s8[s][:, t, :], kc[s][:, t, :].rearrange("p (h d) -> p h d", h=XH_N),
                                            AX_X, ALU.add)
                    if t == MT - 1:
                        ins.then_inc(s8_ready, 1)

                def bias4(s):
                    bk = got(G, f"st{s}", h)
                    do(dve.tensor_reduce(mx4[s][0:XH_N, :], bk[0:XH_N, 0:M_N], AX_X, ALU.max))
                    dve.tensor_scalar(mx4[s][0:XH_N, :], mx4[s][0:XH_N, :], -x_scale, None, ALU.mult
                                      ).then_inc(m4_ready, 1)

                def probs4(s):
                    taken(G, f"st{s}", h)
                    do(dve.reciprocal(r4[s][0:XH_N, :], sm4[s][0:XH_N, :]))
                    dve.tensor_scalar(e4[s][0:XH_N, :], e4[s][0:XH_N, :], r4[s][0:XH_N, :], None, ALU.mult
                                      ).then_inc(p4_ready, 1)

                def out4(s):
                    bk = got(G, f"os{s}", h)
                    give(G, f"os{s}", dve.tensor_copy(atv[:, :, bass.ds(h * 2 + (s + T), 1)],
                                                      bk[:, 0:KT].unsqueeze(2)))

                key_products(0, 0)
                key_products(0, 1)
                bias4(0)
                key_products(1, 0)
                probs4(0)
                key_products(1, 1)
                out4(0)
                bias4(1)
                probs4(1)
                out4(1)
                lane.restart()
            with dve.Fori(0, KT // 2) as pair:
                j = pair * 2
                for i in range(2):
                    for n in range(3):
                        dve.wait_ge(proj_full, 3 * j + (3 * (W_CO + i) + n + 1))
                        dst = x1[:, bass.ds(j * NT + (i * NT + n * GW), GW)]
                        dve.tensor_tensor(dst, dst, psum[:, n, 0:GW], ALU.add).then_inc(sum_taken, 1)

            G = ff_plan
            taken(G, "fst")
            dve.reciprocal(xrn, xstat).then_inc(rn_ready, 1)
            normed(G, "fb", v_ff)
            for half_ in range(2):
                base = W_FU + half_ * 2 * FH
                with dve.Fori(0, FH) as j:
                    for n in range(3):
                        dve.wait_ge(proj_taken, 3 * j + (A_END + half_ * 3 * FH + n + 1))
                        hidden = hf[:, bass.ds(j * NT + n * GW, GW)]
                        dve.tensor_tensor(hidden, hidden, psum[:, n, 0:GW], ALU.mult).then_inc(sum_taken, 1)
                with dve.Fori(0, KT) as j:
                    for n in range(3):
                        dve.wait_ge(proj_full, 6 * j + (3 * (base + FH + 1) + n + 1))
                        dst = x1[:, bass.ds(j * NT + n * GW, GW)]
                        dve.tensor_tensor(dst, dst, psum[:, n, 0:GW], ALU.add).then_inc(sum_taken, 1)
            taken(G, "zst")
            do(dve.reciprocal(xrn, xstat))
            dve.wait_ge(gfin_loaded, 16)
            for c in range(NC + 1):
                for j in range(2):
                    bk = got(G, f"y{c}_{j}")
                    give(G, f"y{c}_{j}", dve.scalar_tensor_tensor(
                        out=ytok[:, c, j * 512:(j + 1) * 512], in0=bk, scalar=xrn[:, c:c + 1],
                        in1=gfin[:, j * 512:(j + 1) * 512], op0=ALU.mult, op1=ALU.mult))
                taken(G, f"y{c}_1")
                dve.sem_inc(yt_ready, 1)

        @block.gpsimd
        def _(pool):
            lane = Lane(pool, pool_step)

            def do(ins):
                lane.step(ins)
                lane.settle()

            def waited():
                lane.step(pool)
                lane.settle()

            def earlier_taps(y, x, col, tmp):
                for i in range(CW - 1):
                    for a, n, src in ((0, 512, x[:, i:i + 512]), (512, 512, x[:, 512 + i:T + i]),
                                      (T, NB, col[:, i:24:3])):
                        t = tmp[:, 0:n] if n > NB else tmp[:, 512:512 + NB]
                        do(pool.tensor_scalar(t, src, col[:, 24 + i:25 + i], None, ALU.mult))
                        ins = pool.tensor_tensor(y[:, a:a + n], y[:, a:a + n], t, ALU.add)
                        if i < CW - 2 or n > NB:
                            do(ins)
                return ins

            pool.memset(hb, 0.0)
            pool.memset(wsc, 0.0)
            pool.memset(cstage[0:32, :], 0.0).then_inc(consts_ready, 1)
            do(pool.memset(ones[:, :], 1.0))
            do(pool.memset(eps[:, :], EPS))
            do(pool.memset(bd8[:, :], 1.0))
            do(pool.memset(expand[0:32, :], 1.0))
            do(pool.affine_select(out=ident[:, :], in_=ones[:, :], pattern=[[-1, P]], compare_op=ALU.is_equal,
                                  fill=0.0, base=0, channel_multiplier=1))
            do(pool.affine_select(out=triu[:, :], in_=ones[:, :], pattern=[[1, P]], compare_op=ALU.is_ge,
                                  fill=0.0, base=0, channel_multiplier=-1))
            b8 = bd8[:, :].rearrange("p (b e) -> p b e", b=NB)
            do(pool.affine_select(out=b8, in_=b8, pattern=[[-1, NB], [0, P]], compare_op=ALU.is_equal,
                                  fill=0.0, base=0, channel_multiplier=1))
            ex = expand[0:32, :].rearrange("p (h e) -> p h e", h=SH_N)
            do(pool.affine_select(out=ex, in_=ex, pattern=[[-1, SH_N], [0, HD]], compare_op=ALU.is_equal,
                                  fill=0.0, base=0, channel_multiplier=1))
            do(pool.memset(lvl[:, :], 0.0))
            for L in range(7):
                b = 1 << L
                m = cols(lvl, L).rearrange("p (n s r) -> p n s r", s=2, r=b)[:, :, 0, :]
                nblk = P // (2 * b)
                do(pool.memset(m, 1.0))
                do(pool.affine_select(out=m, in_=m, pattern=[[-2 * b, nblk], [0, b]], compare_op=ALU.is_ge,
                                      fill=0.0, base=-b, channel_multiplier=1))
                do(pool.affine_select(out=m, in_=m, pattern=[[2 * b, nblk], [0, b]], compare_op=ALU.is_ge,
                                      fill=0.0, base=2 * b - 1, channel_multiplier=-1))
            pool.sem_inc(consts_ready, 1)
            pool.drain().then_inc(phase_done, 1)
            pool.wait_ge(phase_done, SETUP_ENDS)

            G = gdn_plan

            def convolve(h, u):
                wait(pool, proj_taken, 12 * h + 3 * u + 3)
                waited()
                y, x, col = conv[u], raw[u], cwf[:, u, :]
                do(pool.tensor_scalar(y, x[:, 3:3 + NT], col[:, 27:28], None, ALU.mult))
                earlier_taps(y, x, col, tap).then_inc(conv_done, 1)

            def mix(h, u):
                pool.wait_ge(tanh_ready, 4 * h + u + 1)
                waited()
                do(pool.tensor_scalar(tnh[u % 2], tnh[u % 2], 1.0, None, ALU.add))
                pool.tensor_tensor(conv[u], conv[u], tnh[u % 2], ALU.mult).then_inc(qkv_ready, 1)

            pool.wait_ge(cw_ready, 1)
            for u in range(3):
                convolve(0, u)
            for u in range(3):
                mix(0, u)
                pool.wait_ge(qkv_ready, u + 1)
                pool.sem_inc(tanh_used, 1)

            def body(h, more):
                lane.restart()
                pool.wait_ge(tanh_ready, 4 * h + 4)
                wait(pool, oa_ready, h)
                waited()
                do(pool.tensor_scalar(tnh[1], tnh[1], 1.0, None, ALU.add))
                pool.tensor_tensor(ggs, tnh[1], ggr, ALU.mult).then_inc(gate_ready, 1)
                pool.wait_ge(gate_ready, h + 1)
                pool.sem_inc(tanh_used, 1)
                for i, d in enumerate((dec1, dec2)):
                    pool.wait_ge(dec_exp, 2 * h + i + 1)
                    waited()
                    dv = d.rearrange("p (c i) -> p c i", c=NC)
                    pool.affine_select(out=dv, in_=dv, pattern=[[0, NC], [-1, P] if i == 0 else [1, P]],
                                       compare_op=ALU.is_gt if i == 0 else ALU.is_ge, fill=0.0, base=0,
                                       channel_multiplier=1 if i == 0 else -1).then_inc(dec_masked, 1)
                for j in range(2):
                    pool.wait_ge(bank_taken[G.bank(f"kk{j}")], G.after(f"kk{j}", h))
                for L in range(7):
                    if L == 2:
                        pool.wait_ge(bank_full[G.bank("y1")], G.after("y1", h))
                        pool.wait_ge(bank_taken[G.bank("y1")], G.after("y1", h))
                    elif L > 2:
                        pool.wait_ge(bank_full[G.bank(f"p{L - 2}_1")], G.after(f"p{L - 2}_1", h))
                    waited()
                    pool.tensor_tensor(
                        aml[L % 2].rearrange("p (c i) -> p c i", c=NC), amat.rearrange("p (c i) -> p c i", c=NC),
                        per_chunk(cols(lvl, L), NC), ALU.mult).then_inc(am_ready, 1)
                pool.wait_ge(hs_ready, h + 1)
                pool.wait_ge(sdec_loaded, 16 * h + 16)
                sdv = sdec.rearrange("p (b e) -> p b e", b=NB)
                pool.tensor_tensor(sdv, sdv, spread(hs8[:, 0:NB]), ALU.mult).then_inc(sd_ready, 1)
                if more:
                    pool.wait_ge(cw_ready, h + 2)
                    pool.wait_ge(bank_taken[G.bank("b8")], G.after("b8", h))
                    pool.wait_ge(bank_taken[G.bank("tv1")], G.after("tv1", h))
                    convolve(h + 1, 0)
                    convolve(h + 1, 1)
                    for u in range(3):
                        if u == 1:
                            convolve(h + 1, 2)
                        mix(h + 1, u)
                        pool.wait_ge(qkv_ready, 3 * (h + 1) + u + 1)
                        pool.sem_inc(tanh_used, 1)

            body(0, True)
            with pool.Fori(1, GH_N - 1) as h:
                body(h, True)
            body(GH_N - 1, False)
            pool.drain().then_inc(phase_done, 1)
            pool.wait_ge(phase_done, 10)
            pool.drain().then_inc(phase_done, 1)
            pool.wait_ge(phase_done, 15)

            lane.restart()

            def convolve(g, u):
                wait(pool, proj_taken, 18 * g + (A_SSM + 3 * u + 3))
                waited()
                y, x, col = sconv[u], sraw[u], scw[:, u, :]
                do(pool.tensor_scalar(y, x[:, 3:3 + NT], col[:, 27:28], col[:, 28:29], ALU.mult, ALU.add))
                earlier_taps(y, x, col, stap).then_inc(sconv_done, 1)

            def mix(g, u):
                pool.wait_ge(stanh_ready, 6 * g + u + 1)
                waited()
                src, dst = (sconv[u], sconv[u]) if u < 4 else (zraw[u - 4], zs[u - 4])
                do(pool.tensor_scalar(stnh[u % 2], stnh[u % 2], 1.0, None, ALU.add))
                ins = pool.tensor_tensor(dst, stnh[u % 2], src, ALU.mult)
                if u < 4:
                    ins.then_inc(sx_ready, 1)
                    pool.wait_ge(sx_ready, 4 * g + u + 1)
                else:
                    ins.then_inc(z_ready, 1)
                    pool.wait_ge(z_ready, 2 * g + u - 3)
                pool.sem_inc(stanh_used, 1)

            pool.wait_ge(scw_ready, 1)
            for u in range(4):
                convolve(0, u)
            for u in range(4):
                mix(0, u)

            def body(g, more):
                lane.restart()
                wait(pool, y_ready, 2 * g)
                mix(g, 4)
                mix(g, 5)
                pool.wait_ge(shx_ready, g + 1)
                pool.wait_ge(ssd_loaded, 32 * g + 32)
                for q in range(2):
                    sv = ssd[:, q * NB * P:(q + 1) * NB * P].rearrange("p (b n) -> p b n", b=NB)
                    ins = pool.tensor_tensor(sv, sv, spread(shx[:, 17 * q + NB:17 * q + 2 * NB]), ALU.mult)
                ins.then_inc(ssd_ready, 1)
                if more:
                    pool.wait_ge(scw_ready, g + 2)
                    pool.wait_ge(x_used, g + 1)
                    convolve(g + 1, 0)
                    convolve(g + 1, 1)
                    mix(g + 1, 0)
                    mix(g + 1, 1)
                    convolve(g + 1, 2)
                    convolve(g + 1, 3)
                    mix(g + 1, 2)
                    mix(g + 1, 3)

            G = ssm_plan
            body(0, True)
            with pool.Fori(1, SG_N - 1) as g:
                body(g, True)
            body(SG_N - 1, False)
            pool.drain().then_inc(phase_done, 1)
            pool.wait_ge(phase_done, 20)
            pool.drain().then_inc(phase_done, 1)
            pool.wait_ge(phase_done, 25)

            G = attn_plan
            lane.restart()
            with pool.Fori(0, XH_N) as h:
                for s in range(2):
                    pool.wait_ge(rs_ready, 2 * h + s + 1)
                    waited()
                    for c in range(4):
                        ins = pool.tensor_scalar(pr[s][:, c, :], pr[s][:, c, :], prs[s][:, c:c + 1], None, ALU.mult)
                    ins.then_inc(p_ready, 1)
                    pool.wait_ge(kc_loaded[s], 16 * h + 16)
                    pool.wait_ge(bank_taken[G.bank(f"qb{s}1")], G.after(f"qb{s}1", h))
                    pool.tensor_tensor(kc[s][:, 1, :], kc[s][:, 1, :], qrep[s], ALU.mult).then_inc(kprod_ready, 1)
                lane.restart()


INPUTS = ("x_prompt", "x_sample", "mem_prompt", "state_gdn_conv", "state_gdn", "state_ssm_conv", "state_ssm",
          "cache_mem_k", "cache_mem_v", "g_mix", "w_in", "gdn_conv_w", "gdn_A_log", "gdn_dt_bias", "gdn_norm_w",
          "w_gdn_up", "ssm_conv_w", "ssm_conv_b", "ssm_dt_bias", "ssm_A_log", "ssm_D", "ssm_norm_w", "w_ssm_up",
          "w_out", "g_mem", "w_mk", "w_mv", "g_x", "w_cq", "w_co", "g_ff", "w_ff_up", "w_ff_down", "g_final")


def output_shapes(inputs):
    shape = {n: tuple(inputs[n].shape) for n in inputs}
    conv_g, conv_s, cache = shape["state_gdn_conv"], shape["state_ssm_conv"], shape["cache_mem_k"]
    one = (1, 1)
    return {
        "y_prompt": shape["x_prompt"], "y_sample": shape["x_sample"],
        "p_gdn_conv": one + conv_g[2:], "p_gdn": one + shape["state_gdn"][2:],
        "p_ssm_conv": one + conv_s[2:], "p_ssm": one + shape["state_ssm"][2:],
        "p_mem_k": one + cache[2:], "p_mem_v": one + cache[2:],
        "s_gdn_conv": conv_g, "s_gdn": shape["state_gdn"], "s_ssm_conv": conv_s, "s_ssm": shape["state_ssm"],
    }


def kernel(**inputs):
    import numpy as np
    import concourse.bacc as bacc
    from concourse.bass_utils import run_bass_kernel_spmd

    nc = bacc.Bacc("TRN2", target_bir_lowering=False, num_devices=1)
    arrays, io = {}, {}
    for name in INPUTS:
        arrays[f"in_{name}_dram"] = a = np.ascontiguousarray(inputs[name])
        io[name] = nc.dram_tensor(f"in_{name}_dram", a.shape, mybir.dt.from_np(a.dtype), kind="ExternalInput").ap()
    outs = output_shapes(inputs)
    for i, (name, shape) in enumerate(outs.items()):
        io[name] = nc.dram_tensor(f"out_{i}_dram", shape, F32, kind="ExternalOutput").ap()
    hybrid_step(nc, io)
    r = run_bass_kernel_spmd(nc, [arrays], core_ids=[0])
    return tuple(r.results[0][f"out_{i}_dram"] for i in range(len(outs)))
```

```python
from contextlib import ExitStack

import concourse.bass as bass
from concourse import mybir

F32 = mybir.dt.float32
F32R = mybir.dt.float32r
ALU = mybir.AluOpType
ACT = mybir.ActivationFunctionType
AX_X = mybir.AxisListType.X

P = 128


def wait(eng, sem, value):
    if isinstance(value, int) and value <= 0:
        return
    eng.wait_ge(sem, value)


class Banks:

    def __init__(self, base, names):
        self.base, self.place, self.per = dict(base), {}, {b: 0 for b in base}
        nxt, ring = 0, sorted(base)
        for name in names:
            if isinstance(name, tuple):
                name, bank = name
            else:
                bank = ring[nxt % len(ring)]
                nxt += 1
            self.place[name] = (bank, self.per[bank])
            self.per[bank] += 1

    def bank(self, name):
        return self.place[name][0]

    def before(self, name, it=0):
        b, n = self.place[name]
        return self.base[b] + it * self.per[b] + n

    def after(self, name, it=0):
        b, n = self.place[name]
        return it * self.per[b] + (self.base[b] + n + 1)

    def next_base(self, iterations=1):
        return {b: self.base[b] + iterations * self.per[b] for b in self.base}


def rounded(ap):
    return ap.bitcast(F32R)


class Lane:

    def __init__(self, eng, sem):
        self.eng, self.sem, self.n = eng, sem, 0

    def step(self, ins):
        if ins is self.eng:
            ins.sem_inc(self.sem, 1)
        else:
            ins.then_inc(self.sem, 1)
        self.n += 1

    def settle(self):
        if self.n:
            self.eng.wait_ge(self.sem, self.n)

    def restart(self):
        self.settle()
        self.eng.sem_clear(self.sem)
        self.n = 0


def hybrid_step(nc, io):
    x_prompt, x_sample, mem_prompt = io["x_prompt"], io["x_sample"], io["mem_prompt"]
    T, D = x_prompt.shape[1:]
    NB = x_sample.shape[0]
    NT = T + NB
    KT = D // P
    NC = T // P
    NG = 3
    GW = NT // NG
    GH_N = io["state_gdn"].shape[2]
    GC = io["gdn_conv_w"].shape[2]
    GQ = GC // 3
    SC_ = io["ssm_conv_w"].shape[2]
    SH_N = io["ssm_A_log"].shape[1]
    SDI = io["w_ssm_up"].shape[1]
    SG_N = 8
    HPG = SH_N // SG_N
    HD = SDI // SH_N
    FF = io["w_ff_up"].shape[2]
    CW = io["gdn_conv_w"].shape[1]
    CT_N = (GC + SC_) // P
    GT_N = GC // P
    EPS = 1e-6
    assert NG * GW == NT and GW <= 512 and HD * 2 == P and CW == 4

    c_qkv, c_ggate = 0, GC
    c_b = c_ggate + GQ
    c_a = c_b + GH_N
    c_z = c_a + GH_N
    c_xbc = c_z + SDI
    c_dt = c_xbc + SC_
    c_ga = c_dt + SH_N
    c_gb = c_ga + D

    with ExitStack() as ctx:
        place = {}

        def sb(name, cols, rows=P):
            place[name] = (nc.sbuf_base + 31) // 32 * 32
            return ctx.enter_context(nc.sbuf_tensor(name, [rows, cols], F32))

        def sem(name):
            return ctx.enter_context(nc.semaphore(name))

        def overlay(name, under, at_, cols):
            return nc.alloc_sbuf_tensor_at(name, [P, cols], F32, offset=place[under] + 4 * at_)[:, :]

        def scratch(name, shape):
            return nc.dram_tensor(name, shape, F32).ap()

        d_xT = scratch("d_xT", [KT, P, NT])
        d_rows = scratch("d_rows", [SH_N + GH_N, T])
        d_gb8 = scratch("d_gb8", [2, GH_N * NB])
        d_mg = scratch("d_mg", [KT, P, NT])
        d_yb = scratch("d_yb", [SDI // P, P, NT])

        ident = sb("ident", P)
        ones = sb("ones", P)
        triu = sb("triu", P)
        eps = sb("eps", 1)
        VT_N = 5 * KT + SDI // P + 1
        vt = sb("vt", VT_N)
        tables = sb("tables", 7 * P + NB * P + CT_N * 29 + GH_N * 5 * NC + SG_N * 4 * NC * HPG)
        tcut = [0]

        def table(cols):
            tcut[0] += cols
            return tables[:, tcut[0] - cols:tcut[0]]

        lvl = table(7 * P)
        bd8 = table(NB * P)[0:NB, :]
        ct = table(CT_N * 29)
        ctv = ct[:, :].rearrange("p (t r) -> p t r", r=29)
        gh = table(GH_N * 5 * NC)
        sh = table(SG_N * 4 * NC * HPG)
        dtx = sb("dtx", (SH_N // 2) * 17)
        gb8 = sb("gb8", GH_N * NB)
        bb8 = sb("bb8", GH_N * NB)
        xn = sb("xn", KT * NT)
        xnv = xn[:, :].rearrange("p (k t) -> p k t", k=KT)
        slab = [sb(f"slab{i}", KT * P) for i in range(2)]
        slabv = [s[:, :].rearrange("p (k c) -> p k c", k=KT) for s in slab]
        AR = 37100
        arena = sb("arena", AR)
        cut = [0]

        def carve(cols):
            a = cut[0]
            cut[0] += cols
            assert cut[0] <= AR, cut[0]
            return arena[:, a:a + cols]

        psum = ctx.enter_context(nc.psum_tensor("psum", [P, 8, 512], F32))

        slab_loaded = [sem(f"slab_loaded{i}") for i in range(2)]
        proj_full = sem("proj_full")
        proj_taken = sem("proj_taken")
        bank_full = {b: sem(f"bank_full{b}") for b in range(3, 8)}
        bank_taken = {b: sem(f"bank_taken{b}") for b in range(3, 8)}
        phase_done = sem("phase_done")
        act_step, dve_step, pool_step = (sem(n) for n in ("act_step", "dve_step", "pool_step"))
        consts_ready, ident_ready = sem("consts_ready"), sem("ident_ready")
        params_loaded = sem("params_loaded")
        x_loaded = [sem(f"x_loaded{i}") for i in range(3)]
        sq_ready = sem("sq_ready")
        rn_ready = sem("rn_ready")
        raw72_done, rows_ready, rx_ready, tab_exp = (sem(n) for n in ("raw72_done", "rows_ready", "rx_ready", "tab_exp"))
        dve_to_act, act_to_dve = sem("dve_to_act"), sem("act_to_dve")
        gbr_loaded, sdec_loaded, sdec_stored, S_stored, rw_stored = (
            sem(n) for n in ("gbr_loaded", "sdec_loaded", "sdec_stored", "S_stored", "rw_stored"))
        qg_ready = sem("qg_ready")
        tanh_ready = sem("tanh_ready")
        tanh_used = sem("tanh_used")
        conv_done = sem("conv_done")
        qkv_ready = sem("qkv_ready")
        gate_ready = sem("gate_ready")
        cw_ready, hs_ready = sem("cw_ready"), sem("hs_ready")
        dec_diff, dec_exp, dec_masked, eg_ready = (sem(n) for n in ("dec_diff", "dec_exp", "dec_masked", "eg_ready"))
        am_ready = sem("am_ready")
        sd_ready = sem("sd_ready")
        oa_ready = sem("oa_ready")
        sum_taken = sem("sum_taken")
        mg_ready, mg_stored = sem("mg_ready"), [sem(f"mg_stored{i}") for i in range(2)]
        sp_step = sem("sp_step")
        csb_loaded, ssd_loaded, ssd_stored, stf_stored, srw_stored, yb_stored = (
            sem(n) for n in ("csb_loaded", "ssd_loaded", "ssd_stored", "stf_stored", "srw_stored", "yb_stored"))
        yb_loaded = [sem(f"yb_loaded{i}") for i in range(2)]
        mg_loaded, x1_loaded = sem("mg_loaded"), sem("x1_loaded")
        sconv_done, sx_ready, z_ready, stanh_ready, stanh_used = (
            sem(n) for n in ("sconv_done", "sx_ready", "z_ready", "stanh_ready", "stanh_used"))
        scw_ready, shx_ready, sdiff, sdec_exp, ecs_ready, ml_ready, cd_ready, ssd_ready, y_ready, yb_ready = (
            sem(n) for n in ("scw_ready", "shx_ready", "sdiff", "sdec_exp", "ecs_ready", "ml_ready", "cd_ready",
                             "ssd_ready", "y_ready", "yb_ready"))
        x_used = sem("x_used")
        mem_loaded, mem_stored, copies_done, gfin_loaded = (
            sem(n) for n in ("mem_loaded", "mem_stored", "copies_done", "gfin_loaded"))
        kc_loaded = [sem(f"kc_loaded{i}") for i in range(2)]
        vc_loaded = [sem(f"vc_loaded{i}") for i in range(2)]
        q_ready, vh_ready, mx_ready, rs_ready, p_ready = (
            sem(n) for n in ("q_ready", "vh_ready", "mx_ready", "rs_ready", "p_ready"))
        kprod_ready, s8_ready, m4_ready, p4_ready = (
            sem(n) for n in ("kprod_ready", "s8_ready", "m4_ready", "p4_ready"))
        w_split = sem("w_split")
        xt_ready = sem("xt_ready")
        xr_ready = sem("xr_ready")
        xs_ready = sem("xs_ready")
        hr_ready, h_ready = sem("hr_ready"), sem("h_ready")
        ohi_ready = sem("ohi_ready")
        yt_ready, y_stored = sem("yt_ready"), sem("y_stored")
        stored = sem("stored")

        w_in = io["w_in"][0].rearrange("(k p) c -> p k c", p=P)

        v_mix, v_mem, v_x, v_ff, v_fin, v_ssm = 0, KT, 2 * KT, 3 * KT, 4 * KT, 5 * KT
        v_gdn = v_ssm + SDI // P

        cut[0] = 0
        xload = carve(9 * D).rearrange("p (t d) -> p t d", t=9)
        xT = carve(KT * NT).rearrange("p (k t) -> p k t", k=KT)
        cstage = carve(GC + SC_)
        vstage = carve(P)
        expand = carve(SH_N * HD)
        wsc = carve(KT * 72).rearrange("p (k c) -> p k c", k=KT)
        raw72 = carve(NT)
        hb = carve(2)
        sp_t = carve(NT)
        xl_flat = arena[:, 0:9 * D]
        t_e, t_u, t_l, t_c = (xl_flat[:, i * NT:(i + 1) * NT] for i in range(4))
        rows72 = xl_flat[:, 4 * NT:5 * NT]
        tok72 = xl_flat[:, 5 * NT:5 * NT + NC * 72].rearrange("p (c h) -> p c h", c=NC)
        tokd = xl_flat[:, 6 * NT:6 * NT + NC * 32].rearrange("p (c h) -> p c h", c=NC)
        cst = xl_flat[:, 6 * NT + 256:6 * NT + 256 + 320].rearrange("p (c h) -> p c h", c=NC)
        tote = xl_flat[:, 6 * NT + 576:6 * NT + 576 + 320].rearrange("p (c h) -> p c h", c=NC)
        dout = xl_flat[:, 7 * NT:7 * NT + 320].rearrange("p (c h) -> p c h", c=NC)
        rx = carve(17)
        egc = carve(GH_N * NC).rearrange("p (c h) -> p c h", c=NC)
        stat = carve(9)
        rnorm = carve(9)
        csr_full = carve(T)

        cut[0] = 0
        oa = carve(KT * NT)
        oav = oa.rearrange("p (k t) -> p k t", k=KT)
        raw = [carve(NT + 3) for _ in range(3)]
        conv = [carve(NT) for _ in range(3)]
        ggr, ggs = carve(NT), carve(NT)
        tnh = [carve(NT) for _ in range(2)]
        qn, kn = carve(NT), carve(NT)
        gbr = carve(T)
        dec1, dec2 = carve(T), carve(T)
        amat, aml1 = carve(T), carve(T)
        aml0 = dec1
        X, Y, Pp = carve(T), carve(T), carve(T)
        kbe, kd, vb, qg = carve(T), carve(T), carve(T), carve(T)
        wtn = X
        aml = [aml0, aml1]
        vnew = [carve(P) for _ in range(2)]
        Sst = [carve(P) for _ in range(2)]
        oT = carve(NT)
        sdec = carve(NB * P)
        hs = carve(5 * NC)
        hs8 = carve(2 * NB)
        st2, rn2 = carve(18), carve(18)
        cwf = carve(3 * 29).rearrange("p (u r) -> p u r", u=3)
        rwst = carve(3 * P)
        k8, v8n, vs8 = carve(P), carve(NB), carve(NB)
        vbd = amat
        sq2 = qn

        cut[0] = KT * NT
        tgate = [carve(NT) for _ in range(2)]
        mgst = [carve(NT) for _ in range(2)]

        cut[0] = 0
        sraw = [carve(NT + 3) for _ in range(4)]
        sconv = [carve(NT) for _ in range(4)]
        zraw, zs = [carve(NT) for _ in range(2)], [carve(NT) for _ in range(2)]
        stnh = [carve(NT) for _ in range(2)]
        csb = carve(HPG * T)
        btok = carve(T)
        xdt, xdd = carve(T * 2), carve(T * 2)
        cbm = carve(T)
        ml = carve(HPG * T)
        SST = [carve(2 * P) for _ in range(2)]
        yT = [carve(NT) for _ in range(2)]
        ml_sq = [ml[:, 0:NT], ml[:, NT:2 * NT]]
        ssd = carve(2 * NB * P)
        shs, shx, snw = carve(4 * NC * HPG), carve(2 * 17), carve(2)
        scw = carve(4 * 29).rearrange("p (u r) -> p u r", u=4)
        bdg, cdg = carve(NB * P), carve(NB * P)
        stmp = carve(4 * P)
        ssq, srn = carve(9), carve(9)
        xdts, ysm = carve(2 * NB), carve(2 * NB)
        srw = carve(4 * P)
        stf = carve(2 * P)

        cut[0] = 0
        x1 = carve(KT * NT)
        x1v = x1.rearrange("p (k t) -> p k t", k=KT)
        mg = carve(KT * NT)
        mgv = mg.rearrange("p (k t) -> p k t", k=KT)
        yb = carve(2 * KT * NT)
        ybv = yb.rearrange("p (k t) -> p k t", k=2 * KT)
        tgate2 = [carve(NT) for _ in range(2)]
        tsum = carve(NT)

        tcut[0] = 0
        spare = table

        M_N, XH_N = io["cache_mem_k"].shape[2], io["cache_mem_k"].shape[3]
        MT, XD = M_N // P, D // XH_N
        assert MT == 2 and XD == 2 * P and KT * P == XH_N * XD and NB == 2 * XH_N
        x_scale = float(XD) ** -0.5
        cut[0] = KT * NT
        qT = carve(KT * NT)
        at_from = cut[0]
        carve(KT * NT)
        at = overlay("at", "arena", at_from, KT * NT)
        xlow = overlay("xlow", "xn", 0, KT * NT)
        xlowv = xlow.rearrange("p (k t) -> p k t", k=KT)
        atv = at.rearrange("p (k t) -> p k t", k=KT)
        KTm = carve(KT * M_N)
        Vtok = carve(MT * D).rearrange("p (t c) -> p t c", t=MT)
        kc = [carve(MT * D).rearrange("p (t c) -> p t c", t=MT) for _ in range(2)]
        vc = [carve(MT * D).rearrange("p (t c) -> p t c", t=MT) for _ in range(2)]
        memtok, memT, memsq = kc[0], kc[1].rearrange("p t c -> p (t c)"), vc[0].rearrange("p t c -> p (t c)")
        r1 = overlay("r1", "arena", KT * NT, KT * NT)
        xB, atB = at, r1
        xBv, atBv = (t.rearrange("p (k t) -> p k t", k=KT) for t in (xB, atB))
        memTv, memsqv = (m.rearrange("p (k m) -> p k m", k=KT) for m in (memT, memsq))
        mn = qT[:, 0:KT * M_N].rearrange("p (k m) -> p k m", k=KT)
        Ktok = qT[:, KT * M_N:KT * M_N + MT * D].rearrange("p (t c) -> p t c", t=MT)
        cut2 = [0]

        def part(buf, at_, n):
            at_[0] += n
            return buf[:, at_[0] - n:at_[0]]

        qtok = part(xn, cut2, D)
        qm = [part(xn, cut2, D) for _ in range(2)]
        pr = [part(xn, cut2, 4 * M_N).rearrange("p (c m) -> p c m", c=4) for _ in range(2)]
        PT = part(xn, cut2, 4 * M_N).rearrange("p (t i) -> p t i", t=MT)
        qh = [part(xn, cut2, 2 * 512).rearrange("p (k i) -> p k i", k=2) for _ in range(2)]
        vh = spare(MT * XD).rearrange("p (t d) -> p t d", t=MT)
        qrep = [spare(D), spare(D)]
        wparts = overlay("wparts", "tables", 0, 4 * KT * P)
        wh, wl = ([wparts[:, (2 * part_ + i) * KT * P:(2 * part_ + i + 1) * KT * P] for i in range(2)]
                  for part_ in range(2))
        tcut[0] = 4 * KT * P
        xstat, xrn, mstat, mrn = spare(9), spare(9), spare(MT), spare(MT)
        nmx, psm, prs = ([spare(4) for _ in range(2)] for _ in range(3))
        s8 = [spare(MT * XH_N).rearrange("p (t h) -> p t h", t=MT) for _ in range(2)]
        pT8 = [spare(MT * XH_N) for _ in range(2)]
        mx4, sm4, r4 = ([spare(1) for _ in range(2)] for _ in range(3))
        e4 = [spare(M_N) for _ in range(2)]

        cut[0] = KT * NT
        hA = carve(KT * NT)
        assert cut[0] == 2 * KT * NT
        cut[0] += KT * NT
        hB = overlay("hB", "arena", cut[0], KT * NT)
        carve(KT * NT)
        gfin = carve(D)
        hlow = r1
        hlowv, hBv = (t.rearrange("p (k t) -> p k t", k=KT) for t in (hlow, hB))
        ytok = arena[:, KT * NT:KT * NT + 9 * D].rearrange("p (c d) -> p c d", c=9)

        base0 = {b: 0 for b in range(3, 8)}
        setup_plan = Banks(base0, [f"xt{t}_{j}" for t in range(9) for j in range(2)]
                           + ["vt"] + [f"ct{i}" for i in range(4)]
                           + ["st", "bc0", "bc1", "bc2"]
                           + ["sc0", "sc1", "sc2"] + ["ta0", "ta1", "td", "cs", "tot", "csr0", "csr1", "dtx"])
        names = ["rw", "st", "bq0", "bq1", "bk0", "bk1", "b8", "tv0", "tv1", "tk0", "tk1", "t8",
                 "kk0", "kk1", "qk0", "qk1", "y0", "y1"]
        for L in range(1, 7):
            names += [f"p{L}_0", f"p{L}_1"]
            for j in range(2):
                names += [f"yp{L}_{j}"] + ([f"xp{L}_{j}"] if L < 6 else [])
        names += ["w0", "w1"]
        for c in range(NC):
            if c % 4 == 0:
                names += [(f"ot{c // 4}", 7)]
            names += [(f"vn{c}", 3 + c % 2), (f"su{c}", 5 + c % 2)]
        names += ["ks", "v8", "oo0", "oo1", "od", "nst", "nb0", "nb1", "nb8"]
        gdn_plan = Banks(setup_plan.next_base(), names)
        FILL = {"rw": 8, "norm": 8, "turn": 8, "kkqk": 8, "scan": 4, "decode": 8, "level": 4}
        STEPS = ["rw", "norm", "turn", "kkqk"] + [f"level{L}" for L in range(1, 7)] \
            + [f"scan{c}" for c in range(NC)] + ["decode"]

        def fills(step):
            n = lambda s: FILL[s.rstrip("0123456789")]
            i = STEPS.index(step)
            return sum(n(s) for s in STEPS[:i]), sum(n(s) for s in STEPS[:i + 1])

        snames = ["rw"] + ["tb0", "tb1", "tx0", "tx1", "tx2", "tx3", "t8", "cb0", "cb1"]
        for c in range(NC):
            snames += [(f"su{c}", 5 + c % 2)] + ([(f"y{c // 2}", 3 + c // 2 % 2)] if c % 2 == 0 else [])
        snames += [("fs", 7), "bb0", "bb1", "cc0", "cc1", "nst", "nb0", "nb1", "nb8"]
        ssm_plan = Banks(gdn_plan.next_base(GH_N), snames)
        SFILL = {"rw": 8, "tb": 8, "tx": 16, "cb": 24, "scan": 8, "fs": 8, "decode": 0, "norm": 16}
        SSTEPS = ["rw", "tb", "tx", "cb"] + [f"scan{c}" for c in range(NC)] + ["fs", "decode", "norm"]

        def sfills(step):
            n = lambda s: SFILL[s.rstrip("0123456789")]
            i = SSTEPS.index(step)
            return sum(n(s) for s in SSTEPS[:i]), sum(n(s) for s in SSTEPS[:i + 1])

        mem_plan = Banks(ssm_plan.next_base(SG_N), ["mt00", "mt01", "mt10", "mt11", "xst", "mst", "mbc",
                                                    "xb0", "xb1", "xb2"] + [f"kt{i}" for i in range(4)]
                         + ["qt0", "qt1"])
        anames = [f"{n}{s}{i}" for s in range(2) for n in ("sc", "qb") for i in range(2)]
        for s in range(2):
            anames += [f"pt{s}0", f"pt{s}1", f"st{s}", f"o{s}0", f"o{s}1", f"pb{s}", f"os{s}"]
        attn_plan = Banks(mem_plan.next_base(), anames)
        ff_plan = Banks(attn_plan.next_base(XH_N), ["fst", "fb0", "fb1", "fb2", "zst"]
                        + [f"y{c}_{j}" for c in range(NC + 1) for j in range(2)])

        W_UPA = 4 * GH_N
        W_SSM = W_UPA + 2 * KT
        W_UPB = W_SSM + 6 * SG_N
        W_OUT = W_UPB + 3 * KT
        A_UPA = 3 * W_UPA
        A_SSM = A_UPA + 3 * KT
        A_UPB = A_SSM + 18 * SG_N
        V_UPB = 3 * KT
        V_OUT = V_UPB + 3 * KT
        W_MK = W_OUT + KT
        W_MV = W_MK + KT
        W_CQ = W_MV + KT
        W_CO = W_CQ + KT
        W_FU = W_CO + KT
        FQ_N = FF // P // KT
        W_SPLIT = W_CQ
        A_MV = A_UPB + 3 * KT
        A_CQ = A_MV + KT
        A_END = A_CQ + 3 * KT
        V_MK = V_OUT + 3 * KT
        V_CO = V_MK + KT
        V_FU = V_CO + 3 * KT
        V_Q = 6 * KT
        SQ_SSM, RN_SSM = KT + 3 * GH_N, 1 + 2 * GH_N
        SQ_X, RN_X = SQ_SSM + 2 * SG_N, RN_SSM + SG_N

        block = ctx.enter_context(nc.Block())

        def token_range(c):
            return (c * P, (c + 1) * P) if c < NC else (NT - P, NT)

        def cols(ap, c):
            return ap[:, c * P:(c + 1) * P]

        def half(ap, j):
            return ap[:, j * 512:(j + 1) * 512].rearrange("p (c i) -> p c i", c=4)

        def spread(col, n=P):
            return col.unsqueeze(2).broadcast_to([col.shape[0], col.shape[1], n])

        def per_chunk(mat, n):
            return mat.unsqueeze(1).broadcast_to([mat.shape[0], n, mat.shape[1]])

        SETUP_ENDS = 5

        @block.sync
        def _(sp):
            def load_slab(base, it, k, src):
                wait(sp, proj_full, 3 * it + 3 * (base + k - 1))
                if not isinstance(it, int):
                    sp.sem_inc(sp_step, 1)
                sp.dma_start(slabv[k % 2], src).then_inc(slab_loaded[k % 2], 16)

            def par(dst, src):
                sp.dma_start(dst, src).then_inc(params_loaded, 16)

            for t in range(NC):
                sp.dma_start(xload[:, t, :], x_prompt[0, t * P:(t + 1) * P, :]).then_inc(x_loaded[t // 3], 16)
            sp.dma_start(xload[0:NB, NC, :], x_sample[:, 0, :]).then_inc(x_loaded[2], 16)
            for n, name in enumerate(["g_mix", "g_mem", "g_x", "g_ff"]):
                par(vstage[n * KT:(n + 1) * KT, :], io[name][0].rearrange("(t p) -> t p", p=P))
            par(vstage[4 * KT:5 * KT, :], io["g_final"].rearrange("(t p) -> t p", p=P))
            par(vstage[v_ssm:v_gdn, :], io["ssm_norm_w"][0].rearrange("(t p) -> t p", p=P))
            par(vstage[v_gdn:VT_N, :], io["gdn_norm_w"])
            sp.wait_ge(consts_ready, 1)
            par(cstage[0:24, 0:GC], io["state_gdn_conv"][0].rearrange("b i c -> (b i) c"))
            par(cstage[0:24, GC:GC + SC_], io["state_ssm_conv"][0].rearrange("b i c -> (b i) c"))
            par(cstage[24:28, 0:GC], io["gdn_conv_w"][0])
            par(cstage[24:28, GC:GC + SC_], io["ssm_conv_w"][0])
            par(cstage[28:29, GC:GC + SC_], io["ssm_conv_b"])
            par(hb[32:32 + GH_N, 0:1], io["gdn_dt_bias"].rearrange("o h -> h o"))
            par(hb[0:SH_N, 0:1], io["ssm_dt_bias"].rearrange("o h -> h o"))
            par(hb[32:32 + GH_N, 1:2], io["gdn_A_log"].rearrange("o h -> h o"))
            par(hb[0:SH_N, 1:2], io["ssm_A_log"].rearrange("o h -> h o"))
            par(wsc[:, :, 0:SH_N], w_in[:, :, c_dt:c_dt + SH_N])
            par(wsc[:, :, 32:32 + GH_N], w_in[:, :, c_a:c_a + GH_N])
            par(wsc[:, :, 64:64 + GH_N], w_in[:, :, c_b:c_b + GH_N])
            par(rx[0:SH_N, 16:17], io["ssm_D"].rearrange("o h -> h o"))
            def head_slab(h, u):
                col = h * P + (u * GQ if u < 3 else c_ggate)
                load_slab(0, 4 * h, u, w_in[:, :, bass.ds(col, P)])

            head_slab(0, 0)
            head_slab(0, 1)
            for b in range(3, 8):
                sp.wait_ge(bank_taken[b], setup_plan.after([n for n in setup_plan.place if n.startswith("xt")
                                                            and setup_plan.bank(n) == b][-1]))
            sp.dma_start(d_xT.rearrange("k p t -> p k t"), xT).then_inc(stored, 16)
            sp.wait_ge(rows_ready, 1)
            sp.dma_start(d_rows[:, :], csr_full[0:SH_N + GH_N, :]).then_inc(stored, 16)
            sp.dma_start(d_gb8[0].rearrange("(h b) -> h b", b=NB), rows72[32:32 + GH_N, T:NT]).then_inc(stored, 16)
            sp.dma_start(d_gb8[1].rearrange("(h b) -> h b", b=NB), rows72[64:64 + GH_N, T:NT]).then_inc(stored, 16)
            sp.wait_ge(stored, 64)
            sp.dma_start(gb8[:, :], d_gb8[0].partition_broadcast(P)).then_inc(params_loaded, 16)
            sp.dma_start(bb8[:, :], d_gb8[1].partition_broadcast(P)).then_inc(params_loaded, 16)

            for kind in ("gdn", "ssm"):
                sp.dma_start(io[f"s_{kind}_conv"][0, :, 0:CW - 2, :], io[f"state_{kind}_conv"][0, :, 1:CW - 1, :]
                             ).then_inc(copies_done, 16)

            def gb_load(h):
                sp.dma_start(gbr, d_rows[bass.ds(h + SH_N, 1), :].rearrange("o t -> (o t)").partition_broadcast(P)
                             ).then_inc(gbr_loaded, 16)

            def sd_load(h):
                sp.dma_start(sdec.rearrange("p (b e) -> p b e", b=NB),
                             io["state_gdn"][0, :, bass.ds(h, 1)].rearrange("b o k e -> k (b o) e")
                             ).then_inc(sdec_loaded, 16)

            sp.drain().then_inc(phase_done, 1)
            sp.wait_ge(phase_done, SETUP_ENDS)
            gb_load(0)
            head_slab(0, 2)
            head_slab(0, 3)

            def body(h):
                wait(sp, sdec_stored, h * 16)
                sd_load(h)
                for u in range(3):
                    head_slab(h + 1, u)
                wait(sp, qg_ready, h + 1)
                gb_load(h + 1)
                head_slab(h + 1, 3)

            body(0)
            with sp.Fori(1, GH_N - 1) as h:
                body(h)
            sp.wait_ge(sdec_stored, (GH_N - 1) * 16)
            sd_load(GH_N - 1)

            w_gup = io["w_gdn_up"][0].rearrange("(k p) c -> p k c", p=P)

            def upa_slab(j, u):
                src = w_in[:, :, bass.ds(j * P + c_ga, P)] if u == 0 else w_gup[:, :, bass.ds(j * P, P)]
                load_slab(W_UPA, 2 * j, u, src)

            def merged_store(j, i):
                sp.wait_ge(mg_ready, j + i + 1)
                sp.sem_inc(sp_step, 1)
                sp.dma_start(d_mg[bass.ds(j + i, 1)].rearrange("o p t -> p (o t)"), mgst[i]).then_inc(mg_stored[i], 16)

            upa_slab(0, 0)
            upa_slab(0, 1)
            sp.drain().then_inc(phase_done, 1)
            sp.wait_ge(phase_done, 10)
            for u in range(2):
                upa_slab(1, u)
            with sp.Fori(0, KT // 2 - 1) as pair:
                j = pair * 2
                for i in range(2):
                    for u in range(2):
                        upa_slab(j + (2 + i), u)
                    merged_store(j, i)
            for i in range(2):
                merged_store(KT - 2, i)

            def ssm_slab(g, u):
                col = [g * P + (c_xbc + SDI), g * P + (c_xbc + SDI + SG_N * P), g * 2 * P + c_xbc,
                       g * 2 * P + (c_xbc + P), g * 2 * P + c_z, g * 2 * P + (c_z + P)][u]
                load_slab(W_SSM, 6 * g, u, w_in[:, :, bass.ds(col, P)])

            def csb_load(g):
                for r in range(HPG):
                    sp.dma_start(csb[:, r * T:(r + 1) * T],
                                 d_rows[bass.ds(HPG * g + r, 1), :].rearrange("o t -> (o t)").partition_broadcast(P)
                                 ).then_inc(csb_loaded, 16)

            s_in = io["state_ssm"][0].rearrange("b (i r) p n -> (r p) i b n", r=2)

            def ssd_load(g):
                for q in range(2):
                    sp.dma_start(ssd[:, q * NB * P:(q + 1) * NB * P].rearrange("p (b n) -> p b n", b=NB),
                                 s_in[:, bass.ds(2 * g + q, 1)].rearrange("p o b n -> p (o b) n")
                                 ).then_inc(ssd_loaded, 16)

            ssm_slab(0, 0)
            ssm_slab(0, 1)
            sp.drain().then_inc(phase_done, 1)
            sp.wait_ge(phase_done, 15)
            for u in range(2, 6):
                ssm_slab(0, u)

            def body(g, more):
                wait(sp, bank_full[ssm_plan.bank("y3")], 0 if isinstance(g, int) and g == 0
                     else ssm_plan.after("y3", g - 1))
                csb_load(g)
                if more:
                    ssm_slab(g + 1, 0)
                    ssm_slab(g + 1, 1)
                wait(sp, ssd_stored, 32 * g)
                ssd_load(g)
                if more:
                    for u in range(2, 6):
                        ssm_slab(g + 1, u)

            body(0, True)
            with sp.Fori(1, SG_N - 1) as g:
                body(g, True)
            body(SG_N - 1, False)

            w_sup = io["w_ssm_up"][0].rearrange("(s k p) c -> s p k c", p=P, k=KT)

            def upb_slab(j, i, u):
                src = (w_in[:, :, bass.ds(j * P + (c_gb + i * P), P)] if u == 0
                       else w_sup[u - 1][:, :, bass.ds(j * P + i * P, P)])
                load_slab(W_UPB, 3 * j, 3 * i + u, src)

            upb_slab(0, 0, 0)
            upb_slab(0, 0, 1)
            sp.drain().then_inc(phase_done, 1)
            sp.wait_ge(phase_done, 20)
            sp.wait_ge(yb_stored, 32 * SG_N)
            for i in range(2):
                sp.dma_start(ybv[:, i * KT:(i + 1) * KT, :], d_yb[i * KT:(i + 1) * KT].rearrange("k p t -> p k t")
                             ).then_inc(yb_loaded[i], 16)
            for i in range(2):
                sp.wait_ge(mg_stored[i], 16 * KT // 2)
            upb_slab(0, 0, 2)
            sp.dma_start(mgv, d_mg.rearrange("k p t -> p k t")).then_inc(mg_loaded, 16)
            upb_slab(0, 1, 0)
            upb_slab(0, 1, 1)
            sp.dma_start(x1v, d_xT.rearrange("k p t -> p k t")).then_inc(x1_loaded, 16)
            upb_slab(0, 1, 2)
            with sp.Fori(1, KT // 2) as pair:
                j = pair * 2
                for i in range(2):
                    for u in range(3):
                        upb_slab(j, i, u)
            def square_slabs(base, w):
                wv = w.rearrange("(k p) c -> p k c", p=P)
                with sp.Fori(0, wv.shape[2] // P // 2) as pair:
                    j = pair * 2
                    for i in range(2):
                        load_slab(base, j, i, wv[:, :, bass.ds(j * P + i * P, P)])

            sp.wait_ge(sum_taken, V_OUT)
            sp.dma_start(memtok, mem_prompt[0].rearrange("(t p) c -> p t c", p=P)).then_inc(mem_loaded, 16)
            square_slabs(W_OUT, io["w_out"][0])
            sp.drain().then_inc(phase_done, 1)

            square_slabs(W_MK, io["w_mk"][0])
            square_slabs(W_MV, io["w_mv"][0])
            sp.wait_ge(sum_taken, V_MK + KT)
            sp.dma_start(io["p_mem_k"][0, 0].rearrange("(t p) h d -> p t (h d)", p=P), Ktok).then_inc(mem_stored, 16)
            def split_slab(base, it, k, src):
                n = base - W_SPLIT + k
                if isinstance(it, int) and it + n < 2:
                    sp.wait_ge(proj_full, 3 * (it + base + k - 1))
                else:
                    sp.wait_ge(w_split, it + (n - 1))
                if not isinstance(it, int):
                    sp.sem_inc(sp_step, 1)
                sp.dma_start(slabv[k % 2], src).then_inc(slab_loaded[k % 2], 16)

            def split_slabs(base, w, first=0):
                wv = w.rearrange("(k p) c -> p k c", p=P)
                for pair0 in range(first, 1):
                    for i in range(2):
                        split_slab(base, 2 * pair0, i, wv[:, :, i * P:(i + 1) * P])
                with sp.Fori(1, KT // 2) as pair:
                    j = pair * 2
                    for i in range(2):
                        split_slab(base, j, i, wv[:, :, bass.ds(j * P + i * P, P)])

            split_slabs(W_CQ, io["w_cq"][0])
            sp.wait_ge(proj_taken, A_CQ)
            sp.dma_start(io["p_mem_v"][0, 0].rearrange("(t p) h d -> p t (h d)", p=P), Vtok).then_inc(mem_stored, 16)
            w_co = io["w_co"][0].rearrange("(k p) c -> p k c", p=P)
            for i in range(2):
                split_slab(W_CO, 0, i, w_co[:, :, i * P:(i + 1) * P])
            with sp.Fori(0, XH_N - 1) as h:
                for s in range(2):
                    for name, slot, loaded in (("cache_mem_k", kc[s], kc_loaded[s]), ("cache_mem_v", vc[s], vc_loaded[s])):
                        if slot is kc[s]:
                            sp.wait_ge(s8_ready, 2 * h + s + 1)
                        else:
                            sp.wait_ge(bank_full[attn_plan.bank(f"os{s}")], attn_plan.after(f"os{s}", h))
                        sp.sem_inc(sp_step, 1)
                        sp.dma_start(slot, io[name][0, bass.ds(h * 2 + (s + 2), 1)].rearrange(
                            "b (t p) h d -> p (b t) (h d)", p=P)).then_inc(loaded, 16)
            split_slabs(W_CO, io["w_co"][0], first=1)

            for q in range(FQ_N):
                part_ = slice(q * KT * P, (q + 1) * KT * P)
                split_slabs(W_FU + 2 * KT * q, io["w_ff_up"][0][:, part_])
                if q == 0:
                    sp.dma_start(gfin, io["g_final"].partition_broadcast(P)).then_inc(gfin_loaded, 16)
                split_slabs(W_FU + 2 * KT * q + KT, io["w_ff_down"][0][part_, :])
            for c in range(NC + 1):
                sp.wait_ge(yt_ready, c + 1)
                if c < NC:
                    sp.dma_start(io["y_prompt"][0, c * P:(c + 1) * P, :], ytok[:, c, :]).then_inc(y_stored, 16)
                else:
                    sp.dma_start(io["y_sample"][:, 0, :], ytok[P - NB:P, c, :]).then_inc(y_stored, 16)
            sp.wait_ge(y_stored, 16 * (NC + 1))
            sp.wait_ge(mem_stored, 32)
            sp.wait_ge(copies_done, 32)

        @block.tensor
        def _(pe):
            def hand(plan, name, it, mms):
                b = plan.bank(name)
                wait(pe, bank_taken[b], plan.before(name, it))
                for mm in mms(psum[:, b, :]):
                    last = mm
                last.then_inc(bank_full[b], 1)

            def taken(plan, name, it=0):
                pe.wait_ge(bank_taken[plan.bank(name)], plan.after(name, it))

            def stats(sq, n, bank, col=0, k=KT):
                for c in range(NC + 1):
                    a, z = token_range(c)
                    for i in range(k):
                        yield pe.matmul(bank[:, col + c:col + c + 1], sq[i][:, a:z], ones[:, 0:1],
                                        start=(i == 0), stop=(i == k - 1))

            def across(bank, rn, cs, at=0):
                for c in cs:
                    if c < NC:
                        yield pe.matmul(bank[:, (c % 4) * P:(c % 4 + 1) * P], rn(c).broadcast_to([P, P]), ident[:, :],
                                        start=True, stop=True)
                    else:
                        yield pe.matmul(bank[:, at:at + NB], rn(c).broadcast_to([P, P]), ident[:, P - NB:P],
                                        start=True, stop=True)

            def project(it, base, m0, m1, before, act_in=None, join=()):
                for m in range(m0, m1):
                    u, n, k = m // (3 * KT), m // KT % 3, m % KT
                    if k == 0:
                        if n == 0:
                            pe.wait_ge(slab_loaded[(base + u) % 2], 8 * it + 16 * ((base + u) // 2 + 1))
                        if u not in join:
                            wait(pe, *before(u, n))
                    src = xnv if act_in is None else act_in[u]
                    mm = pe.matmul(psum[:, n, 0:GW], slabv[(base + u) % 2][:, k, :], src[:, k, n * GW:(n + 1) * GW],
                                   start=(k == 0 and u not in join), stop=(k == KT - 1 and u + 1 not in join))
                    if k == KT - 1:
                        mm.then_inc(proj_full, 1)

            def qkvg(h, m0, m1):
                project(4 * h, 0, m0, m1, lambda u, n: (proj_taken, 12 * h + 3 * u + n - 2))

            pe.wait_ge(ident_ready, 1)
            for t in range(9):
                if t % 3 == 0:
                    pe.wait_ge(x_loaded[t // 3], 16 * 3)
                rows = P if t < NC else NB
                for j in range(2):
                    hand(setup_plan, f"xt{t}_{j}", 0, lambda bk, t=t, j=j, rows=rows: (
                        pe.transpose(bk[:, i * P:i * P + rows], xload[0:rows, t, (4 * j + i) * P:(4 * j + i + 1) * P],
                                     ident[0:rows, 0:rows]) for i in range(4)))
            pe.wait_ge(consts_ready, 2)
            pe.wait_ge(params_loaded, 16 * 20)
            hand(setup_plan, "vt", 0, lambda bk: [pe.transpose(bk[:, 0:VT_N], vstage[0:VT_N, :], ident[0:VT_N, 0:VT_N])])
            for q in range(4):
                hand(setup_plan, f"ct{q}", 0, lambda bk, q=q: (
                    pe.transpose(bk[:, i * 29:(i + 1) * 29], cstage[0:29, (14 * q + i) * P:(14 * q + i + 1) * P],
                                 ident[0:29, 0:29]) for i in range(CT_N // 4)))
            pe.wait_ge(sq_ready, KT)
            hand(setup_plan, "st", 0, lambda bk: stats([xnv[:, k, :] for k in range(KT)], NT, bk))
            pe.wait_ge(rn_ready, 1)
            for j in range(3):
                hand(setup_plan, f"bc{j}", 0, lambda bk, j=j: across(
                    bk, lambda c: rnorm[:, c:c + 1], range(4 * j, min(4 * j + 4, NC + 1))))
            taken(setup_plan, "bc2")
            for n in range(3):
                hand(setup_plan, f"sc{n}", 0, lambda bk, n=n: (
                    pe.matmul(bk[0:72, 0:GW], wsc[:, k, :], xnv[:, k, n * GW:(n + 1) * GW],
                              start=(k == 0), stop=(k == KT - 1)) for k in range(KT)))
            qkvg(0, 0, 24)
            pe.wait_ge(raw72_done, 1)
            for j in range(2):
                hand(setup_plan, f"ta{j}", 0, lambda bk, j=j: (
                    pe.transpose(bk[:, i * 72:(i + 1) * 72], rows72[0:72, (4 * j + i) * P:(4 * j + i + 1) * P],
                                 ident[0:72, 0:72]) for i in range(4)))
            hand(setup_plan, "td", 0, lambda bk: (
                pe.transpose(bk[:, c * 32:(c + 1) * 32], sp_t[0:32, c * P:(c + 1) * P], ident[0:32, 0:32])
                for c in range(NC)))
            taken(setup_plan, "ta0")
            taken(setup_plan, "ta1")
            hand(setup_plan, "cs", 0, lambda bk: [
                pe.matmul(bk[:, 0:40 * NC], triu[:, :], tok72[:, :, 0:40], start=True, stop=True)])
            hand(setup_plan, "tot", 0, lambda bk: [
                pe.matmul(bk[:, 0:40 * NC], ones[:, :], tok72[:, :, 0:40], start=True, stop=True)])
            for j in range(2):
                hand(setup_plan, f"csr{j}", 0, lambda bk, j=j: (
                    pe.matmul(bk[0:40, i * P:(i + 1) * P], tok72[:, 4 * j + i, 0:40], triu[:, :],
                              start=True, stop=True) for i in range(4)))
            pe.wait_ge(rx_ready, 1)
            hand(setup_plan, "dtx", 0, lambda bk: (
                pe.matmul(bk[:, i * 17:(i + 1) * 17], expand[0:SH_N, i * P:(i + 1) * P], rx[0:SH_N, :],
                          start=True, stop=True) for i in range(SH_N // 2)))
            pe.drain().then_inc(phase_done, 1)
            pe.wait_ge(phase_done, SETUP_ENDS)

            G = gdn_plan
            qkvg(0, 24, 96)

            def body(h, more):
                def fill(step, part=None):
                    if more:
                        a, z = fills(step)
                        if part is not None:
                            mid = (a + z) // 2
                            a, z = ((a, mid), (mid, z))[part]
                        qkvg(h + 1, a, z)

                pe.wait_ge(proj_taken, 12 * h + 12)
                hand(G, "rw", h, lambda bk: (
                    pe.transpose(bk[0:11, u * P:(u + 1) * P], raw[u][:, T:T + 11], ident[:, :]) for u in range(3)))
                fill("rw")
                pe.wait_ge(sq_ready, KT + 3 * h + 2)
                hand(G, "st", h, lambda bk: [m for i, s in enumerate((sq2, oT)) for m in stats([s], NT, bk, 9 * i, 1)])
                pe.wait_ge(rn_ready, 2 * h + 2)
                for i, t in enumerate("qk"):
                    for j in range(2):
                        hand(G, f"b{t}{j}", h, lambda bk, i=i, j=j: across(
                            bk, lambda c: rn2[:, 9 * i + c:9 * i + c + 1], range(4 * j, 4 * j + 4)))
                hand(G, "b8", h, lambda bk: [m for i in range(2) for m in across(
                    bk, lambda c: rn2[:, 9 * i + c:9 * i + c + 1], [NC], at=NB * i)])
                fill("norm")
                pe.wait_ge(qkv_ready, 3 * h + 3)
                for j in range(2):
                    hand(G, f"tv{j}", h, lambda bk, j=j: (
                        pe.transpose(cols(bk, i), cols(conv[2], 4 * j + i), ident[:, :]) for i in range(4)))
                taken(G, "b8", h)
                for j in range(2):
                    hand(G, f"tk{j}", h, lambda bk, j=j: (
                        pe.transpose(cols(bk, i), cols(kn, 4 * j + i), ident[:, :]) for i in range(4)))
                hand(G, "t8", h, lambda bk: [pe.transpose(bk[0:NB, 0:P], kn[:, T:NT], ident[:, :])])
                fill("turn")
                for name, rhs in (("kk", kn), ("qk", qn)):
                    for j in range(2):
                        hand(G, f"{name}{j}", h, lambda bk, j=j, rhs=rhs: (
                            pe.matmul(cols(bk, i), cols(kn, 4 * j + i), cols(rhs, 4 * j + i), start=True, stop=True)
                            for i in range(4)))
                fill("kkqk")
                pe.wait_ge(am_ready, 7 * h + 1)
                for j in range(2):
                    hand(G, f"y{j}", h, lambda bk, j=j: (
                        pe.transpose(cols(bk, i), cols(aml[0], 4 * j + i), ident[:, :]) for i in range(4)))
                for L in range(1, 7):
                    pe.wait_ge(am_ready, 7 * h + L + 1)
                    for j in range(2):
                        taken(G, f"y{j}" if L == 1 else f"yp{L - 1}_{j}", h)
                        hand(G, f"p{L}_{j}", h, lambda bk, j=j, L=L: (
                            pe.matmul(cols(bk, i), cols(aml[L % 2], 4 * j + i), cols(Y, 4 * j + i),
                                      start=True, stop=True) for i in range(4)))
                    fill(f"level{L}")
                    for j in range(2):
                        taken(G, f"p{L}_{j}", h)
                        if L > 1:
                            taken(G, f"xp{L - 1}_{j}", h)
                        hand(G, f"yp{L}_{j}", h, lambda bk, j=j: (
                            pe.matmul(cols(bk, i), cols(X, 4 * j + i), cols(Pp, 4 * j + i),
                                      start=True, stop=True) for i in range(4)))
                        if L < 6:
                            hand(G, f"xp{L}_{j}", h, lambda bk, j=j: (
                                pe.matmul(cols(bk, i), cols(Pp, 4 * j + i), cols(X, 4 * j + i),
                                          start=True, stop=True) for i in range(4)))
                for j in range(2):
                    taken(G, f"yp6_{j}", h)
                    hand(G, f"w{j}", h, lambda bk, j=j: (
                        pe.matmul(cols(bk, i), cols(kbe, 4 * j + i), cols(Y, 4 * j + i), start=True, stop=True)
                        for i in range(4)))
                pe.wait_ge(qg_ready, h + 1)
                for c in range(NC):
                    j = c // 4

                    def new_values(bk, c=c):
                        yield pe.matmul(bk[:, 0:P], cols(Y, c), cols(vb, c), start=True, stop=(c == 0))
                        if c:
                            yield pe.matmul(bk[:, 0:P], cols(wtn, c), Sst[c % 2], start=False, stop=True)

                    if c % 4 == 0:
                        taken(G, f"w{j}", h)
                    if c:
                        taken(G, f"su{c - 1}", h)
                    hand(G, f"vn{c}", h, new_values)
                    fill(f"scan{c}", 0)
                    taken(G, f"vn{c}", h)
                    hand(G, f"su{c}", h, lambda bk, c=c: [
                        pe.matmul(bk[:, 0:P], cols(kd, c), vnew[c % 2], start=True, stop=True)])
                    if c % 4 == 0:
                        wait(pe, bank_taken[7], G.before(f"ot{j}", h))
                    out = psum[:, 7, (c % 4) * P:(c % 4 + 1) * P]
                    if c:
                        pe.matmul(out, Sst[c % 2], cols(qg, c), start=True, stop=False)
                    mm = pe.matmul(out, vnew[c % 2], cols(dec2, c), start=(c == 0), stop=True)
                    if c % 4 == 3:
                        mm.then_inc(bank_full[7], 1)
                    fill(f"scan{c}", 1)
                    if not more:
                        project(0, W_UPA, 3 * c, 3 * c + 3, lambda u, n: (proj_taken, A_UPA))
                pe.wait_ge(sd_ready, h + 1)
                sdv = sdec.rearrange("p (b e) -> p b e", b=NB)
                hand(G, "ks", h, lambda bk: (
                    pe.matmul(bk[:, b:b + 1], sdv[:, b, :], kn[:, T + b:T + b + 1], start=True, stop=True)
                    for b in range(NB)))
                taken(G, "ks", h)
                hand(G, "v8", h, lambda bk: [pe.transpose(bk[0:NB, 0:P], v8n, ident[:, :])])
                fill("decode")
                taken(G, "v8", h)
                for j in range(2):
                    hand(G, f"oo{j}", h, lambda bk, j=j: [
                        pe.matmul(bk[:, :], k8[0:NB, :], vbd[0:NB, j * 512:(j + 1) * 512], start=True, stop=True)])
                taken(G, "oo0", h)
                taken(G, "oo1", h)
                hand(G, "od", h, lambda bk: (
                    pe.matmul(bk[:, b:b + 1], sdv[:, b, :], qn[:, T + b:T + b + 1], start=True, stop=True)
                    for b in range(NB)))
                pe.wait_ge(sq_ready, KT + 3 * h + 3)
                hand(G, "nst", h, lambda bk: stats([sq2], NT, bk, 0, 1))
                pe.wait_ge(rn_ready, 2 * h + 3)
                for j, name in enumerate(("nb0", "nb1", "nb8")):
                    hand(G, name, h, lambda bk, j=j: across(
                        bk, lambda c: rn2[:, c:c + 1], range(4 * j, min(4 * j + 4, NC + 1))))

            body(0, True)
            with pe.Fori(1, GH_N - 1) as h:
                body(h, True)
            body(GH_N - 1, False)
            pe.wait_ge(oa_ready, GH_N)
            pe.drain().then_inc(phase_done, 1)
            pe.wait_ge(phase_done, 10)

            def up_a(j, first):
                project(2 * j, W_UPA, 24 if first else 0, 2 * 24, lambda u, n: (
                    (proj_taken, 3 * j + (A_UPA + n + 1)) if u else (sum_taken, 3 * j + (n - 2))), [xnv, oav])

            up_a(0, True)
            with pe.Fori(1, KT) as j:
                up_a(j, False)
            pe.drain().then_inc(phase_done, 1)
            pe.wait_ge(phase_done, 15)

            G = ssm_plan

            def bcxz(g, m0, m1):
                project(6 * g, W_SSM, m0, m1, lambda u, n: (proj_taken, 18 * g + (A_SSM + 3 * u + n - 2)))

            bcxz(0, 0, 144)
            bT, cT, xT0, xT1 = sconv

            def body(g, more):
                def fill(step):
                    if more:
                        bcxz(g + 1, *sfills(step))

                pe.wait_ge(proj_taken, 18 * g + (A_SSM + 18))
                hand(G, "rw", g, lambda bk: (
                    pe.transpose(bk[0:11, u * P:(u + 1) * P], sraw[u][:, T:T + 11], ident[:, :]) for u in range(4)))
                fill("rw")
                pe.wait_ge(sx_ready, 4 * g + 4)
                for j in range(2):
                    hand(G, f"tb{j}", g, lambda bk, j=j: (
                        pe.transpose(cols(bk, i), cols(bT, 4 * j + i), ident[:, :]) for i in range(4)))
                fill("tb")
                for j in range(4):
                    hand(G, f"tx{j}", g, lambda bk, j=j: (
                        pe.transpose(cols(bk, i), cols(sconv[2 + i % 2], 2 * j + i // 2), ident[:, :])
                        for i in range(4)))
                hand(G, "t8", g, lambda bk: (
                    pe.transpose(bk[0:NB, i * P:(i + 1) * P], sconv[i][:, T:NT], ident[:, :]) for i in range(2)))
                fill("tx")
                for j in range(2):
                    hand(G, f"cb{j}", g, lambda bk, j=j: (
                        pe.matmul(cols(bk, i), cols(bT, 4 * j + i), cols(cT, 4 * j + i), start=True, stop=True)
                        for i in range(4)))
                fill("cb")
                if not more:
                    project(0, W_UPB, 0, 24, lambda u, n: (proj_taken, A_UPB))
                taken(G, "tb1", g)
                taken(G, "tx3", g)
                pe.wait_ge(ml_ready, 4 * g + 4)
                pe.wait_ge(cd_ready, g + 1)
                for c in range(NC):
                    if c:
                        taken(G, f"su{c - 1}", g)
                    hand(G, f"su{c}", g, lambda bk, c=c: [
                        pe.matmul(bk[:, 0:2 * P], cols(btok, c), xdd[:, 2 * P * c:2 * P * (c + 1)],
                                  start=True, stop=True)])
                    name = f"y{c // 2}"
                    if c % 2 == 0:
                        wait(pe, bank_taken[G.bank(name)], G.before(name, g))
                    for r in range(HPG):
                        rows, col = slice(HD * (r % 2), HD * (r % 2 + 1)), (2 * (c % 2) + r // 2) * P
                        out = psum[rows, G.bank(name), col:col + P]
                        head = slice(r * HD, (r + 1) * HD)
                        mm = pe.matmul(out, xdt[:, 2 * P * c:2 * P * (c + 1)][:, head],
                                       cols(ml[:, r * T:(r + 1) * T], c), start=True, stop=(c == 0))
                        if c:
                            mm = pe.matmul(out, SST[c % 2][:, head], cols(csb[:, r * T:(r + 1) * T], c),
                                           start=False, stop=True)
                    if c % 2:
                        mm.then_inc(bank_full[G.bank(name)], 1)
                    fill(f"scan{c}")
                taken(G, "su7", g)
                hand(G, "fs", g, lambda bk: (
                    pe.transpose(bk[:, i * P:(i + 1) * P], cols(SST[0], i), ident[:, :]) for i in range(2)))
                fill("fs")
                for name, rhs in (("bb", bdg), ("cc", cdg)):
                    for j in range(2):
                        hand(G, f"{name}{j}", g, lambda bk, j=j, rhs=rhs: [
                            pe.matmul(bk[:, :], ones[0:NB, :], rhs[0:NB, j * 512:(j + 1) * 512],
                                      start=True, stop=True)])
                fill("decode")
                fill("norm")
                pe.wait_ge(sq_ready, 2 * g + (SQ_SSM + 2))
                hand(G, "nst", g, lambda bk: stats(ml_sq, NT, bk, 0, 2))
                pe.wait_ge(rn_ready, g + (RN_SSM + 1))
                for j, name in enumerate(("nb0", "nb1", "nb8")):
                    hand(G, name, g, lambda bk, j=j: across(
                        bk, lambda c: srn[:, c:c + 1], range(4 * j, min(4 * j + 4, NC + 1))))

            body(0, True)
            with pe.Fori(1, SG_N - 1) as g:
                body(g, True)
            body(SG_N - 1, False)
            pe.drain().then_inc(phase_done, 1)
            pe.wait_ge(phase_done, 20)


            def up_b(j, i, first):
                for u in range(1 if first else 0, 3):
                    if first:
                        pe.wait_ge(yb_loaded[u - 1], 16)
                    project(3 * j, W_UPB + 3 * i, 24 * u, 24 * (u + 1), lambda u, n: (
                        (proj_taken, 3 * j + (A_UPB + 3 * i + n + 1)) if u else
                        (sum_taken, 3 * j + (V_UPB + 3 * i + n - 2))),
                        [xnv, ybv[:, 0:KT, :], ybv[:, KT:2 * KT, :]], join=(2,))

            up_b(0, 0, True)
            up_b(0, 1, False)
            with pe.Fori(1, KT // 2) as pair:
                j = pair * 2
                up_b(j, 0, False)
                up_b(j, 1, False)
            pe.wait_ge(sum_taken, V_OUT)
            with pe.Fori(0, KT // 2) as pair:
                j = pair * 2
                project(j, W_OUT, 0, 48, lambda u, n: (sum_taken, 3 * j + (V_OUT + 3 * u + n - 2)), [mgv, mgv])
            pe.drain().then_inc(phase_done, 1)
            pe.wait_ge(phase_done, 25)

            G = mem_plan
            pe.wait_ge(mem_loaded, 16)
            for t in range(MT):
                for j in range(2):
                    hand(G, f"mt{t}{j}", 0, lambda bk, t=t, j=j: (
                        pe.transpose(cols(bk, i), memtok[:, t, (4 * j + i) * P:(4 * j + i + 1) * P], ident[:, :])
                        for i in range(4)))
            pe.wait_ge(sq_ready, SQ_X + KT)
            hand(G, "xst", 0, lambda bk: stats([xnv[:, k, :] for k in range(KT)], NT, bk))
            pe.wait_ge(sq_ready, SQ_X + KT + 1)
            hand(G, "mst", 0, lambda bk: (
                pe.matmul(bk[:, c:c + 1], memsqv[:, k, c * P:(c + 1) * P], ones[:, 0:1], start=(k == 0),
                          stop=(k == KT - 1)) for c in range(MT) for k in range(KT)))
            pe.wait_ge(rn_ready, RN_X + 1)
            hand(G, "mbc", 0, lambda bk: across(bk, lambda c: mrn[:, c:c + 1], range(MT)))
            taken(G, "mbc")

            def mem_rows(base, sem_, count):
                with pe.Fori(0, KT // 2) as pair:
                    j = pair * 2
                    for i in range(2):
                        pe.wait_ge(slab_loaded[(base + i) % 2], 8 * j + 16 * ((base + i) // 2 + 1))
                        pe.wait_ge(sem_, j + (count + i - 1))
                        for t in range(MT):
                            for k in range(KT):
                                mm = pe.matmul(psum[:, i, t * P:(t + 1) * P], mn[:, k, t * P:(t + 1) * P],
                                               slabv[(base + i) % 2][:, k, :], start=(k == 0), stop=(k == KT - 1))
                        mm.then_inc(proj_full, 3)

            mem_rows(W_MK, sum_taken, V_MK)
            pe.wait_ge(rn_ready, RN_X + 2)
            for j in range(3):
                hand(G, f"xb{j}", 0, lambda bk, j=j: across(
                    bk, lambda c: xrn[:, c:c + 1], range(4 * j, min(4 * j + 4, NC + 1))))
            pe.wait_ge(sum_taken, V_MK + KT)
            mem_rows(W_MV, proj_taken, A_MV)
            for q in range(4):
                hand(G, f"kt{q}", 0, lambda bk, q=q: (
                    pe.transpose(cols(bk, 2 * i + t), Ktok[:, t, (2 * q + i) * P:(2 * q + i + 1) * P], ident[:, :])
                    for i in range(2) for t in range(MT)))
            def project3(it, base, before, hi, lo, at_group=None, late=None):
                for u in range(2):
                    slot = (base + u) % 2
                    pe.wait_ge(w_split, it + (base - W_SPLIT + u + 1))
                    for n in range(3):
                        wait(pe, *before(u, n))
                        if at_group is not None and u == 0:
                            pe.wait_ge(*at_group(n))
                        for k in range(KT):
                            if late is not None and u == 0 and n == 0 and k == KT - 1:
                                pe.wait_ge(*late)
                            w_hi, w_lo = (rounded(w[slot][:, k * P:(k + 1) * P]) for w in (wh, wl))
                            x_hi, x_lo = (rounded(x[:, k, n * GW:(n + 1) * GW]) for x in (hi, lo))
                            out = psum[:, n, 0:GW]
                            pe.matmul(out, w_hi, x_hi, start=(k == 0), stop=False)
                            pe.matmul(out, w_hi, x_lo, start=False, stop=False)
                            mm = pe.matmul(out, w_lo, x_hi, start=False, stop=(k == KT - 1))
                        mm.then_inc(proj_full, 1)

            def project_all(base, before, hi, lo, at_group=None, late=None):
                project3(0, base, lambda u, n: before(0, u, n), hi, lo, at_group, late)
                with pe.Fori(1, KT // 2) as pair:
                    j = pair * 2
                    project3(j, base, lambda u, n: before(j, u, n), hi, lo)

            pe.wait_ge(proj_taken, A_CQ)
            project_all(W_CQ, lambda j, u, n: (proj_taken, 3 * j + (A_CQ + 3 * u + n - 2)), xBv, xlowv,
                        at_group=lambda n: (xs_ready, 2 * n + 2))
            pe.wait_ge(proj_taken, A_END)
            for j in range(2):
                hand(G, f"qt{j}", 0, lambda bk, j=j: (
                    pe.transpose(bk[0:NB, i * P:(i + 1) * P], qT[:, (4 * j + i) * NT + T:(4 * j + i + 1) * NT],
                                 ident[:, :]) for i in range(4)))
            G = attn_plan
            with pe.Fori(0, XH_N) as h:
                for s in range(2):
                    pe.wait_ge(q_ready, 2 * h + s + 1)
                    for i in range(2):
                        hand(G, f"sc{s}{i}", h, lambda bk, i=i, s=s: (
                            pe.matmul(bk[:, c * M_N:(c + 1) * M_N], qh[s][:, k, (2 * i + c) * P:(2 * i + c + 1) * P],
                                      KTm[:, bass.ds(h * 2 * M_N + k * M_N, M_N)], start=(k == 0), stop=(k == 1))
                            for c in range(2) for k in range(2)))
                    for i in range(2):
                        hand(G, f"qb{s}{i}", h, lambda bk, i=i, s=s: [
                            pe.matmul(bk, ones[0:NB, :], qm[s][0:NB, i * 512:(i + 1) * 512], start=True, stop=True)])
                for s in range(2):
                    pe.wait_ge(p_ready, 2 * h + s + 1)
                    for t in range(MT):
                        hand(G, f"pt{s}{t}", h, lambda bk, s=s, t=t: (
                            pe.transpose(cols(bk, c), pr[s][:, c, t * P:(t + 1) * P], ident[:, :]) for c in range(4)))
                    pe.wait_ge(s8_ready, 2 * h + s + 1)
                    hand(G, f"st{s}", h, lambda bk, s=s: (
                        pe.transpose(bk[0:XH_N, t * P:(t + 1) * P], s8[s][:, t, :], ident[:, :]) for t in range(MT)))
                    pe.wait_ge(vh_ready, h + 1)
                    taken(G, f"pt{s}0", h)
                    taken(G, f"pt{s}1", h)
                    for k in range(2):
                        hand(G, f"o{s}{k}", h, lambda bk, k=k: (
                            pe.matmul(bk, vh[:, t, k * P:(k + 1) * P], PT[:, t, :], start=(t == 0), stop=(t == MT - 1))
                            for t in range(MT)))
                    pe.wait_ge(p4_ready, 2 * h + s + 1)
                    hand(G, f"pb{s}", h, lambda bk, s=s: (
                        pe.matmul(bk[:, t * XH_N:(t + 1) * XH_N], e4[s][0:XH_N, t * P:(t + 1) * P],
                                  ident[0:XH_N, 0:XH_N], start=True, stop=True) for t in range(MT)))
                    taken(G, f"pb{s}", h)
                    pe.wait_ge(vc_loaded[s], 16 * h + 16)
                    hand(G, f"os{s}", h, lambda bk, s=s: (
                        pe.matmul(bk[:, k:k + 1], vc[s][:, t, k * P:(k + 1) * P],
                                  pT8[s][:, t * XH_N + k // 2:t * XH_N + k // 2 + 1], start=(t == 0), stop=(t == MT - 1))
                        for k in range(KT) for t in range(MT)))
            taken(G, "os1", XH_N - 1)
            project_all(W_CO, lambda j, u, n: (sum_taken, 3 * j + (V_CO + 3 * u + n - 2)), atBv, atv)

            G = ff_plan
            pe.wait_ge(sq_ready, SQ_X + 2 * KT + 1)
            hand(G, "fst", 0, lambda bk: stats([xnv[:, k, :] for k in range(KT)], NT, bk))
            pe.wait_ge(rn_ready, RN_X + 3)
            for j in range(3):
                hand(G, f"fb{j}", 0, lambda bk, j=j: across(
                    bk, lambda c: xrn[:, c:c + 1], range(4 * j, min(4 * j + 4, NC + 1))))
            for q in range(FQ_N):
                base, v0 = W_FU + 2 * KT * q, V_FU + V_Q * q
                project_all(base, lambda j, u, n: (sum_taken, 3 * j + (v0 + 3 * u + n - 2)), xBv, xlowv,
                            at_group=(lambda n: (xs_ready, 6 + 2 * n + 2)) if q == 0 else None)
                pe.wait_ge(h_ready, KT * q + KT - 1)
                project_all(base + KT, lambda j, u, n: (sum_taken, 3 * j + (v0 + 3 * KT + 3 * u + n - 2)), hBv, hlowv,
                            late=(h_ready, KT * q + KT))
            pe.wait_ge(sq_ready, SQ_X + 3 * KT + 1)
            hand(G, "zst", 0, lambda bk: stats([xnv[:, k, :] for k in range(KT)], NT, bk))
            for c in range(NC + 1):
                a, z = token_range(c)
                for j in range(2):
                    hand(G, f"y{c}_{j}", 0, lambda bk, j=j, a=a, z=z: (
                        pe.transpose(cols(bk, i), x1v[:, 4 * j + i, a:z], ident[:, :]) for i in range(4)))

        @block.scalar
        def _(act):
            lane = Lane(act, act_step)

            def got(plan, name, it=0):
                b = plan.bank(name)
                act.wait_ge(bank_full[b], plan.after(name, it))
                return psum[:, b, :]

            def move(plan, name, it, dst, src, func=ACT.Copy, **kw):
                act.activation(dst, src(got(plan, name, it)), func, **kw).then_inc(bank_taken[plan.bank(name)], 1)

            S0 = setup_plan
            for t in range(9):
                n = P if t < NC else NB
                for j in range(2):
                    move(S0, f"xt{t}_{j}", 0, xT[:, 4 * j:4 * j + 4, t * P:t * P + n],
                         lambda bk, n=n: bk.rearrange("p (k i) -> p k i", k=4)[:, :, 0:n])
            move(S0, "vt", 0, vt[:, :], lambda bk: bk[:, 0:VT_N])
            for q in range(4):
                move(S0, f"ct{q}", 0, ct[:, q * 14 * 29:(q + 1) * 14 * 29], lambda bk: bk[:, 0:14 * 29])
            act.wait_ge(bank_taken[S0.bank("ct3")], S0.after("ct3"))
            for k in range(KT):
                act.activation(xnv[:, k, :], xT[:, k, :], ACT.Square).then_inc(sq_ready, 1)
            act.wait_ge(consts_ready, 2)
            move(S0, "st", 0, stat, lambda bk: bk[:, 0:9], ACT.Sqrt, scale=1.0 / D, bias=eps[:, :])
            for n in range(3):
                move(S0, f"sc{n}", 0, raw72[0:72, n * GW:(n + 1) * GW], lambda bk: bk[0:72, 0:GW])
            act.wait_ge(bank_taken[S0.bank("sc2")], S0.after("sc2"))
            act.wait_ge(params_loaded, 16 * 20)
            act.activation(hb[0:40, 1:2], hb[0:40, 1:2], ACT.Exp).then_inc(act_to_dve, 1)
            act.activation(rows72[64:72, :], raw72[64:72, :], ACT.Exp, scale=-1.0).then_inc(act_to_dve, 1)
            act.wait_ge(dve_to_act, 1)
            act.activation(t_e[0:40, :], t_e[0:40, :], ACT.Exp).then_inc(act_to_dve, 1)
            act.wait_ge(dve_to_act, 2)
            act.activation(t_l[0:40, :], t_u[0:40, :], ACT.Ln).then_inc(act_to_dve, 1)
            for j in range(2):
                move(S0, f"ta{j}", 0, tok72[:, 4 * j:4 * j + 4, :],
                     lambda bk: bk[:, 0:288].rearrange("p (c h) -> p c h", c=4))
            move(S0, "td", 0, tokd, lambda bk: bk[:, 0:256].rearrange("p (c h) -> p c h", c=NC))
            move(S0, "cs", 0, cst, lambda bk: bk[:, 0:320].rearrange("p (c h) -> p c h", c=NC))
            for j in range(2):
                move(S0, f"csr{j}", 0, csr_full[0:40, j * 512:(j + 1) * 512], lambda bk: bk[0:40, :])
            act.wait_ge(bank_taken[S0.bank("csr1")], S0.after("csr1"))
            act.activation(egc, cst[:, :, 32:40], ACT.Exp).then_inc(rows_ready, 1)
            act.wait_ge(dve_to_act, 3)
            act.activation(tote, tote, ACT.Exp)
            act.activation(dout, dout, ACT.Exp).then_inc(tab_exp, 1)
            dtxv = dtx[:, :].rearrange("p (i c) -> p i c", c=17)
            move(S0, "dtx", 0, dtxv, lambda bk: bk[:, 0:SH_N // 2 * 17].rearrange("p (i c) -> p i c", c=17))
            act.wait_ge(bank_taken[S0.bank("dtx")], S0.after("dtx"))
            act.activation(dtxv[:, :, 8:16], dtxv[:, :, 8:16], ACT.Exp)
            act.wait_ge(params_loaded, 16 * 22)
            act.activation(gb8[:, :], gb8[:, :], ACT.Exp)
            act.drain().then_inc(phase_done, 1)
            act.wait_ge(phase_done, SETUP_ENDS)

            G = gdn_plan

            def evacuate(h, a, z):
                for g in range(a, z):
                    u, n = g // 3, g % 3
                    act.wait_ge(proj_full, 12 * h + g + 1)
                    if u < 3:
                        if n == 0:
                            wait(act, conv_done, 3 * (h - 1) + u + 1)
                        act.activation(raw[u][:, 3 + n * GW:3 + (n + 1) * GW], psum[:, n, 0:GW], ACT.Copy
                                       ).then_inc(proj_taken, 1)
                    else:
                        if n == 0:
                            wait(act, gate_ready, h)
                        act.activation(ggr[:, n * GW:(n + 1) * GW], psum[:, n, 0:GW], ACT.Copy, scale=0.5
                                       ).then_inc(proj_taken, 1)

            def tanh_conv(h, u):
                act.wait_ge(conv_done, 3 * h + u + 1)
                wait(act, tanh_used, 4 * h + u - 1)
                act.activation(tnh[u % 2], conv[u], ACT.Tanh).then_inc(tanh_ready, 1)

            def tanh_gate(h):
                act.wait_ge(proj_taken, 12 * h + 12)
                act.wait_ge(tanh_used, 4 * h + 2)
                act.activation(tnh[1], ggr, ACT.Tanh).then_inc(tanh_ready, 1)

            evacuate(0, 0, 12)
            for u in range(3):
                tanh_conv(0, u)

            def stores(h):
                act.wait_ge(bank_taken[G.bank("su7")], G.after("su7", h))
                act.dma_start(io["p_gdn"][0, 0, bass.ds(h, 1)].rearrange("o k e -> k (o e)"), Sst[0]
                              ).then_inc(S_stored, 16)
                act.wait_ge(bank_taken[G.bank("oo1")], G.after("oo1", h))
                act.dma_start(io["s_gdn"][0, :, bass.ds(h, 1)].rearrange("b o k e -> k (b o) e"),
                              sdec.rearrange("p (b e) -> p b e", b=NB)).then_inc(sdec_stored, 16)

            def body(h, first, more):
                def evac(step):
                    if more:
                        a, z = fills(step)
                        evacuate(h + 1, a // 8, z // 8)

                if not first:
                    stores(h - 1)
                wait(act, rw_stored, 32 * h)
                move(G, "rw", h, rwst[0:11, :], lambda bk: bk[0:11, 0:3 * P])
                act.wait_ge(bank_taken[G.bank("rw")], G.after("rw", h))
                pc = io["p_gdn_conv"][0, 0].rearrange("r (u x) -> r u x", u=3)[:, :, bass.ds(h * P, P)]
                sc = io["s_gdn_conv"][0, :, CW - 2, :].rearrange("b (u x) -> b u x", u=3)[:, :, bass.ds(h * P, P)]
                act.dma_start(pc, rwst[0:3, :].rearrange("r (u x) -> r u x", u=3)).then_inc(rw_stored, 16)
                act.dma_start(sc, rwst[3:11, :].rearrange("r (u x) -> r u x", u=3)).then_inc(rw_stored, 16)
                act.wait_ge(qkv_ready, 3 * h + 2)
                wait(act, oa_ready, h)
                act.activation(sq2, conv[0], ACT.Square).then_inc(sq_ready, 1)
                act.activation(oT, conv[1], ACT.Square).then_inc(sq_ready, 1)
                tanh_gate(h)
                evac("rw")
                move(G, "st", h, st2, lambda bk: bk[:, 0:18], ACT.Sqrt, bias=eps[:, :])
                act.wait_ge(dec_diff, h + 1)
                act.activation(dec1, dec1, ACT.Exp, scale=-1.0).then_inc(dec_exp, 1)
                act.activation(dec2, dec2, ACT.Exp).then_inc(dec_exp, 1)
                act.activation(gbr, gbr, ACT.Exp).then_inc(eg_ready, 1)
                evac("norm")
                evac("turn")
                evac("kkqk")
                for L in range(1, 7):
                    for j in range(2):
                        move(G, f"p{L}_{j}", h, half(Pp, j), lambda bk: bk.rearrange("p (c i) -> p c i", c=4))
                    evac(f"level{L}")
                for j in range(2):
                    bk = got(G, f"w{j}", h)
                    act.mul(half(wtn, j), bk.rearrange("p (c i) -> p c i", c=4), -1.0
                            ).then_inc(bank_taken[G.bank(f"w{j}")], 1)
                for c in range(NC):
                    move(G, f"vn{c}", h, vnew[c % 2], lambda bk: bk[:, 0:P])
                    if c % 4 == 3:
                        move(G, f"ot{c // 4}", h, oT[:, (c - 3) * P:(c + 1) * P], lambda bk: bk[:, :])
                    evac(f"scan{c}")
                    if more and c in (1, 4, 7):
                        tanh_conv(h + 1, c // 3)
                evac("decode")
                move(G, "od", h, oT[:, T:NT], lambda bk: bk[:, 0:NB])
                act.wait_ge(bank_taken[G.bank("od")], G.after("od", h))
                act.activation(sq2, oT, ACT.Square).then_inc(sq_ready, 1)
                move(G, "nst", h, st2[:, 0:9], lambda bk: bk[:, 0:9], ACT.Sqrt, scale=1.0 / P, bias=eps[:, :])

            body(0, True, True)
            with act.Fori(1, GH_N - 1) as h:
                body(h, False, True)
            body(GH_N - 1, False, False)
            stores(GH_N - 1)
            act.wait_ge(S_stored, 16 * GH_N)
            act.wait_ge(sdec_stored, 16 * GH_N)
            act.wait_ge(rw_stored, 32 * GH_N)
            act.drain().then_inc(phase_done, 1)
            act.wait_ge(phase_done, 10)

            def merge_gate(it, slab0, taken0, j, tg, free):
                wait(act, *free)
                for n in range(3):
                    act.wait_ge(proj_full, it[0] + (3 * slab0 + n + 1))
                    act.activation(tg[:, n * GW:(n + 1) * GW], psum[:, n, 0:GW], ACT.Tanh, scale=0.5
                                   ).then_inc(proj_taken, 1)

            for j0 in range(2):
                merge_gate((6 * j0,), W_UPA, 0, j0, tgate[j0], (mg_ready, 0))
            with act.Fori(1, KT // 2) as pair:
                j = pair * 2
                for i in range(2):
                    merge_gate((6 * j,), W_UPA + 2 * i, 0, j, tgate[i], (mg_ready, j + (i - 1)))
            act.drain().then_inc(phase_done, 1)
            act.wait_ge(phase_done, 15)

            G = ssm_plan

            def evacuate(g, a, z):
                for m in range(a, z):
                    u, n = m // 3, m % 3
                    act.wait_ge(proj_full, 18 * g + (3 * W_SSM + m + 1))
                    if n == 0 and u < 4:
                        wait(act, sconv_done, 4 * (g - 1) + u + 1)
                    elif n == 0:
                        wait(act, z_ready, 2 * (g - 1) + (u - 4) + 1)
                    if u < 4:
                        act.activation(sraw[u][:, 3 + n * GW:3 + (n + 1) * GW], psum[:, n, 0:GW], ACT.Copy
                                       ).then_inc(proj_taken, 1)
                    else:
                        act.activation(zraw[u - 4][:, n * GW:(n + 1) * GW], psum[:, n, 0:GW], ACT.Copy, scale=0.5
                                       ).then_inc(proj_taken, 1)

            def stanh(g, u):
                if u < 4:
                    act.wait_ge(sconv_done, 4 * g + u + 1)
                else:
                    act.wait_ge(proj_taken, 18 * g + (A_SSM + 3 * u + 3))
                wait(act, stanh_used, 6 * g + u - 1)
                act.activation(stnh[u % 2], sconv[u] if u < 4 else zraw[u - 4], ACT.Tanh).then_inc(stanh_ready, 1)

            evacuate(0, 0, 18)
            for u in range(4):
                stanh(0, u)
            s_out = io["s_ssm"][0].rearrange("b (i r) p n -> (r p) i b n", r=2)
            p_out = io["p_ssm"][0, 0].rearrange("(i r) p n -> (r p) i n", r=2)

            def stores(g):
                act.wait_ge(y_ready, 2 * g + 2)
                for q in range(2):
                    act.dma_start(s_out[:, bass.ds(2 * g + q, 1)].rearrange("p o b n -> p (o b) n"),
                                  ssd[:, q * NB * P:(q + 1) * NB * P].rearrange("p (b n) -> p b n", b=NB)
                                  ).then_inc(ssd_stored, 16)
                act.wait_ge(yb_ready, g + 1)
                for q in range(2):
                    act.dma_start(d_yb[bass.ds(2 * g + q, 1)].rearrange("o p t -> p (o t)"), yT[q]
                                  ).then_inc(yb_stored, 16)

            def body(g, first, more):
                def evac(step):
                    if more:
                        a, z = sfills(step)
                        evacuate(g + 1, a // 8, z // 8)

                if not first:
                    stores(g - 1)
                wait(act, srw_stored, 96 * g)
                move(G, "rw", g, srw[0:11, :], lambda bk: bk[0:11, :])
                act.wait_ge(bank_taken[G.bank("rw")], G.after("rw", g))
                pc, sc = io["p_ssm_conv"][0, 0], io["s_ssm_conv"][0, :, CW - 2, :]
                for a, n, col in ((0, P, SDI), (P, P, SDI + SG_N * P), (2 * P, 2 * P, 0)):
                    dst = bass.ds(g * n + col, n)
                    act.dma_start(pc[:, dst], srw[0:3, a:a + n]).then_inc(srw_stored, 16)
                    act.dma_start(sc[:, dst], srw[3:11, a:a + n]).then_inc(srw_stored, 16)
                for u in (4, 5):
                    stanh(g, u)
                evac("rw")
                for j in range(2):
                    move(G, f"tb{j}", g, half(btok, j), lambda bk: bk.rearrange("p (c i) -> p c i", c=4))
                evac("tb")
                for r in range(HPG):
                    act.wait_ge(sdiff, 4 * g + r + 1)
                    act.activation(ml[:, r * T:(r + 1) * T], ml[:, r * T:(r + 1) * T], ACT.Exp).then_inc(sdec_exp, 1)
                    act.activation(csb[:, r * T:(r + 1) * T], csb[:, r * T:(r + 1) * T], ACT.Exp
                                   ).then_inc(ecs_ready, 1)
                evac("tx")
                evac("cb")
                for c in range(NC):
                    evac(f"scan{c}")
                    if more and c in (1, 3, 6):
                        stanh(g + 1, c // 2 if c < 6 else 2)
                wait(act, stf_stored, 32 * g)
                move(G, "fs", g, stf, lambda bk: bk[:, 0:2 * P])
                act.wait_ge(bank_taken[G.bank("fs")], G.after("fs", g))
                for q in range(2):
                    act.dma_start(p_out[:, bass.ds(2 * g + q, 1)].rearrange("p o n -> p (o n)"), cols(stf, q)
                                  ).then_inc(stf_stored, 16)
                evac("fs")
                if more:
                    stanh(g + 1, 3)
                evac("decode")
                for q in range(2):
                    act.wait_ge(y_ready, 2 * g + q + 1)
                    act.activation(ml_sq[q], yT[q], ACT.Square).then_inc(sq_ready, 1)
                move(G, "nst", g, ssq, lambda bk: bk[:, 0:9], ACT.Sqrt, scale=1.0 / (2 * P), bias=eps[:, :])
                evac("norm")

            body(0, True, True)
            with act.Fori(1, SG_N - 1) as g:
                body(g, False, True)
            body(SG_N - 1, False, False)
            stores(SG_N - 1)
            for s_ in (ssd_stored, stf_stored, yb_stored):
                act.wait_ge(s_, 32 * SG_N)
            act.wait_ge(srw_stored, 96 * SG_N)
            act.drain().then_inc(phase_done, 1)
            act.wait_ge(phase_done, 20)

            for i in range(2):
                merge_gate((0,), W_UPB + 3 * i, 0, 0, tgate2[i], (mg_ready, 0))
            with act.Fori(1, KT // 2) as pair:
                j = pair * 2
                for i in range(2):
                    merge_gate((9 * j,), W_UPB + 3 * i, 0, j, tgate2[i], (sum_taken, 3 * j + (V_UPB + 3 * (i - 1))))
            for k in range(KT):
                act.wait_ge(sum_taken, V_OUT + 3 * (k + 1))
                act.activation(xnv[:, k, :], x1v[:, k, :], ACT.Square).then_inc(sq_ready, 1)
            act.drain().then_inc(phase_done, 1)
            act.wait_ge(phase_done, 25)

            G = mem_plan
            for t in range(MT):
                for j in range(2):
                    move(G, f"mt{t}{j}", 0, memTv[:, 4 * j:4 * j + 4, t * P:(t + 1) * P],
                         lambda bk: bk.rearrange("p (k i) -> p k i", k=4))
            for name in ("mt00", "mt01", "mt10", "mt11"):
                act.wait_ge(bank_taken[G.bank(name)], G.after(name))
            act.activation(memsq, memT, ACT.Square).then_inc(sq_ready, 1)
            move(G, "xst", 0, xstat, lambda bk: bk[:, 0:9], ACT.Sqrt, scale=1.0 / D, bias=eps[:, :])
            move(G, "mst", 0, mstat, lambda bk: bk[:, 0:MT], ACT.Sqrt, scale=1.0 / D, bias=eps[:, :])
            act.wait_ge(bank_taken[G.bank("mbc")], G.after("mbc"))
            for b in range(2):
                act.dma_start(kc[b], io["cache_mem_k"][0, b].rearrange("(t p) h d -> p t (h d)", p=P)
                              ).then_inc(kc_loaded[b], 16)
                act.dma_start(vc[b], io["cache_mem_v"][0, b].rearrange("(t p) h d -> p t (h d)", p=P)
                              ).then_inc(vc_loaded[b], 16)
            with act.Fori(0, KT // 2) as pair:
                j = pair * 2
                for i in range(2):
                    act.wait_ge(proj_full, 3 * j + 3 * (W_MV + i + 1))
                    act.activation(Vtok[:, :, bass.ds(j * P + i * P, P)],
                                   psum[:, i, 0:MT * P].rearrange("p (t c) -> p t c", t=MT), ACT.Copy
                                   ).then_inc(proj_taken, 1)
            for q in range(4):
                move(G, f"kt{q}", 0, KTm[:, q * 512:(q + 1) * 512], lambda bk: bk)
            act.wait_ge(mem_stored, 16)
            with act.Fori(0, KT // 2) as pair:
                j = pair * 2
                for i in range(2):
                    for n in range(3):
                        act.wait_ge(proj_full, 3 * j + (3 * (W_CQ + i) + n + 1))
                        act.activation(qT[:, bass.ds(j * NT + (i * NT + n * GW), GW)], psum[:, n, 0:GW], ACT.Copy
                                       ).then_inc(proj_taken, 1)
            for j in range(2):
                move(G, f"qt{j}", 0, qtok[0:NB, j * 512:(j + 1) * 512], lambda bk: bk[0:NB, :])
            G = attn_plan
            with act.Fori(0, XH_N) as h:
                for s in range(2):
                    act.wait_ge(mx_ready, 2 * h + s + 1)
                    for i in range(2):
                        bk = got(G, f"sc{s}{i}", h)
                        for c in range(2):
                            ins = act.activation(pr[s][:, 2 * i + c, :], bk[:, c * M_N:(c + 1) * M_N], ACT.Exp,
                                                 scale=x_scale, bias=nmx[s][:, 2 * i + c:2 * i + c + 1],
                                                 accum_out=psm[s][:, 2 * i + c:2 * i + c + 1])
                        ins.then_inc(bank_taken[G.bank(f"sc{s}{i}")], 1)
                    for i in range(2):
                        move(G, f"qb{s}{i}", h, qrep[s][:, i * 512:(i + 1) * 512], lambda bk: bk)
                for s in range(2):
                    for t in range(MT):
                        move(G, f"pt{s}{t}", h, PT[:, t, :], lambda bk: bk)
                    act.wait_ge(m4_ready, 2 * h + s + 1)
                    move(G, f"st{s}", h, e4[s][0:XH_N, :], lambda bk: bk[0:XH_N, 0:M_N], ACT.Exp,
                         scale=x_scale, bias=mx4[s][0:XH_N, :], accum_out=sm4[s][0:XH_N, :])
                    for k in range(2):
                        act.activation(rounded(atB[:, bass.ds(h * 2 * NT + (k * NT + s * 512), 512)]),
                                       got(G, f"o{s}{k}", h), ACT.Copy).then_inc(ohi_ready, 1)
                    move(G, f"pb{s}", h, pT8[s], lambda bk: bk[:, 0:MT * XH_N])

            G = ff_plan
            for k in range(KT):
                act.wait_ge(sum_taken, V_CO + 3 * (k + 1))
                act.activation(xnv[:, k, :], x1v[:, k, :], ACT.Square).then_inc(sq_ready, 1)
            move(G, "fst", 0, xstat, lambda bk: bk[:, 0:9], ACT.Sqrt, scale=1.0 / D, bias=eps[:, :])
            for q in range(FQ_N):
                with act.Fori(0, KT) as j:
                    for n in range(3):
                        act.wait_ge(proj_full, 3 * j + (3 * (W_FU + 2 * KT * q) + n + 1))
                        act.activation(hA[:, bass.ds(j * NT + n * GW, GW)], psum[:, n, 0:GW], ACT.Relu
                                       ).then_inc(proj_taken, 1)
                    act.wait_ge(sum_taken, 3 * j + (V_FU + V_Q * q + 3))
                    act.activation(rounded(hB[:, bass.ds(j * NT, NT)]), hA[:, bass.ds(j * NT, NT)], ACT.Copy
                                   ).then_inc(hr_ready, 1)
            for k in range(KT):
                act.wait_ge(sum_taken, V_FU + V_Q * FQ_N - 3 * KT + 3 * (k + 1))
                act.activation(xnv[:, k, :], x1v[:, k, :], ACT.Square).then_inc(sq_ready, 1)
            move(G, "zst", 0, xstat, lambda bk: bk[:, 0:9], ACT.Sqrt, scale=1.0 / D, bias=eps[:, :])

        @block.vector
        def _(dve):
            lane = Lane(dve, dve_step)

            def got(plan, name, it=0):
                b = plan.bank(name)
                dve.wait_ge(bank_full[b], plan.after(name, it))
                return psum[:, b, :]

            def give(plan, name, ins):
                ins.then_inc(bank_taken[plan.bank(name)], 1)

            def taken(plan, name, it=0):
                dve.wait_ge(bank_taken[plan.bank(name)], plan.after(name, it))

            def do(ins):
                lane.step(ins)
                lane.settle()

            def conv_step(y, x, col, i, bias, done):
                if i == 0:
                    do(dve.tensor_scalar(y, x[:, 3:3 + NT], col[:, 27:28], *(
                        (col[:, 28:29], ALU.mult, ALU.add) if bias else (None, ALU.mult))))
                    return
                i -= 1
                dve.scalar_tensor_tensor(out=y[:, 0:T], in0=x[:, i:i + T], scalar=col[:, 24 + i:25 + i],
                                         in1=y[:, 0:T], op0=ALU.mult, op1=ALU.add)
                ins = dve.scalar_tensor_tensor(out=y[:, T:NT], in0=col[:, i:24:3], scalar=col[:, 24 + i:25 + i],
                                               in1=y[:, T:NT], op0=ALU.mult, op1=ALU.add)
                if i < CW - 2:
                    do(ins)
                else:
                    ins.then_inc(done, 1)

            S0 = setup_plan
            taken(S0, "ct3")
            taken(S0, "ct2")
            taken(S0, "ct1")
            taken(S0, "ct0")
            taken(S0, "vt")
            do(dve.tensor_scalar(ctv[:, :, 24:29], ctv[:, :, 24:29], 0.5, None, ALU.mult))
            taken(S0, "st")
            dve.reciprocal(rnorm, stat).then_inc(rn_ready, 1)
            for j in range(3):
                bk = got(S0, f"bc{j}")
                a, z = j * 512, min((j + 1) * 512, NT)
                for k in range(KT):
                    ins = dve.scalar_tensor_tensor(out=xnv[:, k, a:z], in0=xT[:, k, a:z],
                                                   scalar=vt[:, v_mix + k:v_mix + k + 1],
                                                   in1=bk[:, 0:z - a], op0=ALU.mult, op1=ALU.mult)
                give(S0, f"bc{j}", ins)
            do(dve.memset(rows72[0:64, :], 0.0))
            taken(S0, "sc2")
            taken(S0, "sc1")
            taken(S0, "sc0")
            do(dve.tensor_scalar(t_c[0:40, :], raw72[0:40, :], hb[0:40, 0:1], None, ALU.add))
            dve.scalar_tensor_tensor(out=t_e[0:40, :], in0=t_c[0:40, :], scalar=-1.0, in1=t_c[0:40, :],
                                     op0=ALU.mult, op1=ALU.min).then_inc(dve_to_act, 1)
            dve.wait_ge(act_to_dve, 3)
            dve.tensor_scalar(t_u[0:40, :], t_e[0:40, :], 1.0, None, ALU.add).then_inc(dve_to_act, 1)
            dve.wait_ge(dve_to_act, 2)
            do(dve.scalar_tensor_tensor(out=t_e[0:40, :], in0=t_u[0:40, :], scalar=1.0, in1=t_e[0:40, :],
                                        op0=ALU.subtract, op1=ALU.subtract))
            do(dve.reciprocal(sp_t[0:40, :], t_u[0:40, :]))
            do(dve.tensor_tensor(t_e[0:40, :], t_e[0:40, :], sp_t[0:40, :], ALU.mult))
            dve.wait_ge(act_to_dve, 4)
            do(dve.scalar_tensor_tensor(out=sp_t[0:40, :], in0=t_c[0:40, :], scalar=0.0, in1=t_l[0:40, :],
                                        op0=ALU.max, op1=ALU.add))
            do(dve.tensor_tensor(sp_t[0:40, :], sp_t[0:40, :], t_e[0:40, :], ALU.subtract))
            do(dve.tensor_scalar(hb[0:40, 1:2], hb[0:40, 1:2], -1.0, None, ALU.mult))
            do(dve.tensor_scalar(rows72[0:40, :], sp_t[0:40, :], hb[0:40, 1:2], None, ALU.mult))
            dve.tensor_scalar(rows72[64:72, :], rows72[64:72, :], 1.0, None, ALU.add).then_inc(raw72_done, 1)
            do(dve.tensor_copy(rx[0:32, 0:8], sp_t[0:32, T:NT]))
            dve.tensor_copy(rx[0:32, 8:16], rows72[0:32, T:NT]).then_inc(rx_ready, 1)
            taken(S0, "cs")
            bk = got(S0, "tot")
            do(dve.tensor_copy(tote, bk[:, 0:320].rearrange("p (c h) -> p c h", c=NC)))
            give(S0, "tot", dve.tensor_tensor(dout, bk[:, 0:320].rearrange("p (c h) -> p c h", c=NC), cst,
                                              ALU.subtract))
            taken(S0, "tot")
            do(dve.memset(raw72[0:1, 0:1], 0.0))
            dve.sem_inc(dve_to_act, 1)
            dve.wait_ge(tab_exp, 1)
            ghv = gh[:, :].rearrange("p (h r c) -> p h r c", h=GH_N, r=5)

            def by_head(t, a, z):
                return t[:, :, a:z].rearrange("p c h -> p h c")

            do(dve.reciprocal(tok72[:, :, 64:72], tok72[:, :, 64:72]))
            do(dve.tensor_copy(ghv[:, :, 0, :], by_head(cst, 32, 40)))
            do(dve.tensor_copy(ghv[:, :, 1, :], by_head(tok72, 64, 72)))
            do(dve.tensor_tensor(ghv[:, :, 2, :], by_head(tok72, 64, 72), by_head(egc, 0, GH_N), ALU.mult))
            do(dve.tensor_copy(ghv[:, :, 3, :], by_head(dout, 32, 40)))
            do(dve.tensor_copy(ghv[:, :, 4, :], by_head(tote, 32, 40)))
            shv = sh[:, :].rearrange("p (g q c r) -> p g q c r", g=SG_N, q=4, c=NC)
            for g in range(SG_N):
                hr = slice(HPG * g, HPG * (g + 1))
                do(dve.tensor_copy(shv[:, g, 0], cst[:, :, hr]))
                do(dve.tensor_copy(shv[:, g, 1], tokd[:, :, hr]))
                do(dve.tensor_tensor(shv[:, g, 2], tokd[:, :, hr], dout[:, :, hr], ALU.mult))
                do(dve.tensor_copy(shv[:, g, 3], tote[:, :, hr]))
            dve.wait_ge(params_loaded, 16 * 22)
            dve.reciprocal(bb8[:, :], bb8[:, :])
            dve.drain().then_inc(phase_done, 1)
            dve.wait_ge(phase_done, SETUP_ENDS)

            G = gdn_plan
            for u in range(3):
                do(dve.memset(raw[u][:, 0:3], 0.0))
            ctg = ctv[:, 0:GT_N, :].rearrange("p (u h) r -> p u h r", u=3)

            def conv_columns(h):
                wait(dve, conv_done, 3 * h)
                dve.tensor_copy(cwf.unsqueeze(2), ctg[:, :, bass.ds(h, 1), :]).then_inc(cw_ready, 1)

            def convolve(h, u, i):
                if i == 0:
                    wait(dve, proj_taken, 12 * h + 3 * u + 3)
                conv_step(conv[u], raw[u], cwf[:, u, :], i, False, conv_done)

            def mix(h, u):
                dve.wait_ge(tanh_ready, 4 * h + u + 1)
                src, dst = (conv[u], conv[u]) if u < 3 else (ggr, ggs)
                out_ready, n = (qkv_ready, 3 * h + u + 1) if u < 3 else (gate_ready, h + 1)
                dve.scalar_tensor_tensor(out=dst, in0=tnh[u % 2 if u < 3 else 1], scalar=1.0, in1=src,
                                         op0=ALU.add, op1=ALU.mult).then_inc(out_ready, 1)
                dve.wait_ge(out_ready, n)
                dve.sem_inc(tanh_used, 1)

            conv_columns(0)
            dve.wait_ge(cw_ready, 1)
            for u in range(3):
                for i in range(CW):
                    convolve(0, u, i)
            for u in range(3):
                mix(0, u)
            BESIDE = {"level1": [(0, 0)], "level2": [(0, 1)], "level3": [(0, 2)], "level4": [(0, 3)],
                      "level5": [(1, 0)], "level6": [(1, 1)], "scan0": [(1, 2)], "scan1": [(1, 3)], "scan2": ["mix0"],
                      "scan4": [(2, 0)], "scan5": [(2, 1)], "scan6": [(2, 2)], "scan7": [(2, 3), "mix1"],
                      "decode": ["mix2"]}

            def body(h, more):
                def beside(step):
                    for m in BESIDE.get(step, ()) if more else ():
                        if isinstance(m, str):
                            mix(h + 1, int(m[-1]))
                        else:
                            if m == (0, 0):
                                dve.wait_ge(cw_ready, h + 2)
                            convolve(h + 1, *m)

                lane.restart()
                wait(dve, sd_ready, h)
                do(dve.tensor_copy(hs, gh[:, bass.ds(h * 5 * NC, 5 * NC)]))
                do(dve.tensor_copy(hs8[:, 0:NB], gb8[:, bass.ds(h * NB, NB)]))
                dve.tensor_copy(hs8[:, NB:2 * NB], bb8[:, bass.ds(h * NB, NB)]).then_inc(hs_ready, 1)
                if more:
                    conv_columns(h + 1)
                gc, beta, bege, dko, dch = (hs[:, i * NC:(i + 1) * NC] for i in range(5))
                dve.wait_ge(gbr_loaded, 16 * h + 16)
                for c in range(NC):
                    dve.tensor_scalar(cols(dec1, c), cols(gbr, c), gc[:, c:c + 1], 0.0, ALU.subtract, ALU.max)
                    ins = dve.tensor_scalar(cols(dec2, c), cols(gbr, c), gc[:, c:c + 1], 0.0, ALU.subtract, ALU.min)
                ins.then_inc(dec_diff, 1)
                taken(G, "st", h)
                dve.reciprocal(rn2, st2).then_inc(rn_ready, 1)
                mix(h, 3)
                for t, src, dst, f in (("q", conv[0], qn, float(P) ** -0.5), ("k", conv[1], kn, 1.0)):
                    for j in range(2):
                        bk = got(G, f"b{t}{j}", h)
                        give(G, f"b{t}{j}", dve.scalar_tensor_tensor(
                            out=dst[:, j * 512:(j + 1) * 512], in0=src[:, j * 512:(j + 1) * 512], scalar=f,
                            in1=bk[:, :], op0=ALU.mult, op1=ALU.mult))
                bk = got(G, "b8", h)
                dve.scalar_tensor_tensor(out=qn[:, T:NT], in0=conv[0][:, T:NT], scalar=float(P) ** -0.5,
                                         in1=bk[:, 0:NB], op0=ALU.mult, op1=ALU.mult)
                give(G, "b8", dve.tensor_tensor(kn[:, T:NT], conv[1][:, T:NT], bk[:, NB:2 * NB], ALU.mult))
                dve.wait_ge(qkv_ready, 3 * h + 3)
                dve.tensor_copy(vs8, conv[2][:, T:NT])
                for j in range(2):
                    bk = got(G, f"tv{j}", h).rearrange("p (c i) -> p c i", c=4)
                    give(G, f"tv{j}", dve.tensor_tensor(half(vb, j), bk, spread(beta[:, 4 * j:4 * j + 4]), ALU.mult))
                for j in range(2):
                    bk = got(G, f"tk{j}", h).rearrange("p (c i) -> p c i", c=4)
                    dve.tensor_tensor(half(kbe, j), bk, spread(bege[:, 4 * j:4 * j + 4]), ALU.mult)
                    give(G, f"tk{j}", dve.tensor_tensor(half(kd, j), bk, spread(dko[:, 4 * j:4 * j + 4]), ALU.mult))
                give(G, "t8", dve.tensor_copy(k8[0:NB, :], got(G, "t8", h)[0:NB, 0:P]))
                dve.wait_ge(dec_masked, 2 * h + 2)
                for j in range(2):
                    bk = got(G, f"kk{j}", h)
                    for i in range(4):
                        c = 4 * j + i
                        ins = dve.scalar_tensor_tensor(out=cols(amat, c), in0=cols(bk, i), scalar=beta[:, c:c + 1],
                                                       in1=cols(dec1, c), op0=ALU.mult, op1=ALU.mult)
                    give(G, f"kk{j}", ins)
                for j in range(2):
                    bk = got(G, f"qk{j}", h).rearrange("p (c i) -> p c i", c=4)
                    give(G, f"qk{j}", dve.tensor_tensor(half(dec2, j), bk, half(dec2, j), ALU.mult))
                dve.wait_ge(eg_ready, h + 1)
                taken(G, "b8", h)
                dve.tensor_tensor(qg, qn[:, 0:T], gbr, ALU.mult).then_inc(qg_ready, 1)
                dve.wait_ge(am_ready, 7 * h + 1)
                for j in range(2):
                    dve.tensor_tensor(half(X, j), per_chunk(ident[:, :], 4), half(aml[0], j), ALU.subtract)
                for j in range(2):
                    bk = got(G, f"y{j}", h).rearrange("p (c i) -> p c i", c=4)
                    give(G, f"y{j}", dve.tensor_tensor(half(Y, j), per_chunk(ident[:, :], 4), bk, ALU.subtract))
                for L in range(1, 7):
                    for j in range(2):
                        bk = got(G, f"yp{L}_{j}", h).rearrange("p (c i) -> p c i", c=4)
                        give(G, f"yp{L}_{j}", dve.tensor_tensor(half(Y, j), half(Y, j), bk, ALU.subtract))
                        if L < 6:
                            bk = got(G, f"xp{L}_{j}", h).rearrange("p (c i) -> p c i", c=4)
                            give(G, f"xp{L}_{j}", dve.tensor_tensor(half(X, j), half(X, j), bk, ALU.subtract))
                    beside(f"level{L}")
                for c in range(NC):
                    bk = got(G, f"su{c}", h)
                    new = Sst[(c + 1) % 2]
                    if c == 0:
                        ins = dve.tensor_copy(new, bk[:, 0:P])
                    else:
                        if c == 1:
                            wait(dve, S_stored, 16 * h)
                        taken(G, f"su{c - 1}", h)
                        ins = dve.scalar_tensor_tensor(out=new, in0=Sst[c % 2], scalar=dch[:, c:c + 1],
                                                       in1=bk[:, 0:P], op0=ALU.mult, op1=ALU.add)
                    give(G, f"su{c}", ins)
                    beside(f"scan{c}")
                bk = got(G, "ks", h)
                do(dve.tensor_tensor(v8n, vs8, bk[:, 0:NB], ALU.subtract))
                give(G, "ks", dve.tensor_tensor(v8n, v8n, hs8[:, NB:2 * NB], ALU.mult))
                bk = got(G, "v8", h)
                give(G, "v8", dve.tensor_tensor(
                    vbd[0:NB, :].rearrange("p (b e) -> p b e", b=NB), per_chunk(bk[0:NB, 0:P], NB),
                    bd8[:, :].rearrange("p (b e) -> p b e", b=NB), ALU.mult))
                for j in range(2):
                    bk = got(G, f"oo{j}", h)
                    part = sdec[:, j * 512:(j + 1) * 512]
                    give(G, f"oo{j}", dve.tensor_tensor(part, part, bk[:, :], ALU.add))
                beside("decode")
                taken(G, "nst", h)
                dve.reciprocal(rn2[:, 0:9], st2[:, 0:9]).then_inc(rn_ready, 1)
                for j, name in enumerate(("nb0", "nb1", "nb8")):
                    bk = got(G, name, h)
                    a, z = j * 512, min((j + 1) * 512, NT)
                    give(G, name, dve.scalar_tensor_tensor(
                        out=oT[:, a:z], in0=oT[:, a:z], scalar=vt[:, v_gdn:v_gdn + 1], in1=bk[:, 0:z - a],
                        op0=ALU.mult, op1=ALU.mult))
                dve.wait_ge(gate_ready, h + 1)
                for name in ("nb0", "nb1", "nb8"):
                    taken(G, name, h)
                dve.tensor_tensor(oa[:, bass.ds(h * NT, NT)], oT, ggs, ALU.mult).then_inc(oa_ready, 1)

            body(0, True)
            with dve.Fori(1, GH_N - 1) as h:
                body(h, True)
            body(GH_N - 1, False)
            dve.drain().then_inc(phase_done, 1)
            dve.wait_ge(phase_done, 10)

            def gated(j, i, first):
                if not first:
                    dve.wait_ge(mg_stored[i], 8 * j)
                for n in range(3):
                    dve.wait_ge(proj_full, 6 * j + (3 * (W_UPA + 2 * i + 1) + n + 1))
                    dve.wait_ge(proj_taken, 3 * j + (A_UPA + 3 * i + n + 1))
                    c = slice(n * GW, (n + 1) * GW)
                    dve.scalar_tensor_tensor(out=mgst[i][:, c], in0=tgate[i][:, c], scalar=1.0, in1=psum[:, n, 0:GW],
                                             op0=ALU.add, op1=ALU.mult).then_inc(sum_taken, 1)
                dve.wait_ge(sum_taken, 3 * j + (3 * i + 3))
                dve.sem_inc(mg_ready, 1)

            gated(0, 0, True)
            gated(0, 1, True)
            with dve.Fori(1, KT // 2) as pair:
                j = pair * 2
                gated(j, 0, False)
                gated(j, 1, False)
            dve.drain().then_inc(phase_done, 1)
            dve.wait_ge(phase_done, 15)

            G = ssm_plan
            for u in range(4):
                do(dve.memset(sraw[u][:, 0:3], 0.0))

            def conv_columns(g):
                wait(dve, sconv_done, 4 * g)
                nx = SDI // P
                dve.tensor_copy(scw[:, 0:1, :], ctv[:, bass.ds(g + (GT_N + nx), 1), :])
                dve.tensor_copy(scw[:, 1:2, :], ctv[:, bass.ds(g + (GT_N + nx + SG_N), 1), :])
                dve.tensor_copy(scw[:, 2:4, :], ctv[:, bass.ds(2 * g + GT_N, 2), :]).then_inc(scw_ready, 1)

            def convolve(g, u, i):
                if i == 0:
                    wait(dve, proj_taken, 18 * g + (A_SSM + 3 * u + 3))
                conv_step(sconv[u], sraw[u], scw[:, u, :], i, True, sconv_done)

            def mix(g, u):
                dve.wait_ge(stanh_ready, 6 * g + u + 1)
                src, dst = (sconv[u], sconv[u]) if u < 4 else (zraw[u - 4], zs[u - 4])
                out_ready, n = (sx_ready, 4 * g + u + 1) if u < 4 else (z_ready, 2 * g + u - 3)
                dve.scalar_tensor_tensor(out=dst, in0=stnh[u % 2], scalar=1.0, in1=src,
                                         op0=ALU.add, op1=ALU.mult).then_inc(out_ready, 1)
                dve.wait_ge(out_ready, n)
                dve.sem_inc(stanh_used, 1)

            conv_columns(0)
            dve.wait_ge(scw_ready, 1)
            for u in range(4):
                for i in range(CW):
                    convolve(0, u, i)
            for u in range(4):
                mix(0, u)
            BESIDE_S = {"scan0": [(0, 0), (0, 1)], "scan1": [(0, 2), (0, 3)], "scan2": [(1, 0), (1, 1)],
                        "scan3": [(1, 2), (1, 3)], "scan4": ["mix0", (2, 0)], "scan5": [(2, 1), (2, 2)],
                        "scan6": [(2, 3), "mix1"], "scan7": [(3, 0), (3, 1), (3, 2), (3, 3)],
                        "norm": ["mix2"], "end": ["mix3"]}

            def body(g, more):
                def beside(step):
                    for m in BESIDE_S.get(step, ()) if more else ():
                        if isinstance(m, str):
                            mix(g + 1, int(m[-1]))
                        else:
                            if m == (0, 0):
                                dve.wait_ge(scw_ready, g + 2)
                            convolve(g + 1, *m)

                lane.restart()
                wait(dve, ssd_ready, g)
                do(dve.tensor_copy(shs, sh[:, bass.ds(g * 4 * NC * HPG, 4 * NC * HPG)]))
                do(dve.tensor_copy(snw, vt[:, bass.ds(2 * g + v_ssm, 2)]))
                dve.tensor_copy(shx, dtx[:, bass.ds(g * 34, 34)]).then_inc(shx_ready, 1)
                if more:
                    conv_columns(g + 1)
                cs, dt, dtd, dch = (shs[:, i * NC * HPG:(i + 1) * NC * HPG].rearrange("p (c r) -> p c r", c=NC)
                                    for i in range(4))
                for j in range(4):
                    bk = got(G, f"tx{j}", g).rearrange("p (c r e) -> p c r e", c=2, r=HPG)
                    for t, dst in ((dt, xdt), (dtd, xdd)):
                        ins = dve.tensor_tensor(
                            dst[:, 512 * j:512 * (j + 1)].rearrange("p (c r e) -> p c r e", c=2, r=HPG), bk,
                            t[:, 2 * j:2 * j + 2, :].unsqueeze(3).broadcast_to([P, 2, HPG, HD]), ALU.mult)
                    give(G, f"tx{j}", ins)
                mix(g, 4)
                mix(g, 5)
                bk = got(G, "t8", g)
                for i, dst in enumerate((bdg, cdg)):
                    ins = dve.tensor_tensor(dst[0:NB, :].rearrange("p (b e) -> p b e", b=NB),
                                            per_chunk(bk[0:NB, i * P:(i + 1) * P], NB),
                                            bd8[:, :].rearrange("p (b e) -> p b e", b=NB), ALU.mult)
                give(G, "t8", ins)
                dve.wait_ge(csb_loaded, 64 * g + 64)
                for r in range(HPG):
                    for c in range(NC):
                        ins = dve.tensor_scalar(cols(ml[:, r * T:(r + 1) * T], c), cols(csb[:, r * T:(r + 1) * T], c),
                                                cs[:, c, r:r + 1], 0.0, ALU.subtract, ALU.min)
                    ins.then_inc(sdiff, 1)
                for j in range(2):
                    bk = got(G, f"cb{j}", g).rearrange("p (c i) -> p c i", c=4)
                    give(G, f"cb{j}", dve.tensor_tensor(half(cbm, j), bk, per_chunk(triu[:, :], 4), ALU.mult))
                taken(G, "cb0", g)
                taken(G, "cb1", g)
                for r in range(HPG):
                    m, e = ml[:, r * T:(r + 1) * T], csb[:, r * T:(r + 1) * T]
                    dve.wait_ge(sdec_exp, 4 * g + r + 1)
                    dve.tensor_tensor(m, m, cbm, ALU.mult).then_inc(ml_ready, 1)
                    dve.wait_ge(ecs_ready, 4 * g + r + 1)
                    ins = dve.tensor_tensor(e, e, sconv[1][:, 0:T], ALU.mult)
                ins.then_inc(cd_ready, 1)
                wait(dve, yb_stored, 32 * g)
                for q in range(2):
                    dve.tensor_scalar(yT[q], sconv[2 + q], shx[:, 17 * q + 16:17 * q + 17], None, ALU.mult)
                    ins = dve.tensor_tensor(xdts[:, q * NB:(q + 1) * NB], sconv[2 + q][:, T:NT],
                                            shx[:, 17 * q:17 * q + NB], ALU.mult)
                ins.then_inc(x_used, 1)
                dve.wait_ge(x_used, g + 1)
                for c in range(NC):
                    bk = got(G, f"su{c}", g)
                    new = SST[(c + 1) % 2]
                    if c == 0:
                        ins = dve.tensor_copy(new, bk[:, 0:2 * P])
                    else:
                        taken(G, f"su{c - 1}", g)
                        do(dve.tensor_tensor(new.rearrange("p (r e) -> p r e", r=HPG),
                                             SST[c % 2].rearrange("p (r e) -> p r e", r=HPG),
                                             spread(dch[:, c, :], HD), ALU.mult))
                        ins = dve.tensor_tensor(new, new, bk[:, 0:2 * P], ALU.add)
                    give(G, f"su{c}", ins)
                    if c % 2:
                        name = f"y{c // 2}"
                        bk = got(G, name, g)
                        for i in range(4):
                            q, cc = i % 2, c - 1 + i // 2
                            ins = dve.tensor_tensor(cols(yT[q], cc), cols(yT[q], cc), cols(bk, i), ALU.add)
                        give(G, name, ins)
                    beside(f"scan{c}")
                dve.wait_ge(ssd_ready, g + 1)
                def last_read(name, q, ins):
                    if q == 0:
                        do(ins)
                    else:
                        give(G, name, ins)
                        taken(G, name, g)

                for j in range(2):
                    bk = got(G, f"bb{j}", g).rearrange("p (b n) -> p b n", b=4)
                    for q in range(2):
                        part = ssd[:, (q * NB + 4 * j) * P:(q * NB + 4 * j + 4) * P]
                        last_read(f"bb{j}", q, dve.tensor_tensor(
                            stmp.rearrange("p (b n) -> p b n", b=4), bk,
                            spread(xdts[:, q * NB + 4 * j:q * NB + 4 * j + 4]), ALU.mult))
                        do(dve.tensor_tensor(part, part, stmp, ALU.add))
                for j in range(2):
                    bk = got(G, f"cc{j}", g)
                    for q in range(2):
                        part = ssd[:, (q * NB + 4 * j) * P:(q * NB + 4 * j + 4) * P]
                        last_read(f"cc{j}", q, dve.tensor_tensor(stmp, part, bk, ALU.mult))
                        do(dve.tensor_reduce(ysm[:, q * NB + 4 * j:q * NB + 4 * j + 4],
                                             stmp.rearrange("p (b n) -> p b n", b=4), AX_X, ALU.add))
                for q in range(2):
                    do(dve.tensor_tensor(yT[q][:, T:NT], yT[q][:, T:NT], ysm[:, q * NB:(q + 1) * NB], ALU.add))
                    dve.wait_ge(z_ready, 2 * g + q + 1)
                    taken(G, "y3", g)
                    dve.tensor_tensor(yT[q], yT[q], zs[q], ALU.mult).then_inc(y_ready, 1)
                taken(G, "nst", g)
                dve.reciprocal(srn, ssq).then_inc(rn_ready, 1)
                beside("norm")
                dve.wait_ge(y_ready, 2 * g + 2)
                for j, name in enumerate(("nb0", "nb1", "nb8")):
                    bk = got(G, name, g)
                    a, z = j * 512, min((j + 1) * 512, NT)
                    for q in range(2):
                        ins = dve.scalar_tensor_tensor(out=yT[q][:, a:z], in0=yT[q][:, a:z],
                                                       scalar=snw[:, q:q + 1], in1=bk[:, 0:z - a],
                                                       op0=ALU.mult, op1=ALU.mult)
                    if name != "nb8":
                        give(G, name, ins)
                    else:
                        give(G, name, ins)
                taken(G, "nb8", g)
                dve.sem_inc(yb_ready, 1)
                beside("end")

            body(0, True)
            with dve.Fori(1, SG_N - 1) as g:
                body(g, True)
            body(SG_N - 1, False)
            dve.drain().then_inc(phase_done, 1)
            dve.wait_ge(phase_done, 20)

            lane.restart()
            dve.wait_ge(mg_loaded, 16)

            def mixed(j, i):
                m = mg[:, bass.ds(j * NT + i * NT, NT)]
                for n in range(3):
                    dve.wait_ge(proj_full, 9 * j + (3 * (W_UPB + 3 * i + 2) + n + 1))
                    dve.wait_ge(proj_taken, 3 * j + (A_UPB + 3 * i + n + 1))
                    c = slice(n * GW, (n + 1) * GW)
                    lane.step(dve.scalar_tensor_tensor(out=tsum[:, c], in0=tgate2[i][:, c], scalar=1.0,
                                                       in1=psum[:, n, 0:GW], op0=ALU.add, op1=ALU.mult))
                    lane.settle()
                    dst = mg[:, bass.ds(j * NT + (i * NT + n * GW), GW)]
                    dve.tensor_tensor(dst, dst, tsum[:, c], ALU.add).then_inc(sum_taken, 1)

            mixed(0, 0)
            mixed(0, 1)
            with dve.Fori(1, KT // 2) as pair:
                j = pair * 2
                lane.restart()
                mixed(j, 0)
                mixed(j, 1)
            dve.wait_ge(x1_loaded, 16)
            with dve.Fori(0, KT // 2) as pair:
                j = pair * 2
                for i in range(2):
                    for n in range(3):
                        dve.wait_ge(proj_full, 3 * j + (3 * (W_OUT + i) + n + 1))
                        dst = x1[:, bass.ds(j * NT + (i * NT + n * GW), GW)]
                        dve.scalar_tensor_tensor(out=dst, in0=psum[:, n, 0:GW], scalar=0.5, in1=dst,
                                                 op0=ALU.mult, op1=ALU.add).then_inc(sum_taken, 1)
            dve.drain().then_inc(phase_done, 1)
            dve.wait_ge(phase_done, 25)

            lane.restart()
            G = mem_plan
            taken(G, "mst")
            dve.reciprocal(mrn, mstat).then_inc(rn_ready, 1)
            dve.reciprocal(xrn, xstat).then_inc(rn_ready, 1)
            bk = got(G, "mbc")
            for k in range(KT):
                ins = dve.scalar_tensor_tensor(out=mn[:, k, :], in0=memTv[:, k, :], scalar=vt[:, v_mem + k:v_mem + k + 1],
                                               in1=bk[:, 0:M_N], op0=ALU.mult, op1=ALU.mult)
            give(G, "mbc", ins)
            with dve.Fori(0, KT // 2) as pair:
                j = pair * 2
                for i in range(2):
                    dve.wait_ge(proj_full, 3 * j + 3 * (W_MK + i + 1))
                    dve.tensor_copy(Ktok[:, :, bass.ds(j * P + i * P, P)],
                                    psum[:, i, 0:MT * P].rearrange("p (t c) -> p t c", t=MT)).then_inc(sum_taken, 1)

            def normed(plan, name, v):
                for j in range(3):
                    bk = got(plan, f"{name}{j}")
                    a, z = j * 512, min((j + 1) * 512, NT)
                    for k in range(KT):
                        ins = dve.scalar_tensor_tensor(out=xnv[:, k, a:z], in0=x1v[:, k, a:z],
                                                       scalar=vt[:, v + k:v + k + 1], in1=bk[:, 0:z - a],
                                                       op0=ALU.mult, op1=ALU.mult)
                        if k == KT // 2 - 1:
                            ins.then_inc(xt_ready, 1)
                        if k == KT - 1:
                            give(plan, f"{name}{j}", ins)
                        if j and k in (0, KT // 2):
                            low_part(j - 1, k // (KT // 2))
                for i in range(2):
                    low_part(2, i)

            def low_part(j, i):
                norms[0] += 1
                dve.wait_ge(xr_ready, norms[0])
                a, z = j * 512, min((j + 1) * 512, NT)
                ks = slice(i * KT // 2, (i + 1) * KT // 2)
                dve.tensor_tensor(rounded(xlowv[:, ks, a:z]), xnv[:, ks, a:z], xBv[:, ks, a:z], ALU.subtract
                                  ).then_inc(xs_ready, 1)

            norms = [0]
            normed(G, "xb", v_x)
            for name in ("qt0", "qt1"):
                taken(G, name)
            G = attn_plan

            lane.restart()
            with dve.Fori(0, XH_N) as h:
                for s in range(2):
                    dve.tensor_copy(qh[s], qT[:, bass.ds(h * 2 * NT, 2 * NT)].rearrange(
                        "p (k t) -> p k t", k=2)[:, :, s * 512:(s + 1) * 512])
                    dve.tensor_tensor(qm[s][0:NB, :], qtok[0:NB, :],
                                      ident[0:NB, bass.ds(h * 2 + s, 1)].broadcast_to([NB, D]), ALU.mult
                                      ).then_inc(q_ready, 1)
                dve.tensor_copy(vh, Vtok[:, :, bass.ds(h * XD, XD)]).then_inc(vh_ready, 1)
                for s in range(2):
                    for i in range(2):
                        bk = got(G, f"sc{s}{i}", h)
                        do(dve.tensor_reduce(nmx[s][:, 2 * i:2 * i + 2], bk.rearrange("p (c m) -> p c m", c=2),
                                             AX_X, ALU.max))
                    dve.tensor_scalar(nmx[s], nmx[s], -x_scale, None, ALU.mult).then_inc(mx_ready, 1)
                for s in range(2):
                    taken(G, f"sc{s}1", h)
                    dve.reciprocal(prs[s], psm[s]).then_inc(rs_ready, 1)

                def key_products(s, t):
                    if t == 0:
                        dve.wait_ge(kc_loaded[s], 16 * h + 16)
                        taken(G, f"qb{s}1", h)
                        do(dve.tensor_tensor(kc[s][:, 0, :], kc[s][:, 0, :], qrep[s], ALU.mult))
                    else:
                        dve.wait_ge(kprod_ready, 2 * h + s + 1)
                    ins = dve.tensor_reduce(s8[s][:, t, :], kc[s][:, t, :].rearrange("p (h d) -> p h d", h=XH_N),
                                            AX_X, ALU.add)
                    if t == MT - 1:
                        ins.then_inc(s8_ready, 1)

                def bias4(s):
                    bk = got(G, f"st{s}", h)
                    do(dve.tensor_reduce(mx4[s][0:XH_N, :], bk[0:XH_N, 0:M_N], AX_X, ALU.max))
                    dve.tensor_scalar(mx4[s][0:XH_N, :], mx4[s][0:XH_N, :], -x_scale, None, ALU.mult
                                      ).then_inc(m4_ready, 1)

                def probs4(s):
                    taken(G, f"st{s}", h)
                    do(dve.reciprocal(r4[s][0:XH_N, :], sm4[s][0:XH_N, :]))
                    dve.tensor_scalar(e4[s][0:XH_N, :], e4[s][0:XH_N, :], r4[s][0:XH_N, :], None, ALU.mult
                                      ).then_inc(p4_ready, 1)

                def out4(s):
                    bk = got(G, f"os{s}", h)[:, 0:KT].unsqueeze(2)
                    col = bass.ds(h * 2 + (s + T), 1)
                    do(dve.tensor_copy(rounded(atBv[:, :, col]), bk))
                    give(G, f"os{s}", dve.tensor_tensor(rounded(atv[:, :, col]), bk, atBv[:, :, col], ALU.subtract))

                def low_output(s):
                    for k in range(2):
                        bk = got(G, f"o{s}{k}", h)
                        dve.wait_ge(ohi_ready, 4 * h + 2 * s + k + 1)
                        part_ = bass.ds(h * 2 * NT + (k * NT + s * 512), 512)
                        give(G, f"o{s}{k}", dve.tensor_tensor(rounded(at[:, part_]), bk, atB[:, part_], ALU.subtract))

                key_products(0, 0)
                key_products(0, 1)
                bias4(0)
                key_products(1, 0)
                probs4(0)
                key_products(1, 1)
                low_output(0)
                out4(0)
                bias4(1)
                probs4(1)
                low_output(1)
                out4(1)
                lane.restart()
            with dve.Fori(0, KT // 2) as pair:
                j = pair * 2
                for i in range(2):
                    for n in range(3):
                        dve.wait_ge(proj_full, 3 * j + (3 * (W_CO + i) + n + 1))
                        dst = x1[:, bass.ds(j * NT + (i * NT + n * GW), GW)]
                        dve.tensor_tensor(dst, dst, psum[:, n, 0:GW], ALU.add).then_inc(sum_taken, 1)

            G = ff_plan
            taken(G, "fst")
            dve.reciprocal(xrn, xstat).then_inc(rn_ready, 1)
            normed(G, "fb", v_ff)
            for q in range(FQ_N):
                with dve.Fori(0, KT) as j:
                    for n in range(3):
                        dve.wait_ge(proj_taken, 3 * j + (A_END + 3 * KT * q + n + 1))
                        hidden = hA[:, bass.ds(j * NT + n * GW, GW)]
                        dve.tensor_tensor(hidden, hidden, psum[:, n, 0:GW], ALU.mult).then_inc(sum_taken, 1)
                    dve.wait_ge(hr_ready, j + (KT * q + 1))
                    tile = bass.ds(j * NT, NT)
                    dve.tensor_tensor(rounded(hlow[:, tile]), hA[:, tile], hB[:, tile], ALU.subtract
                                      ).then_inc(h_ready, 1)
                with dve.Fori(0, KT) as j:
                    for n in range(3):
                        dve.wait_ge(proj_full, 3 * j + (3 * (W_FU + 2 * KT * q + KT) + n + 1))
                        dst = x1[:, bass.ds(j * NT + n * GW, GW)]
                        dve.tensor_tensor(dst, dst, psum[:, n, 0:GW], ALU.add).then_inc(sum_taken, 1)
            taken(G, "zst")
            do(dve.reciprocal(xrn, xstat))
            dve.wait_ge(gfin_loaded, 16)
            for c in range(NC + 1):
                for j in range(2):
                    bk = got(G, f"y{c}_{j}")
                    give(G, f"y{c}_{j}", dve.scalar_tensor_tensor(
                        out=ytok[:, c, j * 512:(j + 1) * 512], in0=bk, scalar=xrn[:, c:c + 1],
                        in1=gfin[:, j * 512:(j + 1) * 512], op0=ALU.mult, op1=ALU.mult))
                taken(G, f"y{c}_1")
                dve.sem_inc(yt_ready, 1)

        @block.gpsimd
        def _(pool):
            lane = Lane(pool, pool_step)

            def do(ins):
                lane.step(ins)
                lane.settle()

            def waited():
                lane.step(pool)
                lane.settle()

            do(pool.memset(ones[:, :], 1.0))
            pool.affine_select(out=ident[:, :], in_=ones[:, :], pattern=[[-1, P]], compare_op=ALU.is_equal,
                                  fill=0.0, base=0, channel_multiplier=1).then_inc(ident_ready, 1)
            pool.memset(hb, 0.0)
            pool.memset(wsc, 0.0)
            pool.memset(cstage[0:32, :], 0.0).then_inc(consts_ready, 1)
            do(pool.memset(eps[:, :], EPS))
            do(pool.memset(bd8[:, :], 1.0))
            do(pool.memset(expand[0:32, :], 1.0))
            do(pool.affine_select(out=triu[:, :], in_=ones[:, :], pattern=[[1, P]], compare_op=ALU.is_ge,
                                  fill=0.0, base=0, channel_multiplier=-1))
            b8 = bd8[:, :].rearrange("p (b e) -> p b e", b=NB)
            do(pool.affine_select(out=b8, in_=b8, pattern=[[-1, NB], [0, P]], compare_op=ALU.is_equal,
                                  fill=0.0, base=0, channel_multiplier=1))
            ex = expand[0:32, :].rearrange("p (h e) -> p h e", h=SH_N)
            do(pool.affine_select(out=ex, in_=ex, pattern=[[-1, SH_N], [0, HD]], compare_op=ALU.is_equal,
                                  fill=0.0, base=0, channel_multiplier=1))
            do(pool.memset(lvl[:, :], 0.0))
            for L in range(7):
                b = 1 << L
                m = cols(lvl, L).rearrange("p (n s r) -> p n s r", s=2, r=b)[:, :, 0, :]
                nblk = P // (2 * b)
                do(pool.memset(m, 1.0))
                do(pool.affine_select(out=m, in_=m, pattern=[[-2 * b, nblk], [0, b]], compare_op=ALU.is_ge,
                                      fill=0.0, base=-b, channel_multiplier=1))
                do(pool.affine_select(out=m, in_=m, pattern=[[2 * b, nblk], [0, b]], compare_op=ALU.is_ge,
                                      fill=0.0, base=2 * b - 1, channel_multiplier=-1))
            pool.sem_inc(consts_ready, 1)
            pool.drain().then_inc(phase_done, 1)
            pool.wait_ge(phase_done, SETUP_ENDS)

            G = gdn_plan

            def body(h):
                lane.restart()
                for i, d in enumerate((dec1, dec2)):
                    pool.wait_ge(dec_exp, 2 * h + i + 1)
                    waited()
                    dv = d.rearrange("p (c i) -> p c i", c=NC)
                    pool.affine_select(out=dv, in_=dv, pattern=[[0, NC], [-1, P] if i == 0 else [1, P]],
                                       compare_op=ALU.is_gt if i == 0 else ALU.is_ge, fill=0.0, base=0,
                                       channel_multiplier=1 if i == 0 else -1).then_inc(dec_masked, 1)
                for j in range(2):
                    pool.wait_ge(bank_taken[G.bank(f"kk{j}")], G.after(f"kk{j}", h))
                for L in range(7):
                    if L == 2:
                        pool.wait_ge(bank_full[G.bank("y1")], G.after("y1", h))
                        pool.wait_ge(bank_taken[G.bank("y1")], G.after("y1", h))
                    elif L > 2:
                        pool.wait_ge(bank_full[G.bank(f"p{L - 2}_1")], G.after(f"p{L - 2}_1", h))
                    waited()
                    pool.tensor_tensor(
                        aml[L % 2].rearrange("p (c i) -> p c i", c=NC), amat.rearrange("p (c i) -> p c i", c=NC),
                        per_chunk(cols(lvl, L), NC), ALU.mult).then_inc(am_ready, 1)
                pool.wait_ge(hs_ready, h + 1)
                pool.wait_ge(sdec_loaded, 16 * h + 16)
                sdv = sdec.rearrange("p (b e) -> p b e", b=NB)
                pool.tensor_tensor(sdv, sdv, spread(hs8[:, 0:NB]), ALU.mult).then_inc(sd_ready, 1)
            body(0)
            with pool.Fori(1, GH_N) as h:
                body(h)
            pool.drain().then_inc(phase_done, 1)
            pool.wait_ge(phase_done, 10)
            pool.drain().then_inc(phase_done, 1)
            pool.wait_ge(phase_done, 15)

            lane.restart()

            def body(g):
                lane.restart()
                pool.wait_ge(shx_ready, g + 1)
                pool.wait_ge(ssd_loaded, 32 * g + 32)
                for q in range(2):
                    sv = ssd[:, q * NB * P:(q + 1) * NB * P].rearrange("p (b n) -> p b n", b=NB)
                    ins = pool.tensor_tensor(sv, sv, spread(shx[:, 17 * q + NB:17 * q + 2 * NB]), ALU.mult)
                ins.then_inc(ssd_ready, 1)

            body(0)
            with pool.Fori(1, SG_N) as g:
                body(g)
            pool.drain().then_inc(phase_done, 1)
            pool.wait_ge(phase_done, 20)
            pool.drain().then_inc(phase_done, 1)
            pool.wait_ge(phase_done, 25)

            def high_part(plan, name):
                for j in range(3):
                    a, z = j * 512, min((j + 1) * 512, NT)
                    for i in range(2):
                        if i == 0:
                            pool.wait_ge(xt_ready, (0 if name == "xb" else 3) + j + 1)
                        else:
                            pool.wait_ge(bank_taken[plan.bank(f"{name}{j}")], plan.after(f"{name}{j}"))
                        ks = slice(i * KT // 2, (i + 1) * KT // 2)
                        pool.tensor_scalar(rounded(xBv[:, ks, a:z]), xnv[:, ks, a:z], 1.0, None, ALU.mult
                                           ).then_inc(xr_ready, 1)

            def split(base, it, i):
                slot = i % 2
                pool.wait_ge(slab_loaded[slot], 8 * it + (16 * ((base + i) // 2) + 16))
                pool.wait_ge(proj_full, 3 * it + 3 * (base + i - 1))
                waited()
                do(pool.tensor_scalar(rounded(wh[slot]), slab[slot][:, :], 1.0, None, ALU.mult))
                pool.tensor_tensor(rounded(wl[slot]), slab[slot][:, :], wh[slot], ALU.subtract).then_inc(w_split, 1)

            def split_all(base, first=0):
                for i in range(2 * first, 2):
                    split(base, 0, i)
                lane.restart()
                with pool.Fori(1, KT // 2) as pair:
                    j = pair * 2
                    for i in range(2):
                        split(base, j, i)
                    lane.restart()

            high_part(mem_plan, "xb")
            split_all(W_CQ)

            G = attn_plan
            lane.restart()
            with pool.Fori(0, XH_N) as h:
                for s in range(2):
                    pool.wait_ge(rs_ready, 2 * h + s + 1)
                    waited()
                    for c in range(4):
                        ins = pool.tensor_scalar(pr[s][:, c, :], pr[s][:, c, :], prs[s][:, c:c + 1], None, ALU.mult)
                    ins.then_inc(p_ready, 1)
                    pool.wait_ge(kc_loaded[s], 16 * h + 16)
                    pool.wait_ge(bank_taken[G.bank(f"qb{s}1")], G.after(f"qb{s}1", h))
                    pool.tensor_tensor(kc[s][:, 1, :], kc[s][:, 1, :], qrep[s], ALU.mult).then_inc(kprod_ready, 1)
                lane.restart()
            pool.wait_ge(s8_ready, 2 * XH_N)
            pool.wait_ge(bank_full[G.bank("os1")], G.after("os1", XH_N - 1))
            split_all(W_CO)

            for i in range(2):
                split(W_FU, 0, i)
            high_part(ff_plan, "fb")
            for q in range(FQ_N):
                split_all(W_FU + 2 * KT * q, first=1 if q == 0 else 0)
                split_all(W_FU + 2 * KT * q + KT)


INPUTS = ("x_prompt", "x_sample", "mem_prompt", "state_gdn_conv", "state_gdn", "state_ssm_conv", "state_ssm",
          "cache_mem_k", "cache_mem_v", "g_mix", "w_in", "gdn_conv_w", "gdn_A_log", "gdn_dt_bias", "gdn_norm_w",
          "w_gdn_up", "ssm_conv_w", "ssm_conv_b", "ssm_dt_bias", "ssm_A_log", "ssm_D", "ssm_norm_w", "w_ssm_up",
          "w_out", "g_mem", "w_mk", "w_mv", "g_x", "w_cq", "w_co", "g_ff", "w_ff_up", "w_ff_down", "g_final")


def output_shapes(inputs):
    shape = {n: tuple(inputs[n].shape) for n in inputs}
    conv_g, conv_s, cache = shape["state_gdn_conv"], shape["state_ssm_conv"], shape["cache_mem_k"]
    one = (1, 1)
    return {
        "y_prompt": shape["x_prompt"], "y_sample": shape["x_sample"],
        "p_gdn_conv": one + conv_g[2:], "p_gdn": one + shape["state_gdn"][2:],
        "p_ssm_conv": one + conv_s[2:], "p_ssm": one + shape["state_ssm"][2:],
        "p_mem_k": one + cache[2:], "p_mem_v": one + cache[2:],
        "s_gdn_conv": conv_g, "s_gdn": shape["state_gdn"], "s_ssm_conv": conv_s, "s_ssm": shape["state_ssm"],
    }


def kernel(**inputs):
    import numpy as np
    import concourse.bacc as bacc
    from concourse.bass_utils import run_bass_kernel_spmd

    nc = bacc.Bacc("TRN2", target_bir_lowering=False, num_devices=1)
    arrays, io = {}, {}
    for name in INPUTS:
        arrays[f"in_{name}_dram"] = a = np.ascontiguousarray(inputs[name])
        io[name] = nc.dram_tensor(f"in_{name}_dram", a.shape, mybir.dt.from_np(a.dtype), kind="ExternalInput").ap()
    outs = output_shapes(inputs)
    for i, (name, shape) in enumerate(outs.items()):
        io[name] = nc.dram_tensor(f"out_{i}_dram", shape, F32, kind="ExternalOutput").ap()
    hybrid_step(nc, io)
    r = run_bass_kernel_spmd(nc, [arrays], core_ids=[0])
    return tuple(r.results[0][f"out_{i}_dram"] for i in range(len(outs)))
```
